# Optimizing a Trainium2 kernel written in Bass

```python
import math
import jax, jax.numpy as jnp
from jax import lax
import numpy as np

D_MODEL = 1024
BATCH = 1
SEQ = 512
DEPTH = 1

HEAD_DIM = 64
ATTN_SCALE = HEAD_DIM ** -0.5
SWA_Q_HEADS = 8
SWA_KV_HEADS = 2
SWA_GROUP = SWA_Q_HEADS // SWA_KV_HEADS
SWA_WINDOW = 128
SWA_BLOCK = 128
MOBA_HEADS = 8
MOBA_BLOCK = 256
MOBA_TOPK = 3
MOBA_Q_CHUNK = 32
NUM_BUCKETS = 32
MAX_EXACT = NUM_BUCKETS // 2
MAX_DISTANCE = 2048
N_ATTN_HEADS = SWA_Q_HEADS + MOBA_HEADS
SWA_Q_W = SWA_Q_HEADS * HEAD_DIM
SWA_KV_W = SWA_KV_HEADS * HEAD_DIM
MOBA_W = MOBA_HEADS * HEAD_DIM
N_BRANCHES = 2
IN_WIDTHS = (SWA_Q_W, SWA_KV_W, SWA_KV_W, MOBA_W, MOBA_W, MOBA_W, D_MODEL, D_MODEL)
IN_TOTAL = SWA_Q_W + 2 * SWA_KV_W + 3 * MOBA_W + N_BRANCHES * D_MODEL
D_FF = 4 * D_MODEL
N_MOD = 6
RMS_EPS = 1e-6


def rmsnorm(x, g):
    xf = x.astype(jnp.float32)
    y = xf * lax.rsqrt(jnp.mean(xf * xf, axis=-1, keepdims=True) + RMS_EPS)
    return (y * g.astype(jnp.float32)).astype(x.dtype)

def modulate(h, shift, scale):
    return h * (1.0 + scale[:, None, :]) + shift[:, None, :]

def t5_bucket(dist):
    n = jnp.maximum(dist, 0)
    nf = jnp.maximum(n, 1).astype(jnp.float32)
    large = MAX_EXACT + (jnp.log(nf / MAX_EXACT) / math.log(MAX_DISTANCE / MAX_EXACT)
                         * (NUM_BUCKETS - MAX_EXACT)).astype(jnp.int32)
    large = jnp.minimum(large, NUM_BUCKETS - 1)
    return jnp.where(n < MAX_EXACT, n, large)

def swa_attention(q, k, v, sinks, rel_bias):
    B, S = q.shape[0], q.shape[1]
    L = SWA_BLOCK
    nb = S // L
    qb = q.reshape(B, nb, L, SWA_KV_HEADS, SWA_GROUP, HEAD_DIM)
    kb = k.reshape(B, nb, L, SWA_KV_HEADS, HEAD_DIM)
    vb = v.reshape(B, nb, L, SWA_KV_HEADS, HEAD_DIM)
    pad = ((0, 0), (1, 0), (0, 0), (0, 0), (0, 0))
    kk = jnp.concatenate([jnp.pad(kb, pad)[:, :-1], kb], axis=2)
    vv = jnp.concatenate([jnp.pad(vb, pad)[:, :-1], vb], axis=2)
    s = jnp.einsum('bnqhgd,bnkhd->bnhgqk', qb, kk).astype(jnp.float32) * ATTN_SCALE
    i = jnp.arange(L)[:, None] + L
    j = jnp.arange(2 * L)[None, :]
    dist = i - j
    bias = rel_bias[t5_bucket(dist)][..., :SWA_Q_HEADS].astype(jnp.float32)
    bias = bias.transpose(2, 0, 1).reshape(SWA_KV_HEADS, SWA_GROUP, L, 2 * L)
    kabs = jnp.arange(nb)[:, None, None] * L - L + j[None]
    mask = ((dist >= 0) & (dist < SWA_WINDOW))[None] & (kabs >= 0)
    s = jnp.where(mask[None, :, None, None], s + bias, -jnp.inf)
    sink = sinks.astype(jnp.float32).reshape(SWA_KV_HEADS, SWA_GROUP)[None, None, :, :, None, None]
    m = jnp.maximum(jnp.max(s, axis=-1, keepdims=True), sink)
    p = jnp.exp(s - m)
    p = p / (jnp.sum(p, axis=-1, keepdims=True) + jnp.exp(sink - m))
    o = jnp.einsum('bnhgqk,bnkhd->bnqhgd', p.astype(v.dtype), vv)
    return o.reshape(B, S, SWA_Q_HEADS * HEAD_DIM)

def moba_attention(q, k, v, rel_bias):
    B, S = q.shape[0], q.shape[1]
    H = MOBA_HEADS
    MB = MOBA_BLOCK
    nblk = (S + MB - 1) // MB
    Sp = nblk * MB
    k_eff = max(1, min(MOBA_TOPK, nblk - 1))
    padw = ((0, 0), (0, Sp - S), (0, 0), (0, 0))
    q = jnp.pad(q, padw)
    k = jnp.pad(k, padw)
    v = jnp.pad(v, padw)
    qh = q.transpose(0, 2, 1, 3)
    kb = k.reshape(B, nblk, MB, H, HEAD_DIM).transpose(0, 3, 1, 2, 4)
    vb = v.reshape(B, nblk, MB, H, HEAD_DIM).transpose(0, 3, 1, 2, 4)
    kmean = jnp.mean(kb.astype(jnp.float32), axis=3)
    gate = jnp.einsum('bhsd,bhnd->bhsn', qh.astype(jnp.float32), kmean)
    qblk = jnp.arange(Sp) // MB
    past = jnp.arange(nblk)[None, :] < qblk[:, None]
    gate = jnp.where(past, gate, -jnp.inf)
    _, idx = lax.top_k(gate, k_eff)
    valid = jnp.arange(k_eff)[None, :] < qblk[:, None]
    table_b = rel_bias[:, SWA_Q_HEADS:].T.astype(jnp.float32)
    bi = jnp.arange(B)[:, None, None, None]
    hi = jnp.arange(H)[None, :, None, None]
    hi5 = hi[..., None]
    n_chunks = Sp // MOBA_Q_CHUNK

    def chunk_fn(ci):
        start = ci * MOBA_Q_CHUNK
        q_c = lax.dynamic_slice_in_dim(qh, start, MOBA_Q_CHUNK, axis=2)
        idx_c = lax.dynamic_slice_in_dim(idx, start, MOBA_Q_CHUNK, axis=2)
        valid_c = lax.dynamic_slice_in_dim(valid, start, MOBA_Q_CHUNK, axis=0)
        qpos = start + jnp.arange(MOBA_Q_CHUNK)
        own = start // MB
        k_sel = kb[bi, hi, idx_c]
        v_sel = vb[bi, hi, idx_c]
        s_past = jnp.einsum('bhqd,bhqrkd->bhqrk', q_c, k_sel).astype(jnp.float32) * ATTN_SCALE
        kpos_past = idx_c[..., None] * MB + jnp.arange(MB)
        bias_past = table_b[hi5, t5_bucket(qpos[:, None, None] - kpos_past)]
        s_past = jnp.where(valid_c[None, None, :, :, None], s_past + bias_past, -jnp.inf)
        s_past = s_past.reshape(B, H, MOBA_Q_CHUNK, k_eff * MB)
        k_own = lax.dynamic_index_in_dim(kb, own, axis=2, keepdims=False)
        v_own = lax.dynamic_index_in_dim(vb, own, axis=2, keepdims=False)
        s_own = jnp.einsum('bhqd,bhkd->bhqk', q_c, k_own).astype(jnp.float32) * ATTN_SCALE
        dist_own = qpos[:, None] - (own * MB + jnp.arange(MB))[None, :]
        bias_own = table_b[:, t5_bucket(dist_own)]
        s_own = jnp.where(dist_own >= 0, s_own + bias_own, -jnp.inf)
        p = jax.nn.softmax(jnp.concatenate([s_past, s_own], axis=-1), axis=-1)
        p_past = p[..., :k_eff * MB].reshape(B, H, MOBA_Q_CHUNK, k_eff, MB)
        p_own = p[..., k_eff * MB:]
        o = (jnp.einsum('bhqrk,bhqrkd->bhqd', p_past.astype(v_sel.dtype), v_sel)
             + jnp.einsum('bhqk,bhkd->bhqd', p_own.astype(v_own.dtype), v_own))
        return o

    out = lax.map(chunk_fn, jnp.arange(n_chunks))
    out = out.transpose(1, 0, 3, 2, 4).reshape(B, Sp, H * HEAD_DIM)
    return out[:, :S]

def first_inputs(seed: int = 0) -> dict:
    key = jax.random.key(seed)
    ks = jax.random.split(key, 16)
    f32 = jnp.float32
    nrm = lambda k, shape, s: jax.random.normal(k, shape, f32) * s
    return {
        "x": nrm(ks[0], (BATCH, SEQ, D_MODEL), 1.0),
        "c": nrm(ks[1], (BATCH, D_MODEL), 1.0),
        "ada_w": nrm(ks[2], (DEPTH, D_MODEL, N_MOD * D_MODEL), D_MODEL ** -0.5),
        "ada_b": nrm(ks[3], (DEPTH, N_MOD * D_MODEL), 0.02),
        "norm1_g": 1.0 + nrm(ks[4], (DEPTH, D_MODEL), 0.02),
        "norm2_g": 1.0 + nrm(ks[5], (DEPTH, D_MODEL), 0.02),
        "w_in": nrm(ks[6], (DEPTH, D_MODEL, IN_TOTAL), D_MODEL ** -0.5),
        "attn_sinks": nrm(ks[7], (DEPTH, SWA_Q_HEADS), 0.5),
        "rel_bias": nrm(ks[8], (NUM_BUCKETS, N_ATTN_HEADS), 0.5),
        "w_branch_a": nrm(ks[9], (DEPTH, SWA_Q_W, D_MODEL), SWA_Q_W ** -0.5),
        "w_branch_b": nrm(ks[10], (DEPTH, MOBA_W, D_MODEL), MOBA_W ** -0.5),
        "w_out": nrm(ks[11], (DEPTH, D_MODEL, D_MODEL), D_MODEL ** -0.5),
        "w_mlp_in": nrm(ks[12], (DEPTH, D_MODEL, D_FF), D_MODEL ** -0.5),
        "w_mlp_out": nrm(ks[13], (DEPTH, D_FF, D_MODEL), D_FF ** -0.5),
        "final_g": 1.0 + nrm(ks[14], (D_MODEL,), 0.02),
    }

def first_block(x, c, ada_w, ada_b, norm1_g, norm2_g, w_in, attn_sinks, rel_bias,
              w_branch_a, w_branch_b, w_out, w_mlp_in, w_mlp_out, final_g):
    B, S = x.shape[0], x.shape[1]
    offsets = []
    acc = 0
    for w in IN_WIDTHS[:-1]:
        acc += w
        offsets.append(acc)
    cs = jax.nn.silu(c)
    for l in range(DEPTH):
        mod = cs @ ada_w[l] + ada_b[l]
        shift1, scale1, gate1, shift2, scale2, gate2 = jnp.split(mod, N_MOD, axis=-1)
        h = modulate(rmsnorm(x, norm1_g[l]), shift1, scale1)
        proj = h @ w_in[l]
        qa, ka, va, qb, kb, vb, ga, gb = jnp.split(proj, offsets, axis=-1)
        ya = swa_attention(qa.reshape(B, S, SWA_Q_HEADS, HEAD_DIM),
                           ka.reshape(B, S, SWA_KV_HEADS, HEAD_DIM),
                           va.reshape(B, S, SWA_KV_HEADS, HEAD_DIM),
                           attn_sinks[l], rel_bias) @ w_branch_a[l]
        yb = moba_attention(qb.reshape(B, S, MOBA_HEADS, HEAD_DIM),
                            kb.reshape(B, S, MOBA_HEADS, HEAD_DIM),
                            vb.reshape(B, S, MOBA_HEADS, HEAD_DIM),
                            rel_bias) @ w_branch_b[l]
        merged = jax.nn.sigmoid(ga) * ya + jax.nn.sigmoid(gb) * yb
        x = x + gate1[:, None, :] * (merged @ w_out[l])
        h2 = modulate(rmsnorm(x, norm2_g[l]), shift2, scale2)
        y = jnp.square(jax.nn.relu(h2 @ w_mlp_in[l])) @ w_mlp_out[l]
        x = x + gate2[:, None, :] * y
    return rmsnorm(x, final_g)


DEPTH_2 = 2

CHUNK = 64
N_A = DEPTH_2 // 2
N_B = DEPTH_2 - N_A
CONV_WIDTH = 3
N_HEADS = 16
HEAD_DIM_2 = D_MODEL // N_HEADS
D_FF_2 = -(-8 * D_MODEL // (3 * 256)) * 256
Q_BLOCK = 128
LN_EPS = 1e-5
DEEPNORM_ALPHA = (2.0 * DEPTH_2) ** 0.25
DEEPNORM_BETA = (8.0 * DEPTH_2) ** -0.25


def layer_norm(x, g, b):
    xf = x.astype(jnp.float32)
    mu = jnp.mean(xf, axis=-1, keepdims=True)
    var = jnp.mean(jnp.square(xf - mu), axis=-1, keepdims=True)
    y = (xf - mu) * lax.rsqrt(var + LN_EPS) * g + b
    return y.astype(x.dtype)

def modulate_2(x, shift, scale):
    return x * (1.0 + scale[:, None, :]) + shift[:, None, :]

def short_conv_mixer(h, w_in, conv_w, w_out):
    d = h.shape[-1]
    gb, gc, v = jnp.split(h @ w_in, 3, axis=-1)
    u = gc * v
    conv = lax.conv_general_dilated(
        u, conv_w[:, None, :].astype(u.dtype),
        window_strides=(1,), padding=[(CONV_WIDTH - 1, 0)],
        dimension_numbers=("NWC", "WIO", "NWC"), feature_group_count=d)
    return (gb * conv) @ w_out

def shared_kv(x, c, w_ada_kv, b_ada_kv, w_k, w_v, w_f, b_f):
    bsz, s, _ = x.shape
    kv_shift, kv_scale = jnp.split(jax.nn.silu(c) @ w_ada_kv + b_ada_kv, 2, axis=-1)
    h = modulate_2(x, kv_shift, kv_scale)
    k = (h @ w_k).reshape(bsz, s, N_HEADS, HEAD_DIM_2).transpose(0, 2, 1, 3)
    v = (h @ w_v).reshape(bsz, s, N_HEADS, HEAD_DIM_2).transpose(0, 2, 1, 3)
    log_f = jax.nn.log_sigmoid((h @ w_f + b_f).astype(jnp.float32))
    log_fcum = jnp.cumsum(log_f, axis=1).transpose(0, 2, 1)
    return k, v, log_fcum

def forgetting_attention(h, w_q, k, v, log_fcum, w_o):
    bsz, s, d = h.shape
    q = (h @ w_q).reshape(bsz, s, N_HEADS, HEAD_DIM_2).transpose(0, 2, 1, 3) * (HEAD_DIM_2 ** -0.5)
    outs = []
    for i in range(s // Q_BLOCK):
        q0 = i * Q_BLOCK
        kend = q0 + Q_BLOCK
        qb = q[:, :, q0:kend]
        kb = k[:, :, :kend]
        vb = v[:, :, :kend]
        logits = jnp.einsum("bhqd,bhkd->bhqk", qb, kb, preferred_element_type=jnp.float32)
        logits = logits + log_fcum[:, :, q0:kend, None] - log_fcum[:, :, None, :kend]
        qpos = q0 + jnp.arange(Q_BLOCK)
        kpos = jnp.arange(kend)
        logits = jnp.where(kpos[None, :] <= qpos[:, None], logits, -jnp.inf)
        p = jax.nn.softmax(logits, axis=-1)
        outs.append(jnp.einsum("bhqk,bhkd->bhqd", p.astype(vb.dtype), vb))
    o = jnp.concatenate(outs, axis=2).transpose(0, 2, 1, 3).reshape(bsz, s, d)
    return o @ w_o

def swiglu(h, w_gate, w_up, w_down):
    return (jax.nn.silu(h @ w_gate) * (h @ w_up)) @ w_down

def second_inputs(seed: int = 0) -> dict:
    key = jax.random.key(seed)
    ks = jax.random.split(key, 24)
    D, F, H = D_MODEL, D_FF_2, N_HEADS
    nrm = lambda k, shape, scale: jax.random.normal(k, shape, jnp.float32) * scale
    return {
        "x": nrm(ks[0], (BATCH, SEQ, D), 1.0),
        "c": nrm(ks[1], (BATCH, D), 1.0),
        "w_ada": nrm(ks[2], (DEPTH_2, D, N_MOD * D), 0.5 * D ** -0.5),
        "b_ada": nrm(ks[3], (DEPTH_2, N_MOD * D), 0.02),
        "conv_w_in": nrm(ks[4], (N_A, D, 3 * D), D ** -0.5),
        "conv_w": nrm(ks[5], (N_A, CONV_WIDTH, D), CONV_WIDTH ** -0.5),
        "conv_w_out": nrm(ks[6], (N_A, D, D), DEEPNORM_BETA * D ** -0.5),
        "w_ada_kv": nrm(ks[7], (D, 2 * D), 0.5 * D ** -0.5),
        "b_ada_kv": nrm(ks[8], (2 * D,), 0.02),
        "w_k": nrm(ks[9], (D, D), D ** -0.5),
        "w_v": nrm(ks[10], (D, D), DEEPNORM_BETA * D ** -0.5),
        "w_f": nrm(ks[11], (D, H), D ** -0.5),
        "b_f": jax.random.uniform(ks[12], (H,), jnp.float32, 1.0, 5.0),
        "attn_w_q": nrm(ks[13], (N_B, D, D), D ** -0.5),
        "attn_w_o": nrm(ks[14], (N_B, D, D), DEEPNORM_BETA * D ** -0.5),
        "ffn_w_gate": nrm(ks[15], (DEPTH_2, D, F), D ** -0.5),
        "ffn_w_up": nrm(ks[16], (DEPTH_2, D, F), D ** -0.5),
        "ffn_w_down": nrm(ks[17], (DEPTH_2, F, D), DEEPNORM_BETA * F ** -0.5),
        "ln1_g": 1.0 + nrm(ks[18], (DEPTH_2, D), 0.02),
        "ln1_b": nrm(ks[19], (DEPTH_2, D), 0.02),
        "ln2_g": 1.0 + nrm(ks[20], (DEPTH_2, D), 0.02),
        "ln2_b": nrm(ks[21], (DEPTH_2, D), 0.02),
    }

def second_block(x, c, w_ada, b_ada, conv_w_in, conv_w, conv_w_out, w_ada_kv, b_ada_kv,
              w_k, w_v, w_f, b_f, attn_w_q, attn_w_o, ffn_w_gate, ffn_w_up, ffn_w_down,
              ln1_g, ln1_b, ln2_g, ln2_b):
    c_act = jax.nn.silu(c)
    k = v = log_fcum = None
    for l in range(DEPTH_2):
        sh1, sc1, g1, sh2, sc2, g2 = jnp.split(c_act @ w_ada[l] + b_ada[l], N_MOD, axis=-1)
        h = modulate_2(x, sh1, sc1)
        if l < N_A:
            y = short_conv_mixer(h, conv_w_in[l], conv_w[l], conv_w_out[l])
        else:
            if l == N_A:
                k, v, log_fcum = shared_kv(x, c, w_ada_kv, b_ada_kv, w_k, w_v, w_f, b_f)
            j = l - N_A
            y = forgetting_attention(h, attn_w_q[j], k, v, log_fcum, attn_w_o[j])
        x = layer_norm(DEEPNORM_ALPHA * x + g1[:, None, :] * y, ln1_g[l], ln1_b[l])
        h = modulate_2(x, sh2, sc2)
        y = swiglu(h, ffn_w_gate[l], ffn_w_up[l], ffn_w_down[l])
        x = layer_norm(DEEPNORM_ALPHA * x + g2[:, None, :] * y, ln2_g[l], ln2_b[l])
    return x


def setup_inputs(seed=0):
    out = dict(first_inputs(seed))
    for name, value in second_inputs(seed + 1).items():
        if name != "x":
            out[name + "_2"] = value
    return out


def reference(
    x, c, ada_w, ada_b, norm1_g, norm2_g, w_in, attn_sinks, rel_bias, w_branch_a, w_branch_b,
    w_out, w_mlp_in, w_mlp_out, final_g, c_2, w_ada_2, b_ada_2, conv_w_in_2, conv_w_2,
    conv_w_out_2, w_ada_kv_2, b_ada_kv_2, w_k_2, w_v_2, w_f_2, b_f_2, attn_w_q_2, attn_w_o_2,
    ffn_w_gate_2, ffn_w_up_2, ffn_w_down_2, ln1_g_2, ln1_b_2, ln2_g_2, ln2_b_2,
):
    x = first_block(
        x, c, ada_w, ada_b, norm1_g, norm2_g, w_in, attn_sinks, rel_bias, w_branch_a,
        w_branch_b, w_out, w_mlp_in, w_mlp_out, final_g,
    )
    return second_block(
        x, c_2, w_ada_2, b_ada_2, conv_w_in_2, conv_w_2, conv_w_out_2, w_ada_kv_2, b_ada_kv_2,
        w_k_2, w_v_2, w_f_2, b_f_2, attn_w_q_2, attn_w_o_2, ffn_w_gate_2, ffn_w_up_2,
        ffn_w_down_2, ln1_g_2, ln1_b_2, ln2_g_2, ln2_b_2,
    )


_drawn_inputs = setup_inputs


def setup_inputs(seed=0):
    import zlib

    import numpy as np

    out = dict(_drawn_inputs(seed))
    spreads = {}
    factors = {'norm1_g': 8.0,
     'norm2_g': 3.367,
     'attn_sinks': 64.0,
     'final_g': 2.922,
     'b_ada_2': 4.093,
     'w_ada_kv_2': 2.913,
     'b_ada_kv_2': 8.0,
     'w_k_2': 5.517,
     'w_f_2': 8.0,
     'b_f_2': 8.0,
     'attn_w_q_2': 5.52}
    for name, (base, spread) in spreads.items():
        noise = np.random.default_rng([zlib.crc32(name.encode()), seed]).standard_normal(out[name].shape)
        drawn = base * np.exp(spread * noise) if base else spread * noise
        out[name] = __import__('jax').numpy.asarray(drawn.astype(out[name].dtype))
    for name, factor in factors.items():
        out[name] = (out[name] * factor).astype(out[name].dtype)
    return out
```

```python
import math
from contextlib import ExitStack

import numpy as np

import concourse.bass as bass
from concourse import mybir

F = mybir.dt.float32
R = mybir.dt.float32r
ALU = mybir.AluOpType
ACT = mybir.ActivationFunctionType

P = 128
T = 512
D = 1024
KT = D // P
NEG = -1.0e30
LOW = -3.0e38
RMS_EPS = 1e-6
LN_EPS = 1e-5
ALPHA = math.sqrt(2.0)
QSCALE = 0.125
NW = 2
NRAW = 2
FF1 = 4096
FF2 = 2816

VECS = [("ada_b", 48), ("norm1_g", 8), ("norm2_g", 8), ("final_g", 8), ("b_ada_2", 96), ("b_ada_kv_2", 16),
        ("ln1_g_2", 16), ("ln1_b_2", 16), ("ln2_g_2", 16), ("ln2_b_2", 16), ("conv_w_2", 24)]
VCOL = {}
_n = 0
for _name, _w in VECS:
    VCOL[_name] = _n
    _n += _w
NV = _n
C_ID, C_J, C_ONE, C_MASK, C_HEAD = 0, 128, 256, 384, 896
NC = 912


def buckets(dist):
    n = np.maximum(dist, 0)
    nf = np.maximum(n, 1).astype(np.float32)
    large = 16 + (np.log(nf / np.float32(16)) / np.float32(math.log(128.0)) * np.float32(16)).astype(np.int32)
    return np.where(n < 16, n, np.minimum(large, 31))


def constants():
    c = np.zeros((P, NC), np.float32)
    i = np.arange(P)
    c[i, C_ID + i] = 1.0
    c[i, C_J + P - 1 - i] = 1.0
    c[:, C_ONE:C_ONE + P] = 1.0 / D
    j = np.arange(T)
    c[:, C_MASK:C_MASK + T] = np.where(384 + i[:, None] - j[None, :] >= 0, 0.0, NEG)
    c[:, C_HEAD:C_HEAD + 16] = (i[:, None] % 32 == np.arange(16)[None, :])
    hot = np.zeros((33, 1024), np.float32)
    for col, dist, ok in [(m, 511 - m, 511 - m >= 0) for m in range(640)] + \
                         [(640 + m, 255 - m, 0 <= 255 - m < 128) for m in range(384)]:
        hot[int(buckets(np.array(dist))) if ok else 32, col] = 1.0
    return c, hot


class Bind:

    def matmul(self, *a, **k):
        return lambda e: e.matmul(*a, **k)

    def transpose(self, *a, **k):
        return lambda e: e.transpose(*a, **k)

    def activation(self, *a, **k):
        return lambda e: e.activation(*a, **k)

    def tensor_tensor(self, *a, **k):
        return lambda e: e.tensor_tensor(*a, **k)

    def tensor_scalar(self, *a, **k):
        return lambda e: e.tensor_scalar(*a, **k)

    def tensor_copy(self, *a, **k):
        return lambda e: e.tensor_copy(*a, **k)

    def scalar_tensor_tensor(self, *a, **k):
        return lambda e: e.scalar_tensor_tensor(*a, **k)

    def tensor_tensor_reduce(self, *a, **k):
        return lambda e: e.tensor_tensor_reduce(*a, **k)

    def tensor_tensor_scan(self, *a, **k):
        return lambda e: e.tensor_tensor_scan(*a, **k)

    def reciprocal(self, *a, **k):
        return lambda e: e.reciprocal(*a, **k)

    def memset(self, *a, **k):
        return lambda e: e.memset(*a, **k)

    def dma(self, sem, *a, **k):
        return lambda e: e.dma_start(*a, **k).then_inc(sem, 16)


BIND = Bind()


class Engine:

    def __init__(self, sem, serial=False):
        self.sem, self.count, self.ops, self.seen, self.serial = sem, 0, [], {}, serial

    def put(self, waits, fn, inc=True):
        need = {}
        stack = [waits, self.last() if self.serial and self.count else None]
        while stack:
            w = stack.pop()
            if isinstance(w, list):
                stack.extend(w)
            elif w is not None:
                sem, value = w
                if value > self.seen.get(id(sem), 0):
                    self.seen[id(sem)] = value
                    need[id(sem)] = sem
        self.ops.append(([(s, self.seen[k]) for k, s in need.items()], fn(BIND), inc))
        if inc:
            self.count += 1
        return (self.sem, self.count)

    def last(self):
        return (self.sem, self.count)

    def replay(self, eng):
        for waits, fn, inc in self.ops:
            for sem, value in waits:
                eng.wait_ge(sem, value)
            ins = fn(eng)
            if inc:
                ins.then_inc(self.sem, 1)


class Buf:

    def __init__(self, ap, rel=None):
        self.ap, self.rel = ap, list(rel or [])


class Ring:
    def __init__(self, bufs):
        self.bufs, self.n = bufs, 0

    def next(self):
        self.n += 1
        return self.bufs[(self.n - 1) % len(self.bufs)]


class DmaSem:
    def __init__(self, sem):
        self.sem, self.count = sem, 0


def build(nc, a, out_t, scratch):
    ctx = ExitStack()
    with ctx:
        names = [0]

        def sb(stack, shape, dt):
            names[0] += 1
            return stack.enter_context(nc.sbuf_tensor(f"t{names[0]}", [P] + shape, dt))

        def semaphore(name):
            return ctx.enter_context(nc.semaphore(name))

        pe, act, dve, pool, sp = (Engine(semaphore(f"s_{n}"), n == "pool") for n in ("pe", "act", "dve", "pool", "sp"))
        ndma = [0]

        def dsem():
            ndma[0] += 1
            return DmaSem(semaphore(f"d{ndma[0]}"))

        stores = []

        def dma(ds, waits, dst, src):
            ds.count += 16
            s = ds.sem
            sp.put(waits, lambda e: e.dma(s, dst, src), inc=False)
            return (s, ds.count)

        def barrier():
            return [e.last() for e in (pe, act, dve, pool)] + list(stores)

        psum = [Buf(ctx.enter_context(nc.psum_tensor(f"ps{i}", [P, T], F))) for i in range(8)]

        x_t = sb(ctx, [KT, T], F)
        raw = sb(ctx, [NRAW, 2048], F)
        WH = sb(ctx, [NW, 2048], R)
        WL = sb(ctx, [NW, 2048], R)
        H_t = sb(ctx, [2, KT, T], R)
        csb = sb(ctx, [D], F)
        vec = sb(ctx, [NV], F)
        mods = sb(ctx, [160], F)
        cst = sb(ctx, [NC], F)
        cols = sb(ctx, [64], F)
        stat = sb(ctx, [2, 5, 4], F)
        small = sb(ctx, [32], F)

        ident = cst[:, C_ID:C_ID + P]
        Jm = cst[:, C_J:C_J + P]
        ones = cst[:, C_ONE:C_ONE + P]
        maskT = cst[:, C_MASK:C_MASK + T]
        hmask = cst[:, C_HEAD:C_HEAD + 16]
        zcol, rmse, lne = cols[:, 0:1], cols[:, 1:2], cols[:, 2:3]
        X = [Buf(x_t[:, k, :]) for k in range(KT)]
        xt = [[] for _ in range(KT)]

        d_c, d_v, d_x, d_cs, d_s = (dsem() for _ in range(5))
        t_cst = dma(d_c, [], cst[:, :], a["consts"])
        t_vec = dma(d_v, [], vec[:, :], a["vecs"])
        t_cb = dma(d_cs, [], csb[:, :], a["c_b"])
        t_sink = dma(d_s, [], small[:, 0:8], a["sinks"])
        t_sink = dma(d_s, [], small[0:16, 8:9], a["b_f"])
        xload = [None, None]
        dx = [dsem(), dsem()]

        def load_x(waits):
            for hf in range(2):
                k0 = 4 * hf
                xload[hf] = dma(dx[hf], waits, x_t[:, k0:k0 + 4, :],
                                a["x_t"][k0 * P:(k0 + 4) * P, :].rearrange("(kt p) n -> p kt n", p=P))
                for k in range(k0, k0 + 4):
                    xt[k] = [xload[hf]]

        load_x([])
        t_col = [dve.put([], lambda e, v=v, i=i: e.memset(cols[:, i:i + 1], v))
                 for i, v in enumerate((0.0, RMS_EPS, LN_EPS))]

        plan = []

        def plan_A(w, r0, c0, n):
            plan.extend(("A", w, r0 + 512 * s, c0) for s in range(n))

        def plan_B(w, c0):
            plan.append(("B", w, 0, c0))

        for c0 in (0, 256, 512, 768, 1024):
            plan_B("w_in", c0)
        plan_B("w_in", 1280)
        plan_B("w_in", 1792)
        plan_B("w_in", 1536)
        plan_B("w_in", 2048)
        for hf in range(2):
            plan_A("w_in", 0, 2304 + 512 * hf, 2)
            plan_A("w_branch_a", 0, 512 * hf, 1)
            plan_A("w_in", 0, 3328 + 512 * hf, 2)
            plan_A("w_branch_b", 0, 512 * hf, 1)
        for hf in range(2):
            plan_A("w_out", 0, 512 * hf, 2)
        for f in range(FF1 // 512):
            plan_A("w_mlp_in", 0, 512 * f, 2)
            for hf in range(2):
                plan_A("w_mlp_out", 512 * f, 512 * hf, 1)

        def plan_ffn2(l):
            for f in range(5):
                plan_A(f"gate{l}", 0, 512 * f, 2)
                plan_A(f"up{l}", 0, 512 * f, 2)
                for hf in range(2):
                    plan_A(f"down{l}", 512 * f, 512 * hf, 1)
            plan_B(f"gate{l}", 2560)
            plan_B(f"up{l}", 2560)
            plan.append(("C", f"down{l}", 2560, 0))

        for hf in range(2):
            for c0 in (1024, 2048, 0):
                plan_A("conv_w_in_2", 0, c0 + 512 * hf, 2)
        for hf in range(2):
            plan_A("conv_w_out_2", 0, 512 * hf, 2)
        plan_ffn2(0)
        for hf in range(2):
            plan_A("attn_w_q_2", 0, 512 * hf, 2)
        for g in range(4):
            plan_B("w_k_2", 256 * g)
            plan_B("w_v_2", 256 * g)
        for hf in range(2):
            plan_A("attn_w_o_2", 0, 512 * hf, 2)
        plan_ffn2(1)

        raw_rel = [[] for _ in range(NRAW)]
        raw_sem = [dsem() for _ in range(NRAW)]
        raw_n = [0]
        w_rel = [[] for _ in range(NW)]
        w_dma, w_conv = {}, {}
        state = {"dma": 0, "conv": 0, "take": 0}
        SHAPE = {"A": (4, 512), "B": (8, 256), "C": (2, 1024)}

        raw_busy = [False] * NRAW

        def raw_slot():
            while raw_busy[raw_n[0] % NRAW]:
                raw_n[0] += 1
                assert not all(raw_busy)
            r = raw_n[0] % NRAW
            raw_n[0] += 1
            raw_busy[r] = True
            return r

        def raw_done(r, tickets):
            raw_rel[r] = tickets
            raw_busy[r] = False

        def slot_dma():
            n = state["dma"]
            if n >= len(plan):
                return
            kind, w, r0, c0 = plan[n]
            kt, nn = SHAPE[kind]
            r = raw_slot()
            src = a[w][r0:r0 + kt * P, c0:c0 + nn].rearrange("(kt p) n -> p kt n", p=P)
            dst = raw[:, r, :].rearrange("p (kt n) -> p kt n", kt=kt)
            w_dma[n] = (r, dma(raw_sem[r], raw_rel[r], dst, src))
            state["dma"] += 1

        def slot_conv():
            n = state["conv"]
            if n >= len(plan):
                return
            r, landed = w_dma.pop(n)
            b = n % NW
            hi = act.put([landed, w_rel[b]], lambda e: e.activation(WH[:, b, :], raw[:, r, :], ACT.Copy))
            lo = dve.put([landed, hi, w_rel[b]], lambda e: e.tensor_tensor(
                WL[:, b, :], raw[:, r, :], WH[:, b, :].bitcast(F), ALU.subtract))
            raw_done(r, [hi, lo])
            w_conv[n] = [hi, lo]
            state["conv"] += 1

        class Slot:
            pass

        def take(kind, w, r0, c0):
            n = state["take"]
            assert plan[n] == (kind, w, r0, c0), (plan[n], kind, w, r0, c0)
            while state["conv"] <= n:
                while state["dma"] <= state["conv"]:
                    slot_dma()
                slot_conv()
            ada_step()
            if state["dma"] > n + 1:
                slot_conv()
            while state["dma"] < min(len(plan), n + 2):
                slot_dma()
            if state["conv"] < min(len(plan), n + 2):
                slot_conv()
            slot_dma()
            ada_load()
            state["take"] += 1
            s = Slot()
            kt, nn = SHAPE[kind]
            b = n % NW
            s.hi = WH[:, b, :].rearrange("p (kt n) -> p kt n", kt=kt)
            s.lo = WL[:, b, :].rearrange("p (kt n) -> p kt n", kt=kt)
            s.ready = w_conv.pop(n)
            s.b = b
            return s

        def release(s, ticket):
            w_rel[s.b] = [ticket]

        ada = []
        ada_pending = []
        cs_ready = [None]
        cs_last = [None]
        mod_raw = {}

        def ada_jobs(name, row0, nrows, col0, which):
            for r in range(0, nrows, 256):
                ada.append((name, row0 + r, col0 + r // P, which))

        def silu_c(which, waits, landed):
            sg = raw_slot()
            t = act.put([landed, raw_rel[sg]], lambda e: e.activation(raw[:, sg, 0:D], csb[:, :], ACT.Sigmoid))
            t = dve.put([t], lambda e: e.tensor_tensor(csb[:, :], csb[:, :], raw[:, sg, 0:D], ALU.mult))
            raw_done(sg, [t])
            cs_ready[0] = t

        cs_now = [0]

        def ada_load():
            if not ada or len(ada_pending) >= 1:
                return
            if ada[0][3] != cs_now[0]:
                landed = dma(d_cs, [cs_last[0]], csb[:, :], a["c_b2"])
                silu_c(1, [], landed)
                cs_now[0] = ada[0][3]
            name, row, col, _ = ada.pop(0)
            r = raw_slot()
            src = a[name][row:row + 256, :].rearrange("(a p) k -> p a k", p=P)
            dst = raw[:, r, :].rearrange("p (a k) -> p a k", a=2)
            ada_pending.append((r, dma(raw_sem[r], raw_rel[r], dst, src), col))

        def ada_step():
            while ada_pending:
                r, landed, col = ada_pending.pop(0)
                t = None
                for i in range(2):
                    v = raw[:, r, i * D:(i + 1) * D]
                    t = dve.put([landed, cs_ready[0]], lambda e, v=v, i=i: e.tensor_tensor_reduce(
                        out=v, in0=v, in1=csb[:, :], scale=1.0, scalar=0.0, op0=ALU.mult, op1=ALU.add,
                        accum_out=mods[:, col + i:col + i + 1]))
                raw_done(r, [t])
                cs_last[0] = t
                mod_raw[col] = t

        def ada_until(col_end, col0):
            while any(j[2] < col_end for j in ada) or ada_pending:
                ada_load()
                ada_step()
            return [mod_raw[c] for c in range(col0, col_end, 2)]

        def mod_bias(col0, n, vcol):
            w = ada_until(col0 + n, col0)
            return dve.put([w, t_vec], lambda e: e.tensor_tensor(
                mods[:, col0:col0 + n], mods[:, col0:col0 + n], vec[:, vcol:vcol + n], ALU.add))

        def mcol(v, k):
            return mods[:, v * 8 + k:v * 8 + k + 1]

        def vcol(name, k):
            return vec[:, VCOL[name] + k:VCOL[name] + k + 1]

        def mm3(bank, w_hi, w_lo, h_hi, h_lo, first, last, waits, inc):
            pe.put(waits, lambda e: e.matmul(bank, w_hi, h_hi, start=first, stop=False), inc=False)
            pe.put([], lambda e: e.matmul(bank, w_hi, h_lo, start=False, stop=False), inc=False)
            return pe.put([], lambda e: e.matmul(bank, w_lo, h_hi, start=False, stop=last), inc=inc)

        def gemm_A(w, r0, c0, nslots, rhs, bset, evac):
            banks = [psum[4 * bset + i] for i in range(4)]
            done = [None] * 4
            for s in range(nslots):
                sl = take("A", w, r0 + 512 * s, c0)
                for kt in range(4):
                    hi, lo, tk = rhs(4 * s + kt)
                    first, last = s == 0 and kt == 0, s == nslots - 1 and kt == 3
                    for i in range(4):
                        c = slice(i * P, (i + 1) * P)
                        done[i] = mm3(banks[i].ap[:, :], sl.hi[:, kt, c], sl.lo[:, kt, c], hi, lo, first, last,
                                      [sl.ready, tk, banks[i].rel if first else None], last or (kt == 3 and i == 3))
                release(sl, done[3])
            for i in range(4):
                evac(i, banks[i], done[i])

        def gemm_B(w, c0, rhs, ring, evac):
            sl = take("B", w, 0, c0)
            for i in range(2):
                bank = ring.next()
                for kt in range(8):
                    hi, lo, tk = rhs(kt)
                    c = slice(i * P, (i + 1) * P)
                    t = mm3(bank.ap[:, :], sl.hi[:, kt, c], sl.lo[:, kt, c], hi, lo, kt == 0, kt == 7,
                            [sl.ready, tk, bank.rel if kt == 0 else None], kt == 7)
                    yield
                if i == 1:
                    release(sl, t)
                evac(i, bank, t)

        def gemm_V(w, c0, lhs, ring, evac):
            sl = take("B", w, 0, c0)
            for pair in range(2):
                bank = ring.next()
                for hf in range(2):
                    tok = slice((2 * pair + hf) * P, (2 * pair + hf + 1) * P)
                    o = bank.ap[:, 256 * hf:256 * hf + 256]
                    for kt in range(8):
                        hi, lo, tk = lhs(kt)
                        t = mm3(o, hi[:, tok], lo[:, tok], sl.hi[:, kt, :], sl.lo[:, kt, :], kt == 0, kt == 7,
                                [sl.ready, tk, bank.rel if kt == 0 and hf == 0 else None], kt == 7)
                        if kt % 2:
                            yield
                if pair == 1:
                    release(sl, t)
                evac(pair, bank, t)

        def run(gen):
            for _ in gen or ():
                pass

        def chain(*gens):
            for g in gens:
                yield from g

        def split(src, hi_ap, lo_ap, waits, hi_waits):
            hi = act.put([waits, hi_waits], lambda e: e.activation(hi_ap, src, ACT.Copy))
            lo = dve.put([waits, hi, hi_waits], lambda e: e.tensor_tensor(lo_ap, src, hi_ap.bitcast(F), ALU.subtract))
            return [hi, lo]

        def column_sum(stack_bufs, src, waits, bank):
            acc, = stack_bufs
            t = None
            for k in range(KT):
                if k == 0:
                    t = dve.put([waits[k], acc.rel], lambda e: e.tensor_copy(acc.ap, src(0)))
                else:
                    t = dve.put([waits[k], t], lambda e, k=k: e.tensor_tensor(acc.ap, acc.ap, src(k), ALU.add))
            t = pe.put([t, bank.rel, t_cst], lambda e: e.matmul(bank.ap[:, :], ones, acc.ap, start=True, stop=True))
            acc.rel = [t]
            return t

        def square_sum(acc, sq, src, waits, bank):
            t = None
            for k in range(KT):
                if k == 0:
                    t = act.put([waits[k], acc.rel], lambda e: e.activation(acc.ap, src(0), ACT.Square))
                else:
                    b = sq.next()
                    ts = act.put([waits[k], b.rel], lambda e, k=k, b=b: e.activation(b.ap, src(k), ACT.Square))
                    t = dve.put([ts, t], lambda e, b=b: e.tensor_tensor(acc.ap, acc.ap, b.ap, ALU.add))
                    b.rel = [t]
            t = pe.put([t, bank.rel, t_cst], lambda e: e.matmul(bank.ap[:, :], ones, acc.ap, start=True, stop=True))
            acc.rel = [t]
            return t

        def rstd(rs, bank, ticket, eps):
            t = act.put([ticket, rs.rel, t_col], lambda e: e.activation(rs.ap, bank.ap[:, :], ACT.Sqrt, bias=eps))
            bank.rel = [t]
            return dve.put([t], lambda e: e.reciprocal(rs.ap, rs.ap))

        def norm_bufs(stack, rel):
            tm = Ring([Buf(sb(stack, [T], F)[:, :], rel) for _ in range(3)])
            sq = Ring([Buf(sb(stack, [T], F)[:, :], rel) for _ in range(2)])
            return dict(tm=tm, sq=sq, acc=Buf(sb(stack, [T], F)[:, :], rel), rs=Buf(sb(stack, [T], F)[:, :], rel))

        def modulated(nb, k, src, waits, A, B, cw, dst, rel):
            b = nb["tm"].next()
            t = act.put([waits, cw, b.rel], lambda e: e.activation(b.ap, src, ACT.Identity, bias=B(k), scale=A(k)))
            tk = split(b.ap, dst[0][:, k, :], dst[1][:, k, :], [t], rel)
            b.rel = tk
            return t, tk

        def halves(t):
            return (t[:, 0, :, :], t[:, 1, :, :])

        HH = halves(H_t)
        Ht = [[] for _ in range(KT)]
        Hrel = [[]]

        def rhs_H(k):
            return HH[0][:, k, :], HH[1][:, k, :], Ht[k]

        def normed(nb, layer, eps):
            if layer:
                t = column_sum((nb["acc"],), lambda k: X[k].ap, xt, psum[7])
                for k in range(KT):
                    xt[k] = [dve.put([t, xt[k]], lambda e, k=k: e.tensor_tensor(
                        X[k].ap, X[k].ap, psum[7].ap[:, :], ALU.subtract))]
                psum[7].rel = [xt[KT - 1]]
            t = square_sum(nb["acc"], nb["sq"], lambda k: X[k].ap, xt, psum[3])
            return rstd(nb["rs"], psum[3], t, eps)

        def plus_one(dst, v, w, g=None):
            src = mods[:, v * 8:v * 8 + 8]
            t = dve.put([w, t_vec], lambda e: e.tensor_scalar(dst, src, 1.0, None, ALU.add))
            if g is not None:
                t = dve.put([t], lambda e: e.tensor_tensor(dst, dst, vec[:, VCOL[g]:VCOL[g] + 8], ALU.mult))
            return t

        cA = cols[:, 8:16]
        cB = cols[:, 16:24]

        def colf(t):
            return lambda k: t[:, k:k + 1]

        def rms_h(nb, w, v_shift):
            t_rs = normed(nb, False, rmse)
            for k in range(KT):
                b = nb["tm"].next()
                t = dve.put([t_rs, xt[k], b.rel], lambda e, k=k, b=b: e.tensor_tensor(
                    b.ap, X[k].ap, nb["rs"].ap, ALU.mult))
                t = act.put([t, w], lambda e, k=k, b=b: e.activation(
                    b.ap, b.ap, ACT.Identity, bias=mcol(v_shift, k), scale=cA[:, k:k + 1]))
                Ht[k] = split(b.ap, HH[0][:, k, :], HH[1][:, k, :], [t], Hrel[0])
                b.rel = Ht[k]
                nb["rs"].rel = [t]

        def renorm(nb, layer, eps, g, bias, hs, keep_scale, hook=None):
            t_rs = normed(nb, layer, eps)
            for k in range(KT):
                b = nb["tm"].next()
                t = dve.put([t_rs, xt[k], b.rel], lambda e, k=k, b=b: e.tensor_tensor(
                    b.ap, X[k].ap, nb["rs"].ap, ALU.mult))
                nb["rs"].rel = [t]
                t = act.put([t, t_vec, t_col], lambda e, k=k, b=b: e.activation(
                    X[k].ap, b.ap, ACT.Identity, bias=bias(k), scale=g(k)))
                b.rel = [t]
                xt[k] = [t]
                reads = [t]
                for A, B, w, dst, tick, rel in hs:
                    tr, tick[k] = modulated(nb, k, X[k].ap, xt[k], A, B, w, dst, rel)
                    reads.append(tr)
                if keep_scale is not None:
                    xt[k] = [pool.put(reads, lambda e, k=k: e.tensor_scalar(
                        X[k].ap, X[k].ap, keep_scale, 1.0, ALU.mult, ALU.mult))]

        def residual(k, bank, tk, gate, w):
            xt[k] = [dve.put([tk, xt[k], w], lambda e: e.scalar_tensor_tensor(
                out=X[k].ap, in0=bank.ap[:, :], scalar=gate, in1=X[k].ap, op0=ALU.mult, op1=ALU.add))]
            bank.rel = xt[k]

        S_ring = Ring([psum[0], psum[1]])
        T_ring = Ring([psum[2], psum[3]])
        O_ring = Ring([psum[4]])
        G_ring = Ring([psum[5], psum[6], psum[7]])
        OFF = {"causal": [0, 128, 384, 768], "swa": [0, 128, 384, 640]}

        class Head:
            pass

        def scores(h, ab):
            off = OFF[h.kind]
            st = ab.stats.next()
            sp_ = ab.sp.next()
            h.st, h.sp = st, sp_
            mx, nm, sm, es = (st.ap[:, q, :] for q in (0, 1, 2, 3))
            h.exp = [None] * 4
            nms = []
            for i in range(4):
                k0 = 0 if h.kind == "causal" else max(0, i - 1) * P
                n = (i + 1) * P - k0
                N = max(256, n)
                bank = S_ring.next()
                o = bank.ap[:, 0:N]
                tok = slice(i * P, (i + 1) * P)
                w = [h.q_ready, h.k_ready, bank.rel]
                kr = slice(k0, k0 + N)
                pairs = [(h.q[0][:, tok], h.k[0][:, kr]), (h.q[1][:, tok], h.k[0][:, kr]),
                         (h.q[0][:, tok], h.k[1][:, kr])]
                if h.extra:
                    pairs.append((h.extra[0][:, tok], h.extra[1][:, kr]))
                    w.append(h.extra[2])
                for m, (lt, rr) in enumerate(pairs):
                    tk = pe.put(w if m == 0 else [], lambda e, lt=lt, rr=rr, m=m: e.matmul(
                        o, lt, rr, start=m == 0, stop=m == len(pairs) - 1), inc=m == len(pairs) - 1)
                h.s_done = tk
                piece = sp_.ap[:, off[i]:off[i] + n]
                bias = h.bias(i)
                t = dve.put([tk, h.bias_ready, sp_.rel, st.rel], lambda e: e.tensor_tensor_reduce(
                    out=piece, in0=bank.ap[:, 0:n], in1=bias, scale=1.0, scalar=LOW, op0=ALU.add, op1=ALU.max,
                    accum_out=mx[:, i:i + 1]))
                bank.rel = [t]
                h.bias_done = t
                top = h.sink if h.sink is not None else LOW
                t = dve.put([t, t_sink], lambda e: e.tensor_scalar(
                    nm[:, i:i + 1], mx[:, i:i + 1], top, -1.0, ALU.max, ALU.mult))
                nms.append(t)
                h.exp[i] = act.put([t], lambda e: e.activation(
                    piece, piece, ACT.Exp, bias=nm[:, i:i + 1], accum_out=sm[:, i:i + 1]))
                yield
            if h.sink is not None:
                h.es = act.put([nms, st.rel], lambda e: e.activation(es, nm, ACT.Exp, bias=h.sink))

        def weighted(h, ab):
            off = OFF[h.kind]
            st, sp_ = h.st, h.sp
            sm, es, rs = (st.ap[:, q, :] for q in (2, 3, 4))
            t = None
            if h.sink is not None:
                t = dve.put([h.exp, h.es], lambda e: e.tensor_tensor(sm, sm, es, ALU.add))
            t = dve.put([h.exp, t, st.rel], lambda e: e.reciprocal(rs, sm))
            norm = [None] * 4
            for i in range(4):
                n = ((i + 1) if h.kind == "causal" else min(2, i + 1)) * P
                piece = sp_.ap[:, off[i]:off[i] + n]
                norm[i] = pool.put([t, h.exp[i]], lambda e, i=i, piece=piece: e.tensor_scalar(
                    piece, piece, rs[:, i:i + 1], 1.0, ALU.mult, ALU.mult))
            st.rel = norm
            if h.kind == "causal":
                groups = [[0], [1], [2], [3]]
                blocks = {j: list(range(j, 4)) for j in range(4)}
                base = [0, 512, 896, 1152]
                order = [0, 1, 2, 3]
                need = {0: 0, 1: 1, 2: 2, 3: 3}
                sched = ["t0", "t1", "v0", "t2", "v1", "t3", "v2", "v3"]
            else:
                groups = [[0, 1], [2, 3]]
                blocks = {0: [0, 1], 1: [1, 2], 2: [2, 3], 3: [3]}
                base = [0, 256, 512, 768]
                need = {0: 0, 1: 0, 2: 1, 3: 1}
                sched = ["t0", "t1", "v0", "v2", "v1", "v3"]
            ready = {}
            bank = O_ring.next()
            for step in sched:
                if step[0] == "t":
                    g = groups[int(step[1])]
                    tb = T_ring.next()
                    pos = 0
                    tk = None
                    for j in g:
                        for i in blocks[j]:
                            col = off[i] + (j * P if h.kind == "causal" else (j - max(0, i - 1)) * P)
                            tk = pe.put([norm[i], tb.rel if pos == 0 else None], lambda e, pos=pos, col=col: e.transpose(
                                tb.ap[:, pos:pos + P], sp_.ap[:, col:col + P], ident), inc=True)
                            pos += P
                    b0 = base[g[0]]
                    hi_ap, lo_ap = ab.pt[0][:, b0:b0 + pos], ab.pt[1][:, b0:b0 + pos]
                    ready[int(step[1])] = split(tb.ap[:, 0:pos], hi_ap, lo_ap, [tk], ab.pt_rel[int(step[1])])
                    tb.rel = ready[int(step[1])]
                    h.t_done = tk
                else:
                    j = int(step[1])
                    n = len(blocks[j]) * P
                    o = bank.ap[:, j * P:j * P + n]
                    ph, pl = ab.pt[0][:, base[j]:base[j] + n], ab.pt[1][:, base[j]:base[j] + n]
                    vh, vl = h.v[0](j), h.v[1](j)
                    firstw = [bank.rel if j == 0 else None, h.v_ready, ready[need[j]]]
                    pe.put(firstw, lambda e, o=o, vh=vh, ph=ph, j=j: e.matmul(
                        o, vh, ph, start=j == 0, stop=False, skip_group_check=True), inc=False)
                    pe.put([], lambda e, o=o, vh=vh, pl=pl: e.matmul(
                        o, vh, pl, start=False, stop=False, skip_group_check=True), inc=False)
                    tk = pe.put([], lambda e, o=o, vl=vl, ph=ph, j=j: e.matmul(
                        o, vl, ph, start=False, stop=j == 3, skip_group_check=True))
                    ab.pt_rel[need[j]] = [tk]
                yield
            sp_.rel = [h.t_done]
            r = slice(h.r0, h.r0 + 64)
            h.out_ready = split(bank.ap[r, :], h.o[0][r, :], h.o[1][r, :], [tk], [h.s_done])
            bank.rel = h.out_ready
            h.done = tk

        def attend(heads, ab, gemm, per):
            def fill():
                for _ in range(per):
                    if next(gemm, 1) == 1:
                        return

            gemm = gemm if gemm is not None else iter(())
            heads[0].start()
            for _ in scores(heads[0], ab):
                fill()
            for n, h in enumerate(heads):
                nxt = None
                if n + 1 < len(heads):
                    heads[n + 1].start()
                    nxt = scores(heads[n + 1], ab)
                for _ in weighted(h, ab):
                    if nxt is not None and next(nxt, 1) == 1:
                        nxt = None
                    fill()
                if nxt is not None:
                    run(nxt)
            run(gemm)

        class AttnBufs:
            pass

        ada_jobs("ada_t", 0, 2048, 0, 0)
        silu_c(0, [], t_cb)
        slot_dma()
        ph = ExitStack()
        nb = norm_bufs(ph, [])
        tb33 = sb(ph, [16], F)
        hot = sb(ph, [1024], F)
        rrow = sb(ph, [1024], F)
        tz = Ring([Buf(sb(ph, [T], F)[:, :]) for _ in range(3)])
        tf = Ring([Buf(sb(ph, [T], F)[:, :]) for _ in range(3)])
        d_t, d_r = dsem(), dsem()
        t_tab = dma(d_t, [], tb33[0:32, :], a["rel_bias"])
        t_tab = dma(d_t, [], hot[0:33, :], a["hot"])
        t_m = dve.put([], lambda e: e.memset(tb33[32:33, :], NEG))
        tr = []
        for c0, n in ((0, 512), (512, 128), (640, 384)):
            bank = psum[c0 // 512] if c0 != 640 else psum[2]
            t = pe.put([t_tab, t_m], lambda e, bank=bank, c0=c0, n=n: e.matmul(
                bank.ap[0:16, 0:n], tb33[0:33, :], hot[0:33, c0:c0 + n], start=True, stop=True))
            t = act.put([t], lambda e, bank=bank, c0=c0, n=n: e.activation(
                rrow[0:16, c0:c0 + n], bank.ap[0:16, 0:n], ACT.Copy))
            bank.rel = [t]
            tr.append(t)
        t_rows = dma(d_r, tr, scratch["rows"][:, :], rrow[0:16, :])
        stores.append(t_rows)
        d_tz = [dsem() for _ in range(3)]
        d_tf = [dsem() for _ in range(3)]
        bias_in_dram = {}
        for h in range(16):
            n = 256 if h < 8 else 512
            z = tz.next()
            zi = h % 3
            base = scratch["rows"][0:1, 0:1]
            src = bass.AP(tensor=base.tensor, offset=h * 1024 + (640 if h < 8 else 0), ap=[[1, P], [1, n]])
            t = dma(d_tz[zi], [t_rows, z.rel], z.ap[:, 0:n], src)
            bank = psum[h % 3]
            t = pe.put([t, bank.rel, t_cst], lambda e, bank=bank, z=z, n=n: e.matmul(
                bank.ap[:, 0:n], Jm, z.ap[:, 0:n], start=True, stop=True))
            z.rel = [t]
            f = tf.next()
            t = act.put([t, f.rel], lambda e, bank=bank, f=f, n=n: e.activation(f.ap[:, 0:n], bank.ap[:, 0:n], ACT.Copy))
            bank.rel = [t]
            dst = scratch["toep"][h, :, 0:n]
            t = dma(d_tf[zi], [t], dst, f.ap[:, 0:n])
            f.rel = [t]
            bias_in_dram[h] = t
            stores.append(t)
        t_mod = mod_bias(0, 16, VCOL["ada_b"])
        w1 = plus_one(cA, 1, t_mod, "norm1_g")
        ada_jobs("ada_t", 2048, 4096, 16, 0)
        rms_h(nb, [w1, t_mod], 0)
        x_free = [Ht[k] for k in range(KT)] + [nb["rs"].rel]
        rel1 = barrier()
        ph.close()

        outer = ExitStack()
        Qa = sb(outer, [2, 4, T], R)
        Qb = sb(outer, [2, 4, T], R)
        ph = ExitStack()
        KV = [Buf(sb(ph, [6144], R), rel1) for _ in range(2)]
        pt_t = sb(ph, [2, 1280], R)

        def k_view(b):
            return b.ap[:, 0:4096].rearrange("p (s h n) -> p s h n", s=2, h=4)

        def v_view(b):
            return b.ap[:, 4096:6144].rearrange("p (s t n) -> p s t n", s=2, t=4)

        def zero_halves(b, rel):
            tks = []
            kv = k_view(b)
            for s in range(2):
                for odd in range(2):
                    r = slice(0, 64) if odd else slice(64, 128)
                    v = kv[r, s, odd::2, :].bitcast(F)
                    tks.append(pool.put(rel, lambda e, v=v: e.memset(v, 0.0)))
            return tks

        def attn_bufs(rel, pt):
            ab = AttnBufs()
            xf = x_t[:, :, :].rearrange("p k n -> p (k n)")
            ab.sp = Ring([Buf(xf[:, 0:1280], rel), Buf(xf[:, 1280:2560], rel)])
            ab.bias = Ring([Buf(xf[:, 2560:3072], rel), Buf(xf[:, 3072:3584], rel)])
            ab.stats = Ring([Buf(stat[:, 0, :, :], rel), Buf(stat[:, 1, :, :], rel)])
            ab.pt = (pt[:, 0, :], pt[:, 1, :])
            ab.pt_rel = [list(rel) for _ in range(4)]
            return ab

        ab = attn_bufs(rel1, pt_t)
        d_b = [dsem(), dsem()]
        nbias = [0]
        zeroed = [zero_halves(KV[i], rel1) for i in range(2)]

        def evac_q(dst, ready, t0, rel):
            def f(i, bank, tk):
                hi_ap, lo_ap = dst[:, 0, t0 + i, :], dst[:, 1, t0 + i, :]
                hi = act.put([tk, rel], lambda e: e.activation(hi_ap, bank.ap[:, :], ACT.Copy, scale=QSCALE))
                lo = dve.put([hi], lambda e: e.scalar_tensor_tensor(
                    out=lo_ap, in0=bank.ap[:, :], scalar=QSCALE, in1=hi_ap.bitcast(F), op0=ALU.mult, op1=ALU.subtract))
                bank.rel = [hi, lo]
                ready[t0 + i] = [hi, lo]
            return f

        def evac_k(b, ready):
            def f(i, bank, tk):
                kv = k_view(b)
                for odd in range(2):
                    r = slice(64 * odd, 64 * odd + 64)
                    n = 2 * i + odd
                    ready[n] = split(bank.ap[r, :], kv[r, 0, n, :], kv[r, 1, n, :], [tk], b.rel)
                bank.rel = [ready[2 * i], ready[2 * i + 1]]
            return f

        def evac_v(b, ready):
            def f(pair, bank, tk):
                vv = v_view(b)
                src = bank.ap[:, :].rearrange("p (t n) -> p t n", t=2)
                ready[pair] = split(src, vv[:, 0, 2 * pair:2 * pair + 2, :], vv[:, 1, 2 * pair:2 * pair + 2, :], [tk], b.rel)
                bank.rel = ready[pair]
            return f

        def group_heads(kv, zero, q, q_ready, k_ready, v_ready, t0, make):
            kk, vv = k_view(kv), v_view(kv)
            hs = []
            for n in range(4):
                h = Head()
                h.kind, h.sink, h.extra = "causal", None, None
                p = t0 + n // 2
                h.q = (q[:, 0, p, :], q[:, 1, p, :])
                h.q_ready = q_ready[p]
                h.k = (kk[:, 0, n, :], kk[:, 1, n, :])
                h.k_ready = [k_ready[n], zero]
                c = slice((n // 2) * P, (n // 2 + 1) * P)
                h.v = (lambda j, c=c: vv[:, 0, j, c], lambda j, c=c: vv[:, 1, j, c])
                h.v_ready = [v_ready[0], v_ready[1]]
                h.r0 = 64 * (n % 2)
                h.o = h.q
                make(h, n)
                hs.append(h)
            return hs

        def bias_loader(h, table, n):
            def start():
                b = ab.bias.next()
                i = nbias[0] % 2
                nbias[0] += 1
                h.bias_ready = dma(d_b[i], [b.rel, bias_in_dram[table], x_free], b.ap[:, 0:n],
                                   scratch["toep"][table, :, 0:n])
                if n == 256:
                    h.bias = lambda q: b.ap[:, 128 if q == 0 else 0:256]
                else:
                    h.bias = lambda q: b.ap[:, 128 * (3 - q):512]
                h.bias_buf = b
            return start

        qa_ready, qb_ready = [None] * 4, [None] * 4
        for c in range(2):
            run(gemm_B("w_in", 256 * c, rhs_H, G_ring, evac_q(Qa, qa_ready, 2 * c, rel1)))
        ka_ready, va_ready = {}, {}
        vt = Buf(x_t[:, 7, :], [x_free])

        def evac_kva(i, bank, tk):
            if i == 0:
                evac_k(KV[0], ka_ready)(0, bank, tk)
                return
            t = act.put([tk, vt.rel], lambda e: e.activation(vt.ap, bank.ap[:, :], ACT.Copy))
            bank.rel = [t]
            tb = T_ring.next()
            for j in range(4):
                tk = pe.put([t, tb.rel, t_cst], lambda e, j=j: e.transpose(
                    tb.ap[:, j * P:(j + 1) * P], vt.ap[:, j * P:(j + 1) * P], ident))
            vv = v_view(KV[0])
            src = tb.ap[:, :].rearrange("p (t n) -> p t n", t=4)
            va_ready[0] = split(src, vv[:, 0, :, 0:P], vv[:, 1, :, 0:P], [tk], KV[0].rel)
            tb.rel = va_ready[0]

        run(gemm_B("w_in", 512, rhs_H, G_ring, evac_kva))

        swa = []
        for n in range(8):
            t_, g = n % 4, n // 4
            h = Head()
            h.kind, h.extra = "swa", None
            hd = t_ + 4 * g
            h.sink = small[:, hd:hd + 1]
            h.q = (Qa[:, 0, t_, :], Qa[:, 1, t_, :])
            h.q_ready = qa_ready[t_]
            kk, vv = k_view(KV[0]), v_view(KV[0])
            h.k = (kk[:, 0, g, :], kk[:, 1, g, :])
            h.k_ready = [ka_ready[g], zeroed[0]]
            h.v = (lambda j: v_view(KV[0])[:, 0, j, 0:P], lambda j: v_view(KV[0])[:, 1, j, 0:P])
            h.v_ready = va_ready[0]
            h.r0 = 64 * g
            h.o = h.q
            h.start = bias_loader(h, hd, 256)
            swa.append(h)
        kb_ready = [{}, {}]
        vb_ready = [{}, {}]

        def kv_gemm(g, wk, ck, wv, cv, rhs, buf):
            return chain(gemm_B(wk, ck, rhs, G_ring, evac_k(buf, kb_ready[g % 2])),
                         gemm_V(wv, cv, rhs, G_ring, evac_v(buf, vb_ready[g % 2])))

        def with_bias_release(heads):
            return heads

        def release_bias(h):
            h.bias_buf.rel = [h.bias_done]

        def wrap(hs):
            for n, h in enumerate(hs):
                s0 = h.start

                def start(h=h, s0=s0, n=n):
                    if n >= 2:
                        release_bias(hs[n - 2])
                    s0()
                h.start = start
            return hs

        attend(wrap(swa), ab, chain(
            gemm_B("w_in", 768, rhs_H, G_ring, evac_q(Qb, qb_ready, 0, rel1)),
            gemm_B("w_in", 1024, rhs_H, G_ring, evac_q(Qb, qb_ready, 2, rel1)),
            kv_gemm(1, "w_in", 1280, "w_in", 1792, rhs_H, KV[1])), ab_per := 2)
        for h in swa[-2:]:
            release_bias(h)
        oa_ready = [[swa[t_].out_ready, swa[t_ + 4].out_ready] for t_ in range(4)]
        KV[0].rel = [swa[-1].done]
        ob_ready = [None] * 4
        for g in range(2):
            kv = KV[(g + 1) % 2]

            def make(h, n, g=g):
                h.start = bias_loader(h, 8 + 4 * g + n, 512)

            hs = group_heads(kv, zeroed[(g + 1) % 2], Qb, qb_ready, kb_ready[(g + 1) % 2], vb_ready[(g + 1) % 2], 2 * g, make)
            nxt = kv_gemm(0, "w_in", 1536, "w_in", 2048, rhs_H, KV[0]) if g == 0 else None
            attend(wrap(hs), ab, nxt, 2)
            for h in hs[-2:]:
                release_bias(h)
            kv.rel = [hs[-1].done]
            for p in range(2):
                ob_ready[2 * g + p] = [hs[2 * p].out_ready, hs[2 * p + 1].out_ready]

        rel2 = barrier()
        ph.close()
        ph = ExitStack()
        MG = sb(ph, [2, KT, T], R)
        sg_r = Ring([Buf(sb(ph, [T], F)[:, :], rel2) for _ in range(4)])
        m_r = Ring([Buf(sb(ph, [T], F)[:, :], rel2) for _ in range(4)])
        y_r = Ring([Buf(sb(ph, [T], F)[:, :], rel2) for _ in range(2)])
        load_x(rel2)
        MGt = [None] * KT

        def rhs_of(t, ready):
            return lambda k: (t[:, 0, k, :], t[:, 1, k, :], ready[k])

        for hf in range(2):
            sgs, ms = [None] * 4, [None] * 4

            def evac_sig(i, bank, tk):
                b = sg_r.next()
                t = act.put([tk, b.rel], lambda e: e.activation(b.ap, bank.ap[:, :], ACT.Sigmoid))
                bank.rel = [t]
                sgs[i] = (b, t)

            def evac_ya(i, bank, tk):
                b, t = sgs[i]
                m = m_r.next()
                t = dve.put([tk, t, m.rel], lambda e: e.tensor_tensor(m.ap, bank.ap[:, :], b.ap, ALU.mult))
                bank.rel = [t]
                b.rel = [t]
                ms[i] = (m, t)

            def evac_yb(i, bank, tk):
                b, t = sgs[i]
                y = y_r.next()
                m, tm_ = ms[i]
                t = dve.put([tk, t, y.rel], lambda e: e.tensor_tensor(y.ap, bank.ap[:, :], b.ap, ALU.mult))
                bank.rel = [t]
                b.rel = [t]
                t = pool.put([t, tm_], lambda e: e.tensor_tensor(m.ap, m.ap, y.ap, ALU.add))
                y.rel = [t]
                k = 4 * hf + i
                MGt[k] = split(m.ap, MG[:, 0, k, :], MG[:, 1, k, :], [t], rel2)
                m.rel = MGt[k]

            gemm_A("w_in", 0, 2304 + 512 * hf, 2, rhs_H, 0, evac_sig)
            gemm_A("w_branch_a", 0, 512 * hf, 1, rhs_of(Qa, oa_ready), 1, evac_ya)
            gemm_A("w_in", 0, 3328 + 512 * hf, 2, rhs_H, 0, evac_sig)
            gemm_A("w_branch_b", 0, 512 * hf, 1, rhs_of(Qb, ob_ready), 1, evac_yb)
        Hrel[0] = [pe.last()]
        t_mod = mod_bias(16, 32, VCOL["ada_b"] + 16)
        for l in range(2):
            ada_jobs(f"ada2_{l}", 0, 6144, 48 + 48 * l, 1)
        ada_jobs("adakv_t", 0, 2048, 144, 1)
        for hf in range(2):
            gemm_A("w_out", 0, 512 * hf, 2, rhs_of(MG, MGt), hf, lambda i, bank, tk, hf=hf: residual(
                4 * hf + i, bank, tk, mcol(2, 4 * hf + i), t_mod))
        rel3 = barrier()
        ph.close()
        outer.close()

        ph = ExitStack()
        nb = norm_bufs(ph, rel3)
        AC = [sb(ph, [2, 4, T], R) for _ in range(2)]
        f_r = Ring([Buf(sb(ph, [T], F)[:, :], rel3) for _ in range(4)])
        ac_rel = [rel3, rel3]
        w2 = plus_one(cA, 4, t_mod, "norm2_g")
        rms_h(nb, [w2, t_mod], 3)
        def mlp_in(f):
            act_t = AC[f % 2]
            ready = [None] * 4

            def evac(i, bank, tk):
                b = f_r.next()
                t = act.put([tk, b.rel], lambda e: e.activation(b.ap, bank.ap[:, :], ACT.Relu))
                bank.rel = [t]
                t = pool.put([t], lambda e: e.tensor_tensor(b.ap, b.ap, b.ap, ALU.mult))
                ready[i] = split(b.ap, act_t[:, 0, i, :], act_t[:, 1, i, :], [t], ac_rel[f % 2])
                b.rel = ready[i]
            gemm_A("w_mlp_in", 0, 512 * f, 2, rhs_H, 0, evac)
            return rhs_of(act_t, ready)

        for f in range(FF1 // 512):
            r = mlp_in(f)
            for hf in range(2):
                gemm_A("w_mlp_out", 512 * f, 512 * hf, 1, r, 1 - hf, lambda i, bank, tk, hf=hf: residual(
                    4 * hf + i, bank, tk, mcol(5, 4 * hf + i), t_mod))
            ac_rel[f % 2] = [pe.last()]
        Hrel[0] = [pe.last()]
        rel4 = barrier()
        ph.close()

        def mods2(l):
            return mod_bias(48 + 48 * l, 48, VCOL["b_ada_2"] + 48 * l)

        V0 = 6
        t_m2 = mods2(0)
        ph = ExitStack()
        nb = norm_bufs(ph, rel4)
        wA = plus_one(cA, V0 + 1, t_m2)
        zero = lambda k: zcol
        renorm(nb, False, rmse, lambda k: vcol("final_g", k), zero,
               [(colf(cA), lambda k: mcol(V0, k), [wA, t_m2, t_col], HH, Ht, Hrel[0])], ALPHA)

        YC = sb(ph, [2, KT, T], R)
        g_r = Ring([Buf(sb(ph, [T], F)[:, :], rel4) for _ in range(4)])
        u_r = Ring([Buf(sb(ph, [T + 2], F)[:, :], rel4) for _ in range(2)])
        c_r = Ring([Buf(sb(ph, [T], F)[:, :], rel4) for _ in range(4)])
        for b in u_r.bufs:
            b.rel = [pool.put([rel4], lambda e, b=b: e.memset(b.ap[:, 0:2], 0.0))]
        YCt = [None] * KT
        for hf in range(2):
            gs, cs = [None] * 4, [None] * 4

            def evac_gc(i, bank, tk):
                b = g_r.next()
                t = act.put([tk, b.rel], lambda e: e.activation(b.ap, bank.ap[:, :], ACT.Copy))
                bank.rel = [t]
                gs[i] = (b, t)

            def evac_v2(i, bank, tk):
                k = 4 * hf + i
                b, t = gs[i]
                u, c = u_r.next(), c_r.next()
                t = dve.put([tk, t, u.rel], lambda e: e.tensor_tensor(u.ap[:, 2:T + 2], bank.ap[:, :], b.ap, ALU.mult))
                bank.rel = [t]
                b.rel = [t]
                cw = [vec[:, VCOL["conv_w_2"] + 8 * j + k:VCOL["conv_w_2"] + 8 * j + k + 1] for j in range(3)]
                t = dve.put([t, c.rel, t_vec], lambda e: e.tensor_scalar(c.ap, u.ap[:, 0:T], cw[0], None, ALU.mult))
                for j in (1, 2):
                    t = dve.put([t], lambda e, j=j: e.scalar_tensor_tensor(
                        out=c.ap, in0=u.ap[:, j:T + j], scalar=cw[j], in1=c.ap, op0=ALU.mult, op1=ALU.add))
                u.rel = [t]
                cs[i] = (c, t)

            def evac_gb(i, bank, tk):
                k = 4 * hf + i
                c, t = cs[i]
                t = dve.put([tk, t], lambda e: e.tensor_tensor(c.ap, bank.ap[:, :], c.ap, ALU.mult))
                bank.rel = [t]
                YCt[k] = split(c.ap, YC[:, 0, k, :], YC[:, 1, k, :], [t], rel4)
                c.rel = YCt[k]

            gemm_A("conv_w_in_2", 0, 1024 + 512 * hf, 2, rhs_H, hf, evac_gc)
            gemm_A("conv_w_in_2", 0, 2048 + 512 * hf, 2, rhs_H, 1 - hf, evac_v2)
            gemm_A("conv_w_in_2", 0, 512 * hf, 2, rhs_H, hf, evac_gb)
        Hrel[0] = [pe.last()]
        for hf in range(2):
            gemm_A("conv_w_out_2", 0, 512 * hf, 2, rhs_of(YC, YCt), hf, lambda i, bank, tk, hf=hf: residual(
                4 * hf + i, bank, tk, mcol(V0 + 2, 4 * hf + i), t_m2))
        rel5 = barrier()
        ph.close()

        def ffn2(l, t_m):
            V = 6 + 6 * l
            st = ExitStack()
            rel = barrier()
            nb = norm_bufs(st, rel)
            AC = [sb(st, [2, 4, T], R) for _ in range(2)]
            g_r = Ring([Buf(sb(st, [T], F)[:, :], rel) for _ in range(4)])
            f_r = Ring([Buf(sb(st, [T], F)[:, :], rel) for _ in range(4)])
            ac_rel = [rel, rel]
            wA = plus_one(cA, V + 4, [t_m, rel])
            renorm(nb, True, lne, lambda k: vcol("ln1_g_2", 8 * l + k), lambda k: vcol("ln1_b_2", 8 * l + k),
                   [(colf(cA), lambda k: mcol(V + 3, k), [wA, t_m], HH, Ht, Hrel[0])], ALPHA)

            def evacs(f):
                act_t = AC[f % 2]
                ready = [None] * 4
                gs = [None] * 4

                def evac_g(i, bank, tk):
                    b = g_r.next()
                    t = act.put([tk, b.rel], lambda e: e.activation(b.ap, bank.ap[:, :], ACT.Silu))
                    bank.rel = [t]
                    gs[i] = (b, t)

                def evac_u(i, bank, tk):
                    g, t = gs[i]
                    b = f_r.next()
                    t = dve.put([tk, t, b.rel], lambda e: e.tensor_tensor(b.ap, bank.ap[:, :], g.ap, ALU.mult))
                    bank.rel = [t]
                    g.rel = [t]
                    ready[i] = split(b.ap, act_t[:, 0, i, :], act_t[:, 1, i, :], [t], ac_rel[f % 2])
                    b.rel = ready[i]

                return evac_g, evac_u, rhs_of(act_t, ready)

            def res(hf):
                return lambda i, bank, tk: residual(4 * hf + i, bank, tk, mcol(V + 5, 4 * hf + i), t_m)

            for f in range(5):
                eg, eu, r = evacs(f)
                gemm_A(f"gate{l}", 0, 512 * f, 2, rhs_H, 0, eg)
                gemm_A(f"up{l}", 0, 512 * f, 2, rhs_H, 1, eu)
                for hf in range(2):
                    gemm_A(f"down{l}", 512 * f, 512 * hf, 1, r, hf, res(hf))
                ac_rel[f % 2] = [pe.last()]
            eg, eu, r = evacs(5)
            run(gemm_B(f"gate{l}", 2560, rhs_H, Ring(psum[0:2]), eg))
            run(gemm_B(f"up{l}", 2560, rhs_H, Ring(psum[2:4]), eu))
            Hrel[0] = [pe.last()]
            sl = take("C", f"down{l}", 2560, 0)
            order = [4, 5, 6, 7, 0, 1, 2, 3]
            tks = [None] * 8
            for kt in range(2):
                hi, lo, tk = r(kt)
                for i in range(8):
                    bank = psum[order[i]]
                    c = slice(i * P, (i + 1) * P)
                    tks[i] = mm3(bank.ap[:, :], sl.hi[:, kt, c], sl.lo[:, kt, c], hi, lo, kt == 0, kt == 1,
                                 [sl.ready, tk, bank.rel if kt == 0 else None], kt == 1)
            release(sl, tks[7])
            for i in range(8):
                residual(i, psum[order[i]], tks[i], mcol(V + 5, i), t_m)
            st.close()

        ffn2(0, t_m2)

        t_m3 = mods2(1)
        t_kv = mod_bias(144, 16, VCOL["b_ada_kv_2"])
        V1 = 12
        rel6 = barrier()
        ph = ExitStack()
        Q2 = sb(ph, [2, KT, T], R)
        KVt = sb(ph, [12288], R)
        hq = KVt[:, 0:8192].rearrange("p (s k n) -> p s k n", s=2, k=KT)
        hq = (hq[:, 0, :, :], hq[:, 1, :, :])
        hqt = [None] * KT
        inner = ExitStack()
        nb = norm_bufs(inner, rel6)
        wA = plus_one(cA, V1 + 1, [t_m3, rel6])
        wB = plus_one(cB, 19, [t_kv, rel6])
        renorm(nb, True, lne, lambda k: vcol("ln2_g_2", k), lambda k: vcol("ln2_b_2", k),
               [(colf(cA), lambda k: mcol(V1, k), [wA, t_m3], hq, hqt, rel6),
                (colf(cB), lambda k: mcol(18, k), [wB, t_kv], HH, Ht, Hrel[0])], ALPHA)
        d_sx = dsem()
        t_spill = dma(d_sx, [xt[k] for k in range(KT)], scratch["x"][:, :].rearrange("(kt p) n -> p kt n", p=P), x_t[:, :, :])
        stores.append(t_spill)
        q_ready = [None] * KT
        for hf in range(2):
            gemm_A("attn_w_q_2", 0, 512 * hf, 2, lambda k: (hq[0][:, k, :], hq[1][:, k, :], hqt[k]), hf,
                   evac_q(Q2, q_ready, 4 * hf, rel6))
        q_done = pe.last()
        rel7 = barrier()
        inner.close()
        pt_t = sb(ph, [2, 1280], R)
        KV = [Buf(KVt[:, 6144 * i:6144 * (i + 1)], [q_done]) for i in range(2)]
        zeroed = [zero_halves(KV[i], [q_done]) for i in range(2)]
        AFr = Ring([Buf(sb(ph, [T], R), rel7) for _ in range(2)])
        BF = sb(ph, [T], R)
        st = ExitStack()
        xf = x_t[:, :, :].rearrange("p k n -> p (k n)")
        relx = [t_spill, rel7]
        AF = xf[:, 2560:3072]
        z1, z2, z3 = (xf[0:16, 512 * i:512 * (i + 1)] for i in range(3))
        fr = xf[0:16, 3072:3584]
        e1 = xf[0:16, 3584:4096]
        wfr = sb(st, [P], F)
        wfh, wfl, fhi = sb(st, [P], R), sb(st, [P], R), sb(st, [T], R)
        d_wf = dsem()
        t = dma(d_wf, rel7, wfr[:, :].rearrange("p (k n) -> p k n", k=8), a["w_f_2"].rearrange("(k p) n -> p k n", p=P))
        tw = split(wfr[:, :], wfh[:, :], wfl[:, :], [t], rel7)
        bank = psum[0]
        for k in range(KT):
            hi, lo, tk = rhs_H(k)
            t = mm3(bank.ap[0:16, :], wfh[:, 16 * k:16 * k + 16], wfl[:, 16 * k:16 * k + 16], hi, lo, k == 0, k == 7,
                    [tw, tk, bank.rel], True)
        t = act.put([t, relx], lambda e: e.activation(z1, bank.ap[0:16, :], ACT.Identity, bias=small[0:16, 8:9]))
        bank.rel = [t]
        tz1 = t
        t = act.put([t, relx], lambda e: e.activation(e1, z1, ACT.Abs))
        t = act.put([t], lambda e: e.activation(e1, e1, ACT.Exp, scale=-1.0))
        t = dve.put([t, relx], lambda e: e.tensor_scalar(z2, e1, 2.0, None, ALU.add))
        t = dve.put([t], lambda e: e.reciprocal(z2, z2))
        t = dve.put([t], lambda e: e.tensor_tensor(e1, e1, z2, ALU.mult))
        t = dve.put([t], lambda e: e.tensor_tensor(z2, e1, e1, ALU.mult))
        t = dve.put([t, relx], lambda e: e.tensor_scalar(z3, z2, 2.0 / 17, None, ALU.mult))
        for n in range(15, 2, -2):
            t = dve.put([t], lambda e, n=n: e.scalar_tensor_tensor(
                out=z3, in0=z3, scalar=2.0 / n, in1=z2, op0=ALU.add, op1=ALU.mult))
        t = dve.put([t], lambda e: e.scalar_tensor_tensor(out=z3, in0=z3, scalar=2.0, in1=e1, op0=ALU.add, op1=ALU.mult))
        t = dve.put([t, tz1], lambda e: e.scalar_tensor_tensor(out=z1, in0=z1, scalar=0.0, in1=z3, op0=ALU.min, op1=ALU.subtract))
        t2 = dve.put([t], lambda e: e.memset(z2, 1.0))
        t = dve.put([t, t2, relx], lambda e: e.tensor_tensor_scan(fr, z2, z1, 0.0, ALU.mult, ALU.add))
        thi = act.put([t, rel7], lambda e: e.activation(fhi[0:16, :], fr, ACT.Copy))
        t_lo = dve.put([thi], lambda e: e.tensor_tensor(z3, fr, fhi[0:16, :].bitcast(F), ALU.subtract))
        tz = pool.put([relx], lambda e: e.memset(AF, 0.0))
        tzb = pool.put([rel7], lambda e: e.memset(BF[:, :].bitcast(F), 0.0))
        ft = []
        for r in (64, 96):
            ft.append(pool.put([tz], lambda e, r=r: e.memset(AF[r:r + 16, :], 1.0)))
        for r in (0, 32):
            ft.append(pool.put([tzb], lambda e, r=r: e.memset(BF[r:r + 16, :].bitcast(F), 1.0)))
        ft.append(act.put([tz, thi], lambda e: e.activation(AF[0:16, :], fhi[0:16, :].bitcast(F), ACT.Copy)))
        ft.append(act.put([tz, t_lo], lambda e: e.activation(AF[32:48, :], z3, ACT.Copy)))
        ft.append(act.put([tzb, thi], lambda e: e.activation(BF[64:80, :], fhi[0:16, :].bitcast(F), ACT.Copy, scale=-1.0)))
        ft.append(act.put([tzb, t_lo], lambda e: e.activation(BF[96:112, :], z3, ACT.Copy, scale=-1.0)))
        rel8 = [rel7, t_spill, ft, t_lo]
        st.close()

        ab = attn_bufs(rel8, pt_t)
        kb_ready = [{}, {}]
        vb_ready = [{}, {}]
        run(kv_gemm(0, "w_k_2", 0, "w_v_2", 0, rhs_H, KV[0]))
        o_ready = [None] * KT
        for g in range(4):
            kv = KV[g % 2]

            def make(h, n, g=g):
                hd = 4 * g + n

                def start():
                    b = AFr.next()
                    t = pool.put([ft, b.rel], lambda e: e.tensor_scalar(
                        b.ap[:, :], AF, hmask[:, hd:hd + 1], 1.0, ALU.mult, ALU.mult))
                    h.extra = (b.ap[:, :], BF[:, :], [t, ft])
                    h.bias_ready = None
                    h.bias = lambda q: maskT[:, 128 * (3 - q):512]
                    h.af = b
                h.start = start

            hs = group_heads(kv, zeroed[g % 2], Q2, q_ready, kb_ready[g % 2], vb_ready[g % 2], 2 * g, make)
            for n, h in enumerate(hs):
                s0 = h.start

                def start(h=h, s0=s0, n=n, hs=hs):
                    if n >= 2:
                        hs[n - 2].af.rel = [hs[n - 2].s_done]
                    s0()
                h.start = start
            nxt = None
            if g < 3:
                nxt = kv_gemm(g + 1, "w_k_2", 256 * (g + 1), "w_v_2", 256 * (g + 1), rhs_H, KV[(g + 1) % 2])
            attend(hs, ab, nxt, 2)
            for h in hs[-2:]:
                h.af.rel = [h.s_done]
            kv.rel = [hs[-1].done]
            for p in range(2):
                o_ready[2 * g + p] = [hs[2 * p].out_ready, hs[2 * p + 1].out_ready]
        Hrel[0] = [pe.last()]
        rel9 = barrier()
        d_rx = dsem()
        t = dma(d_rx, rel9, x_t[:, :, :], scratch["x"][:, :].rearrange("(kt p) n -> p kt n", p=P))
        for k in range(KT):
            xt[k] = [t]
        for hf in range(2):
            gemm_A("attn_w_o_2", 0, 512 * hf, 2, rhs_of(Q2, o_ready), hf, lambda i, bank, tk, hf=hf: residual(
                4 * hf + i, bank, tk, mcol(V1 + 2, 4 * hf + i), t_m3))
        ph.close()
        ffn2(1, t_m3)
        ph = ExitStack()
        nb = norm_bufs(ph, barrier())
        renorm(nb, True, lne, lambda k: vcol("ln2_g_2", 8 + k), lambda k: vcol("ln2_b_2", 8 + k), [], None)
        d_o = dsem()
        for hf in range(2):
            t_out = dma(d_o, [xt[k] for k in range(4 * hf, 4 * hf + 4)],
                        out_t[512 * hf:512 * hf + 512, :].rearrange("(kt p) n -> p kt n", p=P), x_t[:, 4 * hf:4 * hf + 4, :])
        ph.close()
        assert state["take"] == len(plan) and not ada and not ada_pending
        finals = [t_out] + stores

        block = ctx.enter_context(nc.Block())

        @block.sync
        def _(eng):
            sp.replay(eng)
            last = {}
            for sem, value in finals:
                last[id(sem)] = (sem, max(value, last.get(id(sem), (sem, 0))[1]))
            for sem, value in last.values():
                eng.wait_ge(sem, value)

        @block.tensor
        def _(eng):
            pe.replay(eng)

        @block.scalar
        def _(eng):
            act.replay(eng)

        @block.vector
        def _(eng):
            dve.replay(eng)

        @block.gpsimd
        def _(eng):
            pool.replay(eng)


def kernel(**inputs):
    import concourse.bacc as bacc
    from concourse.bass_utils import run_bass_kernel_spmd as launch

    g = {k: np.asarray(v) for k, v in inputs.items()}

    def cols(v):
        return np.asarray(v).reshape(-1, P).T

    arrays = {}
    arrays["x_t"] = np.ascontiguousarray(g["x"][0].T)
    arrays["c_b"] = np.ascontiguousarray(np.broadcast_to(g["c"], (P, D)))
    arrays["c_b2"] = np.ascontiguousarray(np.broadcast_to(g["c_2"], (P, D)))
    arrays["ada_t"] = np.ascontiguousarray(g["ada_w"][0].T)
    arrays["ada2_0"] = np.ascontiguousarray(g["w_ada_2"][0].T)
    arrays["ada2_1"] = np.ascontiguousarray(g["w_ada_2"][1].T)
    arrays["adakv_t"] = np.ascontiguousarray(g["w_ada_kv_2"].T)
    arrays["vecs"] = np.ascontiguousarray(np.concatenate([cols(g[n].reshape(-1)) for n, _ in VECS], axis=1))
    arrays["consts"], arrays["hot"] = constants()
    arrays["sinks"] = np.ascontiguousarray(np.broadcast_to(g["attn_sinks"], (P, 8)))
    arrays["b_f"] = np.ascontiguousarray(g["b_f_2"].reshape(16, 1))
    arrays["rel_bias"] = np.ascontiguousarray(g["rel_bias"])
    order = np.concatenate([np.arange(64) + 64 * (t + 4 * two) for t in range(4) for two in range(2)])
    w_in = g["w_in"][0]
    arrays["w_in"] = np.ascontiguousarray(np.concatenate([w_in[:, order], w_in[:, 512:]], axis=1))
    arrays["w_branch_a"] = np.ascontiguousarray(g["w_branch_a"][0][order])
    for n in ("w_branch_b", "w_out", "w_mlp_in", "w_mlp_out", "conv_w_in_2", "conv_w_out_2", "attn_w_q_2", "attn_w_o_2"):
        arrays[n] = np.ascontiguousarray(g[n][0])
    for n in ("w_k_2", "w_v_2", "w_f_2"):
        arrays[n] = np.ascontiguousarray(g[n])
    for l in range(2):
        arrays[f"gate{l}"] = np.ascontiguousarray(g["ffn_w_gate_2"][l])
        arrays[f"up{l}"] = np.ascontiguousarray(g["ffn_w_up_2"][l])
        arrays[f"down{l}"] = np.ascontiguousarray(g["ffn_w_down_2"][l])

    nc = bacc.Bacc("TRN2", target_bir_lowering=False, num_devices=1)
    aps, feeds = {}, {}
    for n, v in arrays.items():
        feeds[f"in_{n}"] = v
        aps[n] = nc.dram_tensor(f"in_{n}", v.shape, mybir.dt.from_np(v.dtype), kind="ExternalInput").ap()
    out_t = nc.dram_tensor("out_t", (D, T), F, kind="ExternalOutput").ap()
    scratch = {"rows": nc.dram_tensor("rows", (16, 1024), F, kind="Internal").ap(),
               "toep": nc.dram_tensor("toep", (16, P, T), F, kind="Internal").ap(),
               "x": nc.dram_tensor("x_keep", (D, T), F, kind="Internal").ap()}
    build(nc, aps, out_t, scratch)
    r = launch(nc, [feeds], core_ids=[0])
    return np.ascontiguousarray(np.asarray(r.results[0]["out_t"]).T)[None]
```

```python
import math
from contextlib import ExitStack

import numpy as np

import concourse.bass as bass
from concourse import mybir

F = mybir.dt.float32
R = mybir.dt.float32r
ALU = mybir.AluOpType
ACT = mybir.ActivationFunctionType

P = 128
T = 512
D = 1024
KT = D // P
NEG = -1.0e30
LOW = -3.0e38
RMS_EPS = 1e-6
LN_EPS = 1e-5
ALPHA = math.sqrt(2.0)
QSCALE = 0.125
NW = 2
NRAW = 2
FF1 = 4096
FF2 = 2816

VECS = [("ada_b", 48), ("norm1_g", 8), ("norm2_g", 8), ("final_g", 8), ("b_ada_2", 96), ("b_ada_kv_2", 16),
        ("ln1_g_2", 16), ("ln1_b_2", 16), ("ln2_g_2", 16), ("ln2_b_2", 16), ("conv_w_2", 24)]
VCOL = {}
_n = 0
for _name, _w in VECS:
    VCOL[_name] = _n
    _n += _w
NV = _n
C_ID, C_J, C_ONE, C_MASK, C_HEAD = 0, 128, 256, 384, 896
NC = 912


def buckets(dist):
    n = np.maximum(dist, 0)
    nf = np.maximum(n, 1).astype(np.float32)
    large = 16 + (np.log(nf / np.float32(16)) / np.float32(math.log(128.0)) * np.float32(16)).astype(np.int32)
    return np.where(n < 16, n, np.minimum(large, 31))


def constants():
    c = np.zeros((P, NC), np.float32)
    i = np.arange(P)
    c[i, C_ID + i] = 1.0
    c[i, C_J + P - 1 - i] = 1.0
    c[:, C_ONE:C_ONE + P] = 1.0 / D
    j = np.arange(T)
    c[:, C_MASK:C_MASK + T] = np.where(384 + i[:, None] - j[None, :] >= 0, 0.0, NEG)
    c[:, C_HEAD:C_HEAD + 16] = (i[:, None] % 32 == np.arange(16)[None, :])
    hot = np.zeros((33, 1024), np.float32)
    for col, dist, ok in [(m, 511 - m, 511 - m >= 0) for m in range(640)] + \
                         [(640 + m, 255 - m, 0 <= 255 - m < 128) for m in range(384)]:
        hot[int(buckets(np.array(dist))) if ok else 32, col] = 1.0
    return c, hot


class Bind:

    def matmul(self, *a, **k):
        return lambda e: e.matmul(*a, **k)

    def transpose(self, *a, **k):
        return lambda e: e.transpose(*a, **k)

    def activation(self, *a, **k):
        return lambda e: e.activation(*a, **k)

    def tensor_tensor(self, *a, **k):
        return lambda e: e.tensor_tensor(*a, **k)

    def tensor_scalar(self, *a, **k):
        return lambda e: e.tensor_scalar(*a, **k)

    def tensor_copy(self, *a, **k):
        return lambda e: e.tensor_copy(*a, **k)

    def scalar_tensor_tensor(self, *a, **k):
        return lambda e: e.scalar_tensor_tensor(*a, **k)

    def tensor_tensor_reduce(self, *a, **k):
        return lambda e: e.tensor_tensor_reduce(*a, **k)

    def tensor_tensor_scan(self, *a, **k):
        return lambda e: e.tensor_tensor_scan(*a, **k)

    def reciprocal(self, *a, **k):
        return lambda e: e.reciprocal(*a, **k)

    def memset(self, *a, **k):
        return lambda e: e.memset(*a, **k)

    def dma(self, sem, *a, **k):
        return lambda e: e.dma_start(*a, **k).then_inc(sem, 16)


BIND = Bind()


class Engine:

    def __init__(self, sem, serial=False):
        self.sem, self.count, self.ops, self.seen, self.serial = sem, 0, [], {}, serial

    def put(self, waits, fn, inc=True):
        need = {}
        stack = [waits, self.last() if self.serial and self.count else None]
        while stack:
            w = stack.pop()
            if isinstance(w, list):
                stack.extend(w)
            elif w is not None:
                sem, value = w
                if value > self.seen.get(id(sem), 0):
                    self.seen[id(sem)] = value
                    need[id(sem)] = sem
        self.ops.append(([(s, self.seen[k]) for k, s in need.items()], fn(BIND), inc))
        if inc:
            self.count += 1
        return (self.sem, self.count)

    def last(self):
        return (self.sem, self.count)

    def replay(self, eng):
        for waits, fn, inc in self.ops:
            for sem, value in waits:
                eng.wait_ge(sem, value)
            ins = fn(eng)
            if inc:
                ins.then_inc(self.sem, 1)


class Buf:

    def __init__(self, ap, rel=None):
        self.ap, self.rel = ap, list(rel or [])


class Ring:
    def __init__(self, bufs):
        self.bufs, self.n = bufs, 0

    def next(self):
        self.n += 1
        return self.bufs[(self.n - 1) % len(self.bufs)]


class DmaSem:
    def __init__(self, sem):
        self.sem, self.count = sem, 0


def build(nc, a, out_t, scratch):
    ctx = ExitStack()
    with ctx:
        names = [0]

        def sb(stack, shape, dt):
            names[0] += 1
            return stack.enter_context(nc.sbuf_tensor(f"t{names[0]}", [P] + shape, dt))

        def semaphore(name):
            return ctx.enter_context(nc.semaphore(name))

        pe, act, dve, pool, sp = (Engine(semaphore(f"s_{n}"), n == "pool") for n in ("pe", "act", "dve", "pool", "sp"))
        ndma = [0]

        def dsem():
            ndma[0] += 1
            return DmaSem(semaphore(f"d{ndma[0]}"))

        stores = []

        def dma(ds, waits, dst, src):
            ds.count += 16
            s = ds.sem
            sp.put(waits, lambda e: e.dma(s, dst, src), inc=False)
            return (s, ds.count)

        def pool_dma(ds, waits, dst, src):
            ds.count += 16
            s = ds.sem
            pool.put(waits, lambda e: e.dma(s, dst, src), inc=False)
            return (s, ds.count)

        def barrier():
            return [e.last() for e in (pe, act, dve, pool)] + list(stores)

        psum = [Buf(ctx.enter_context(nc.psum_tensor(f"ps{i}", [P, T], F))) for i in range(8)]

        x_t = sb(ctx, [KT, T], F)
        raw = sb(ctx, [NRAW, 2048], F)
        WH = sb(ctx, [NW, 2048], R)
        WL = sb(ctx, [NW, 2048], R)
        H_t = sb(ctx, [2, KT, T], R)
        csb = sb(ctx, [D], F)
        vec = sb(ctx, [NV], F)
        mods = sb(ctx, [160], F)
        cst = sb(ctx, [NC], F)
        cols = sb(ctx, [64], F)
        stat = sb(ctx, [2, 5, 4], F)
        small = sb(ctx, [32], F)

        ident = cst[:, C_ID:C_ID + P]
        Jm = cst[:, C_J:C_J + P]
        ones = cst[:, C_ONE:C_ONE + P]
        maskT = cst[:, C_MASK:C_MASK + T]
        hmask = cst[:, C_HEAD:C_HEAD + 16]
        zcol, rmse, lne = cols[:, 0:1], cols[:, 1:2], cols[:, 2:3]
        X = [Buf(x_t[:, k, :]) for k in range(KT)]
        xt = [[] for _ in range(KT)]

        d_c, d_v, d_x, d_cs, d_s = (dsem() for _ in range(5))
        t_cb = dma(d_cs, [], csb[:, :], a["c_b"])
        t_cst = pool_dma(d_c, [], cst[:, :], a["consts"])
        t_vec = pool_dma(d_v, [], vec[:, :], a["vecs"])
        t_sink = pool_dma(d_s, [], small[:, 0:8], a["sinks"])
        t_sink = pool_dma(d_s, [], small[0:16, 8:9], a["b_f"])
        xload = [None, None]
        dx = [dsem(), dsem()]

        def load_x(waits):
            for hf in range(2):
                k0 = 4 * hf
                xload[hf] = dma(dx[hf], waits, x_t[:, k0:k0 + 4, :],
                                a["x_t"][k0 * P:(k0 + 4) * P, :].rearrange("(kt p) n -> p kt n", p=P))
                for k in range(k0, k0 + 4):
                    xt[k] = [xload[hf]]

        t_col = [dve.put([], lambda e, v=v, i=i: e.memset(cols[:, i:i + 1], v))
                 for i, v in enumerate((0.0, RMS_EPS, LN_EPS))]

        plan = []

        def plan_A(w, r0, c0, n):
            plan.extend(("A", w, r0 + 512 * s, c0) for s in range(n))

        def plan_B(w, c0):
            plan.append(("B", w, 0, c0))

        for c0 in (0, 256, 512, 768, 1024):
            plan_B("w_in", c0)
        plan_B("w_in", 1280)
        plan_B("w_in", 1792)
        plan_B("w_in", 1536)
        plan_B("w_in", 2048)
        plan_B("w_in", 2304)
        plan_B("w_in", 2560)
        for hf in range(2):
            if hf:
                plan_A("w_in", 0, 2304 + 512 * hf, 2)
            plan_A("w_branch_a", 0, 512 * hf, 1)
            plan_A("w_in", 0, 3328 + 512 * hf, 2)
            plan_A("w_branch_b", 0, 512 * hf, 1)
        for hf in range(2):
            plan_A("w_out", 0, 512 * hf, 2)
        for f in range(FF1 // 512):
            plan_A("w_mlp_in", 0, 512 * f, 2)
            for hf in range(2):
                plan_A("w_mlp_out", 512 * f, 512 * hf, 1)

        def plan_ffn2(l):
            for f in range(5):
                if f == 4:
                    plan_B(f"gate{l}", 2560)
                    plan_B(f"up{l}", 2560)
                    plan.append(("C", f"down{l}", 2560, 0))
                plan_A(f"gate{l}", 0, 512 * f, 2)
                plan_A(f"up{l}", 0, 512 * f, 2)
                for hf in range(2):
                    plan_A(f"down{l}", 512 * f, 512 * hf, 1)

        for hf in range(2):
            for c0 in (1024, 2048, 0):
                plan_A("conv_w_in_2", 0, c0 + 512 * hf, 2)
        for hf in range(2):
            plan_A("conv_w_out_2", 0, 512 * hf, 2)
        plan_ffn2(0)
        for hf in range(2):
            plan_A("attn_w_q_2", 0, 512 * hf, 2)
        for g in range(4):
            plan_B("w_k_2", 256 * g)
            plan_B("w_v_2", 256 * g)
        for hf in range(2):
            plan_A("attn_w_o_2", 0, 512 * hf, 2)
        plan_ffn2(1)

        class Raw:

            def __init__(self, ap, rel):
                self.ap, self.rel, self.sem, self.busy = ap, list(rel), dsem(), False

            def take(self):
                assert not self.busy
                self.busy = True
                return self

            def done(self, tickets):
                self.rel, self.busy = tickets, False

        raws = [Raw(raw[:, i, :], []) for i in range(NRAW)]
        ada_sems = [DmaSem(semaphore(f"ada{i}")) for i in range(6)]
        ada_raws = []
        w_rel = [[] for _ in range(NW)]
        w_dma, w_conv = {}, {}
        state = {"dma": 0, "conv": 0, "take": 0}
        SHAPE = {"A": (4, 512), "B": (8, 256), "C": (2, 1024)}

        def slot_dma():
            n = state["dma"]
            if n >= len(plan):
                return
            kind, w, r0, c0 = plan[n]
            kt, nn = SHAPE[kind]
            r = raws[n % NRAW].take()
            src = a[w][r0:r0 + kt * P, c0:c0 + nn].rearrange("(kt p) n -> p kt n", p=P)
            dst = r.ap.rearrange("p (kt n) -> p kt n", kt=kt)
            w_dma[n] = (r, dma(r.sem, r.rel, dst, src))
            state["dma"] += 1

        def slot_conv():
            n = state["conv"]
            if n >= len(plan):
                return
            r, landed = w_dma.pop(n)
            b = n % NW
            hi = act.put([landed, w_rel[b]], lambda e: e.activation(WH[:, b, :], r.ap, ACT.Copy))
            lo = dve.put([landed, hi, w_rel[b]], lambda e: e.tensor_tensor(
                WL[:, b, :], r.ap, WH[:, b, :].bitcast(F), ALU.subtract))
            r.done([hi, lo])
            w_conv[n] = [hi, lo]
            state["conv"] += 1

        def ready_for(n):
            while state["conv"] <= n:
                while state["dma"] <= state["conv"]:
                    slot_dma()
                slot_conv()

        def ahead(n):
            if n < len(plan):
                ready_for(n)
            while state["dma"] < min(len(plan), state["conv"] + NRAW):
                slot_dma()

        class Slot:
            pass

        def take(kind, w, r0, c0):
            n = state["take"]
            assert plan[n] == (kind, w, r0, c0), (plan[n], kind, w, r0, c0)
            ready_for(n)
            ada_step(1)
            ahead(n + 1)
            ada_load()
            state["take"] += 1
            s = Slot()
            kt, nn = SHAPE[kind]
            b = n % NW
            s.hi = WH[:, b, :].rearrange("p (kt n) -> p kt n", kt=kt)
            s.lo = WL[:, b, :].rearrange("p (kt n) -> p kt n", kt=kt)
            s.ready = w_conv.pop(n)
            s.b = b
            return s

        def release(s, ticket):
            w_rel[s.b] = [ticket]

        ada = []
        ada_pending = []
        cs_ready = [None]
        cs_last = [None]
        mod_raw = {}

        def ada_jobs(name, row0, nrows, col0, which):
            for r in range(0, nrows, 256):
                ada.append((name, row0 + r, col0 + r // P, which))

        def silu_c(landed):
            r = ada_raws[0].take()
            t = act.put([landed, r.rel], lambda e: e.activation(r.ap[:, 0:D], csb[:, :], ACT.Sigmoid))
            t = dve.put([t], lambda e: e.tensor_tensor(csb[:, :], csb[:, :], r.ap[:, 0:D], ALU.mult))
            r.done([t])
            cs_ready[0] = t

        cs_now = [0]

        def ada_memory(stack, n, rel):
            assert not ada_pending
            ada_raws[:] = [Raw(sb(stack, [2048], F)[:, :], rel) for _ in range(n)]
            for r, sem in zip(ada_raws, ada_sems):
                r.sem = sem

        def ada_end():
            ada_step()
            ada_raws[:] = []

        def ada_load():
            while ada:
                free = [r for r in ada_raws if not r.busy]
                if not free:
                    return
                if ada[0][3] != cs_now[0]:
                    if ada_pending:
                        return
                    silu_c(dma(d_cs, [cs_last[0]], csb[:, :], a["c_b2"]))
                    cs_now[0] = ada[0][3]
                name, row, col, _ = ada.pop(0)
                r = free[0].take()
                src = a[name][row:row + 256, :].rearrange("(a p) k -> p a k", p=P)
                ada_pending.append((r, dma(r.sem, r.rel, r.ap.rearrange("p (a k) -> p a k", a=2), src), col))

        def ada_step(most=100):
            while ada_pending and most:
                most -= 1
                r, landed, col = ada_pending.pop(0)
                t = None
                for i in range(2):
                    v = r.ap[:, i * D:(i + 1) * D]
                    t = dve.put([landed, cs_ready[0]], lambda e: e.tensor_tensor_reduce(
                        out=v, in0=v, in1=csb[:, :], scale=1.0, scalar=0.0, op0=ALU.mult, op1=ALU.add,
                        accum_out=mods[:, col + i:col + i + 1]))
                r.done([t])
                cs_last[0] = t
                mod_raw[col] = t

        def ada_until(col_end, col0):
            need = range(col0, col_end, 2)
            while not all(c in mod_raw for c in need):
                ada_load()
                ada_step(1)
            return [mod_raw[c] for c in need]

        def mod_bias(col0, n, vcol):
            w = ada_until(col0 + n, col0)
            return dve.put([w, t_vec], lambda e: e.tensor_tensor(
                mods[:, col0:col0 + n], mods[:, col0:col0 + n], vec[:, vcol:vcol + n], ALU.add))

        def mcol(v, k):
            return mods[:, v * 8 + k:v * 8 + k + 1]

        def vcol(name, k):
            return vec[:, VCOL[name] + k:VCOL[name] + k + 1]

        def mm3(bank, w_hi, w_lo, h_hi, h_lo, first, last, waits, inc):
            pe.put(waits, lambda e: e.matmul(bank, w_hi, h_hi, start=first, stop=False), inc=False)
            pe.put([], lambda e: e.matmul(bank, w_hi, h_lo, start=False, stop=False), inc=False)
            return pe.put([], lambda e: e.matmul(bank, w_lo, h_hi, start=False, stop=last), inc=inc)

        def gemm_A(w, r0, c0, nslots, rhs, bset, evac, last="i"):
            banks = [psum[4 * bset + i] for i in range(4)]
            done = [None] * 4

            def tile(sl, i, kt, first, final, waits):
                hi, lo, tk = rhs(kt)
                c = slice(i * P, (i + 1) * P)
                return mm3(banks[i].ap[:, :], sl.hi[:, kt % 4, c], sl.lo[:, kt % 4, c], hi, lo, first, final,
                           [sl.ready, tk, waits], final or (kt % 4 == 3 and i == 3))

            for s in range(nslots):
                sl = take("A", w, r0 + 512 * s, c0)
                final = s == nslots - 1
                ks = range(4 * s, 4 * s + 4)
                if final and last == "i":
                    for i in range(4):
                        for kt in ks:
                            done[i] = tile(sl, i, kt, kt == 0, kt == ks[3], banks[i].rel if kt == 0 else None)
                        if i == 3:
                            release(sl, done[3])
                        evac(i, banks[i], done[i])
                else:
                    for kt in ks:
                        for i in range(4):
                            done[i] = tile(sl, i, kt, kt == 0, final and kt == ks[3], banks[i].rel if kt == 0 else None)
                    release(sl, done[3])
                    if final:
                        for i in range(4):
                            evac(i, banks[i], done[i])

        def gemm_B(w, c0, rhs, ring, evac):
            sl = take("B", w, 0, c0)
            for i in range(2):
                bank = ring.next()
                for kt in range(8):
                    hi, lo, tk = rhs(kt)
                    c = slice(i * P, (i + 1) * P)
                    t = mm3(bank.ap[:, :], sl.hi[:, kt, c], sl.lo[:, kt, c], hi, lo, kt == 0, kt == 7,
                            [sl.ready, tk, bank.rel if kt == 0 else None], kt == 7)
                    yield
                if i == 1:
                    release(sl, t)
                evac(i, bank, t)

        def gemm_V(w, c0, lhs, ring, evac):
            sl = take("B", w, 0, c0)
            for pair in range(2):
                bank = ring.next()
                for hf in range(2):
                    tok = slice((2 * pair + hf) * P, (2 * pair + hf + 1) * P)
                    o = bank.ap[:, 256 * hf:256 * hf + 256]
                    for kt in range(8):
                        hi, lo, tk = lhs(kt)
                        t = mm3(o, hi[:, tok], lo[:, tok], sl.hi[:, kt, :], sl.lo[:, kt, :], kt == 0, kt == 7,
                                [sl.ready, tk, bank.rel if kt == 0 and hf == 0 else None], kt == 7)
                        if kt % 2:
                            yield
                if pair == 1:
                    release(sl, t)
                evac(pair, bank, t)

        def run(gen):
            for _ in gen or ():
                pass

        def chain(*gens):
            for g in gens:
                yield from g

        def split(src, hi_ap, lo_ap, waits, hi_waits):
            hi = act.put([waits, hi_waits], lambda e: e.activation(hi_ap, src, ACT.Copy))
            lo = dve.put([waits, hi, hi_waits], lambda e: e.tensor_tensor(lo_ap, src, hi_ap.bitcast(F), ALU.subtract))
            return [hi, lo]

        class Norm:

            def __init__(self, stack, rel, layer):
                m = [Buf(sb(stack, [T], F)[:, :], rel) for _ in range(6)] if stack is not None else rel
                self.acc, self.rs, self.sq = m[0], m[1], Ring(m[2:4])
                self.tm = Ring(m[4:6])
                self.layer = layer
                if layer:
                    self.s, self.dsum = m[4], m[5]
                self.t = self.td = None
                self.wait = []
                self.n = 0

            def add(self, k):
                if not self.layer:
                    self.square(k)
                    return
                if k < 4:
                    self.wait.append(k)
                    return
                if k == 4:
                    t = pe.put([xt[0], psum[3].rel, t_cst], lambda e: e.matmul(
                        psum[3].ap[:, :], ones, X[0].ap, start=True, stop=True))
                    t = act.put([t, self.s.rel], lambda e: e.activation(self.s.ap, psum[3].ap[:, :], ACT.Copy, scale=8.0))
                    psum[3].rel = [t]
                    self.ts = t
                for j in self.wait + [k]:
                    xt[j] = [dve.put([self.ts, xt[j]], lambda e: e.tensor_tensor(
                        X[j].ap, X[j].ap, self.s.ap, ALU.subtract))]
                    if self.td is None:
                        self.td = pool.put([xt[j], self.dsum.rel], lambda e: e.tensor_copy(self.dsum.ap, X[j].ap))
                    else:
                        self.td = pool.put([xt[j], self.td], lambda e: e.tensor_tensor(
                            self.dsum.ap, self.dsum.ap, X[j].ap, ALU.add))
                    self.square(j)
                self.wait = []

            def square(self, k):
                if self.t is None:
                    self.t = act.put([xt[k], self.acc.rel], lambda e: e.activation(self.acc.ap, X[k].ap, ACT.Square))
                else:
                    b = self.sq.next()
                    t = act.put([xt[k], b.rel], lambda e: e.activation(b.ap, X[k].ap, ACT.Square))
                    self.t = dve.put([t, self.t], lambda e: e.tensor_tensor(self.acc.ap, self.acc.ap, b.ap, ALU.add))
                    b.rel = [self.t]

            def finish(self, eps):
                rs, q, d = self.rs, psum[3], psum[7]
                t = pe.put([self.t, q.rel, t_cst], lambda e: e.matmul(q.ap[:, :], ones, self.acc.ap, start=True, stop=True))
                self.acc.rel = [t]
                if not self.layer:
                    t = act.put([t, rs.rel, t_col], lambda e: e.activation(rs.ap, q.ap[:, :], ACT.Sqrt, bias=eps))
                    q.rel = [t]
                    return dve.put([t], lambda e: e.reciprocal(rs.ap, rs.ap))
                td = pe.put([self.td, d.rel, t_cst], lambda e: e.matmul(
                    d.ap[:, :], ones, self.dsum.ap, start=True, stop=True))
                ahead(state["take"] + 1)
                t2 = act.put([td, rs.rel], lambda e: e.activation(rs.ap, d.ap[:, :], ACT.Square))
                t = dve.put([t, t2], lambda e: e.scalar_tensor_tensor(
                    out=rs.ap, in0=rs.ap, scalar=-1.0, in1=q.ap[:, :], op0=ALU.mult, op1=ALU.add))
                q.rel = [t]
                t = act.put([t, t_col], lambda e: e.activation(rs.ap, rs.ap, ACT.Sqrt, bias=eps))
                return dve.put([t], lambda e: e.reciprocal(rs.ap, rs.ap))

        def halves(t):
            return (t[:, 0, :, :], t[:, 1, :, :])

        HH = halves(H_t)
        Ht = [[] for _ in range(KT)]
        Hrel = [[]]

        def rhs_H(k):
            return HH[0][:, k, :], HH[1][:, k, :], Ht[k]

        cA, cB, cC, cD, cE, cF = (cols[:, 8 + 8 * i:16 + 8 * i] for i in range(6))

        def modulated(nm, k, src, waits, A, B, cw, dst, rel):
            b = nm.sq.next()
            t = act.put([waits, cw, b.rel], lambda e: e.activation(
                b.ap, src, ACT.Identity, bias=B[:, k:k + 1], scale=A[:, k:k + 1]))
            tk = split(b.ap, dst[0][:, k, :], dst[1][:, k, :], [t], rel)
            b.rel = tk
            return t, tk

        def mod8(v):
            return mods[:, 8 * v:8 * v + 8]

        def vec8(name, l=0):
            return vec[:, VCOL[name] + 8 * l:VCOL[name] + 8 * l + 8]

        def fold(A, B, w, v_shift, v_scale, g, b):
            t = dve.put([w, t_vec], lambda e: e.scalar_tensor_tensor(
                out=A, in0=mod8(v_scale), scalar=1.0, in1=g, op0=ALU.add, op1=ALU.mult))
            if b is None:
                return [t, dve.put([w], lambda e: e.tensor_copy(B, mod8(v_shift)))]
            t2 = dve.put([w, t_vec], lambda e: e.scalar_tensor_tensor(
                out=B, in0=mod8(v_scale), scalar=1.0, in1=b, op0=ALU.add, op1=ALU.mult))
            return [t, dve.put([t2], lambda e: e.tensor_tensor(B, B, mod8(v_shift), ALU.add))]

        def rms_h(nm, w, A, B):
            t_rs = nm.finish(rmse)
            for k in range(KT):
                b = nm.tm.next()
                t = dve.put([t_rs, xt[k], b.rel], lambda e: e.tensor_tensor(b.ap, X[k].ap, nm.rs.ap, ALU.mult))
                nm.rs.rel = [t]
                tr, Ht[k] = modulated(nm, k, b.ap, [t], A, B, w, HH, Hrel[0])
                b.rel = [tr]

        def renorm(nm, eps, hs, xA, xB, xw, x_eng=None):
            t_rs = nm.finish(eps)
            reads = [[] for _ in range(KT)]
            for n, (A, B, w, dst, tick, rel) in enumerate(hs or [(None,) * 6]):
                for k in range(KT):
                    if n == 0:
                        if nm.layer:
                            xt[k] = [dve.put([t_rs, xt[k]], lambda e: e.tensor_tensor(
                                X[k].ap, X[k].ap, psum[7].ap[:, :], ALU.subtract))]
                            psum[7].rel = xt[k]
                        xt[k] = [dve.put([t_rs, xt[k]], lambda e: e.tensor_tensor(
                            X[k].ap, X[k].ap, nm.rs.ap, ALU.mult))]
                    if A is not None:
                        tr, tick[k] = modulated(nm, k, X[k].ap, xt[k], A, B, w, dst, rel)
                        reads[k].append(tr)
                    if n == max(1, len(hs)) - 1:
                        if x_eng is None:
                            xt[k] = [pool.put([xt[k], reads[k], xw], lambda e: e.tensor_scalar(
                                X[k].ap, X[k].ap, xA[:, k:k + 1], xB[:, k:k + 1], ALU.mult, ALU.add))]
                        else:
                            xt[k] = [act.put([xt[k], reads[k], xw], lambda e: e.activation(
                                X[k].ap, X[k].ap, ACT.Identity, bias=xB[:, k:k + 1], scale=xA[:, k:k + 1]))]

        def scaled(dst, src, f):
            return dve.put([t_vec], lambda e: e.tensor_scalar(dst, src, f, None, ALU.mult))

        def residual(k, bank, tk, gate, w, nm=None):
            xt[k] = [dve.put([tk, xt[k], w], lambda e: e.scalar_tensor_tensor(
                out=X[k].ap, in0=bank.ap[:, :], scalar=gate, in1=X[k].ap, op0=ALU.mult, op1=ALU.add))]
            bank.rel = xt[k]
            if nm is not None:
                nm.add(k)

        S_ring = Ring([psum[0], psum[1]])
        T_ring = Ring([psum[2], psum[3]])
        O_ring = Ring([psum[4]])
        G_ring = Ring([psum[5], psum[6], psum[7]])
        OFF = {"causal": [0, 128, 384, 768], "swa": [0, 128, 384, 640]}

        class Head:
            pass

        def scores(h, ab):
            off = OFF[h.kind]
            st = ab.stats.next()
            sp_ = ab.sp.next()
            h.st, h.sp = st, sp_
            mx, nm, sm, es = (st.ap[:, q, :] for q in (0, 1, 2, 3))
            h.exp = [None] * 4
            nms = []
            for i in range(4):
                k0 = 0 if h.kind == "causal" else max(0, i - 1) * P
                n = (i + 1) * P - k0
                N = max(256, n)
                bank = S_ring.next()
                o = bank.ap[:, 0:N]
                tok = slice(i * P, (i + 1) * P)
                w = [h.q_ready, h.k_ready, bank.rel]
                kr = slice(k0, k0 + N)
                pairs = [(h.q[0][:, tok], h.k[0][:, kr]), (h.q[1][:, tok], h.k[0][:, kr]),
                         (h.q[0][:, tok], h.k[1][:, kr])]
                if h.extra:
                    pairs.append((h.extra[0][:, tok], h.extra[1][:, kr]))
                    w.append(h.extra[2])
                for m, (lt, rr) in enumerate(pairs):
                    tk = pe.put(w if m == 0 else [], lambda e, lt=lt, rr=rr, m=m: e.matmul(
                        o, lt, rr, start=m == 0, stop=m == len(pairs) - 1), inc=m == len(pairs) - 1)
                h.s_done = tk
                piece = sp_.ap[:, off[i]:off[i] + n]
                bias = h.bias(i)
                t = dve.put([tk, h.bias_ready, sp_.rel, st.rel], lambda e: e.tensor_tensor_reduce(
                    out=piece, in0=bank.ap[:, 0:n], in1=bias, scale=1.0, scalar=LOW, op0=ALU.add, op1=ALU.max,
                    accum_out=mx[:, i:i + 1]))
                bank.rel = [t]
                h.bias_done = t
                top = h.sink if h.sink is not None else LOW
                t = dve.put([t, t_sink], lambda e: e.tensor_scalar(
                    nm[:, i:i + 1], mx[:, i:i + 1], top, -1.0, ALU.max, ALU.mult))
                nms.append(t)
                h.exp[i] = act.put([t], lambda e: e.activation(
                    piece, piece, ACT.Exp, bias=nm[:, i:i + 1], accum_out=sm[:, i:i + 1]))
                if i == 3 and h.sink is not None:
                    h.es = act.put([nms, st.rel], lambda e: e.activation(es, nm, ACT.Exp, bias=h.sink))
                yield

        def weighted(h, ab):
            off = OFF[h.kind]
            st, sp_ = h.st, h.sp
            sm, es, rs = (st.ap[:, q, :] for q in (2, 3, 4))
            t = None
            if h.sink is not None:
                t = dve.put([h.exp, h.es], lambda e: e.tensor_tensor(sm, sm, es, ALU.add))
            t = dve.put([h.exp, t, st.rel], lambda e: e.reciprocal(rs, sm))
            norm = [None] * 4
            for i in (3, 2, 1, 0):
                n = ((i + 1) if h.kind == "causal" else min(2, i + 1)) * P
                piece = sp_.ap[:, off[i]:off[i] + n]
                norm[i] = (dve if i % 2 else pool).put([t, h.exp[i]], lambda e, i=i, piece=piece: e.tensor_scalar(
                    piece, piece, rs[:, i:i + 1], 1.0, ALU.mult, ALU.mult))
            st.rel = norm
            if h.kind == "causal":
                groups = [[0], [1], [2], [3]]
                blocks = {j: list(range(j, 4)) for j in range(4)}
                base = [0, 512, 896, 1152]
                order = [0, 1, 2, 3]
                need = {0: 0, 1: 1, 2: 2, 3: 3}
                sched = ["t0", "t1", "v0", "t2", "v1", "t3", "v2", "v3"]
            else:
                groups = [[0, 1], [2, 3]]
                blocks = {0: [0, 1], 1: [1, 2], 2: [2, 3], 3: [3]}
                base = [0, 256, 512, 768]
                need = {0: 0, 1: 0, 2: 1, 3: 1}
                sched = ["t0", "t1", "v0", "v2", "v1", "v3"]
            ready = {}
            bank = O_ring.next()
            for step in sched:
                if step[0] == "t":
                    g = groups[int(step[1])]
                    tb = T_ring.next()
                    pos = 0
                    tk = None
                    for j in g:
                        for i in blocks[j]:
                            col = off[i] + (j * P if h.kind == "causal" else (j - max(0, i - 1)) * P)
                            tk = pe.put([norm[i], tb.rel if pos == 0 else None], lambda e, pos=pos, col=col: e.transpose(
                                tb.ap[:, pos:pos + P], sp_.ap[:, col:col + P], ident), inc=True)
                            pos += P
                    b0 = base[g[0]]
                    hi_ap, lo_ap = ab.pt[0][:, b0:b0 + pos], ab.pt[1][:, b0:b0 + pos]
                    ready[int(step[1])] = split(tb.ap[:, 0:pos], hi_ap, lo_ap, [tk], ab.pt_rel[int(step[1])])
                    tb.rel = ready[int(step[1])]
                    h.t_done = tk
                    if g is groups[-1]:
                        sp_.rel = [tk]
                else:
                    j = int(step[1])
                    n = len(blocks[j]) * P
                    o = bank.ap[:, j * P:j * P + n]
                    ph, pl = ab.pt[0][:, base[j]:base[j] + n], ab.pt[1][:, base[j]:base[j] + n]
                    vh, vl = h.v[0](j), h.v[1](j)
                    firstw = [bank.rel if j == 0 else None, h.v_ready, ready[need[j]]]
                    pe.put(firstw, lambda e, o=o, vh=vh, ph=ph, j=j: e.matmul(
                        o, vh, ph, start=j == 0, stop=False, skip_group_check=True), inc=False)
                    pe.put([], lambda e, o=o, vh=vh, pl=pl: e.matmul(
                        o, vh, pl, start=False, stop=False, skip_group_check=True), inc=False)
                    tk = pe.put([], lambda e, o=o, vl=vl, ph=ph, j=j: e.matmul(
                        o, vl, ph, start=False, stop=j == 3, skip_group_check=True))
                    ab.pt_rel[need[j]] = [tk]
                yield
            r = slice(h.r0, h.r0 + 64)
            h.out_ready = split(bank.ap[r, :], h.o[0][r, :], h.o[1][r, :], [tk], [h.s_done])
            bank.rel = h.out_ready
            h.done = tk

        def attend(heads, ab, gemm=None, steps=0):
            gemm = gemm if gemm is not None else iter(())
            quota = -(-steps // len(heads))

            def fill(n):
                for _ in range(n):
                    next(gemm, None)

            def score_stream():
                for h in heads:
                    yield from scores(h, ab)

            stream = score_stream()
            started = [0]

            def start(n):
                while started[0] < min(n, len(heads)):
                    heads[started[0]].start()
                    started[0] += 1

            start(2)
            for _ in range(6):
                next(stream, None)
                fill(1)
            for n, h in enumerate(heads):
                marks = (0, 2, 5, 6) if h.kind == "causal" else (0, 1, 3, 4)
                nsteps = 8 if h.kind == "causal" else 6
                used = 0
                fill(max(0, quota - nsteps))
                for at, _ in enumerate(weighted(h, ab)):
                    if at == 0:
                        start(n + 3)
                    if at in marks:
                        next(stream, None)
                    if used < quota:
                        fill(1)
                        used += 1
            run(gemm)

        class AttnBufs:
            pass

        ada_jobs("ada_t", 0, 2048, 0, 0)
        ph = ExitStack()
        ada_memory(ph, 6, [])
        nm = Norm(ph, [], False)
        silu_c(t_cb)
        ada_load()
        load_x([])
        tb33 = sb(ph, [16], F)
        hot = sb(ph, [1024], F)
        rrow = sb(ph, [1024], F)
        tz = Ring([Buf(sb(ph, [T], F)[:, :]) for _ in range(5)])
        tf = Ring([Buf(sb(ph, [T], F)[:, :]) for _ in range(5)])
        d_t, d_r = dsem(), dsem()
        t_tab = pool_dma(d_t, [], tb33[0:32, :], a["rel_bias"])
        t_tab = pool_dma(d_t, [], hot[0:33, :], a["hot"])
        t_m = dve.put([], lambda e: e.memset(tb33[32:33, :], NEG))
        tr = []
        for c0, n in ((0, 512), (512, 128), (640, 384)):
            bank = psum[c0 // 512] if c0 != 640 else psum[2]
            t = pe.put([t_tab, t_m], lambda e, bank=bank, c0=c0, n=n: e.matmul(
                bank.ap[0:16, 0:n], tb33[0:33, :], hot[0:33, c0:c0 + n], start=True, stop=True))
            t = act.put([t], lambda e, bank=bank, c0=c0, n=n: e.activation(
                rrow[0:16, c0:c0 + n], bank.ap[0:16, 0:n], ACT.Copy))
            bank.rel = [t]
            tr.append(t)
        t_rows = pool_dma(d_r, tr, scratch["rows"][:, :], rrow[0:16, :])
        stores.append(t_rows)
        d_tz = [dsem() for _ in range(5)]
        d_tf = [dsem() for _ in range(5)]
        bias_in_dram, toep = {}, {}

        def toep_load(h):
            n = 256 if h < 8 else 512
            z = tz.next()
            base = scratch["rows"][0:1, 0:1]
            src = bass.AP(tensor=base.tensor, offset=h * 1024 + (640 if h < 8 else 0), ap=[[1, P], [1, n]])
            toep[h] = (z, n, pool_dma(d_tz[h % 5], [t_rows, z.rel], z.ap[:, 0:n], src))

        for h in range(5):
            toep_load(h)
        for h in range(16):
            z, n, t = toep[h]
            bank = psum[h % 3]
            t = pe.put([t, bank.rel, t_cst], lambda e: e.matmul(
                bank.ap[:, 0:n], Jm, z.ap[:, 0:n], start=True, stop=True))
            z.rel = [t]
            f = tf.next()
            t = act.put([t, f.rel], lambda e: e.activation(f.ap[:, 0:n], bank.ap[:, 0:n], ACT.Copy))
            bank.rel = [t]
            if h + 5 < 16:
                toep_load(h + 5)
            f.rel = [pool_dma(d_tf[h % 5], [t], scratch["toep"][h, :, 0:n], f.ap[:, 0:n])]
            bias_in_dram[h] = f.rel[0]
            stores.append(f.rel[0])
        ada_step(6)
        ada_load()
        slot_dma()
        slot_dma()
        for k in range(KT):
            nm.add(k)
        w1 = fold(cA, cB, mod_bias(0, 16, VCOL["ada_b"]), 0, 1, vec8("norm1_g"), None)
        rms_h(nm, [w1], cA, cB)
        ada_end()
        x_free = [Ht[k] for k in range(KT)] + [nm.rs.rel]
        rel1 = barrier()
        ph.close()

        outer = ExitStack()
        Qa = sb(outer, [2, 4, T], R)
        Qb = sb(outer, [2, 4, T], R)
        sg_r = Ring([Buf(sb(outer, [T], F)[:, :], rel1) for _ in range(4)])
        ph = ExitStack()
        KV = [Buf(sb(ph, [6144], R), rel1) for _ in range(2)]
        pt_t = sb(ph, [2, 1280], R)

        def k_view(b):
            return b.ap[:, 0:4096].rearrange("p (s h n) -> p s h n", s=2, h=4)

        def v_view(b):
            return b.ap[:, 4096:6144].rearrange("p (s t n) -> p s t n", s=2, t=4)

        def zero_halves(b, rel):
            tks = []
            kv = k_view(b)
            for s in range(2):
                for odd in range(2):
                    r = slice(0, 64) if odd else slice(64, 128)
                    v = kv[r, s, odd::2, :].bitcast(F)
                    tks.append(pool.put(rel, lambda e, v=v: e.memset(v, 0.0)))
            return tks

        def attn_bufs(rel, pt):
            ab = AttnBufs()
            xf = x_t[:, :, :].rearrange("p k n -> p (k n)")
            ab.sp = Ring([Buf(xf[:, 0:1280], rel), Buf(xf[:, 1280:2560], rel)])
            ab.bias = Ring([Buf(xf[:, 2560:3072], rel), Buf(xf[:, 3072:3584], rel)])
            ab.stats = Ring([Buf(stat[:, 0, :, :], rel), Buf(stat[:, 1, :, :], rel)])
            ab.pt = (pt[:, 0, :], pt[:, 1, :])
            ab.pt_rel = [list(rel) for _ in range(4)]
            return ab

        ab = attn_bufs(rel1, pt_t)
        d_b = [dsem(), dsem()]
        nbias = [0]
        zeroed = [zero_halves(KV[i], rel1) for i in range(2)]

        def evac_q(dst, ready, t0, rel):
            def f(i, bank, tk):
                hi_ap, lo_ap = dst[:, 0, t0 + i, :], dst[:, 1, t0 + i, :]
                hi = act.put([tk, rel], lambda e: e.activation(hi_ap, bank.ap[:, :], ACT.Copy, scale=QSCALE))
                lo = dve.put([hi], lambda e: e.scalar_tensor_tensor(
                    out=lo_ap, in0=bank.ap[:, :], scalar=QSCALE, in1=hi_ap.bitcast(F), op0=ALU.mult, op1=ALU.subtract))
                bank.rel = [hi, lo]
                ready[t0 + i] = [hi, lo]
            return f

        def evac_k(b, ready):
            def f(i, bank, tk):
                kv = k_view(b)
                for odd in range(2):
                    r = slice(64 * odd, 64 * odd + 64)
                    n = 2 * i + odd
                    ready[n] = split(bank.ap[r, :], kv[r, 0, n, :], kv[r, 1, n, :], [tk], b.rel)
                bank.rel = [ready[2 * i], ready[2 * i + 1]]
            return f

        def evac_v(b, ready):
            def f(pair, bank, tk):
                vv = v_view(b)
                src = bank.ap[:, :].rearrange("p (t n) -> p t n", t=2)
                ready[pair] = split(src, vv[:, 0, 2 * pair:2 * pair + 2, :], vv[:, 1, 2 * pair:2 * pair + 2, :], [tk], b.rel)
                bank.rel = ready[pair]
            return f

        def group_heads(kv, zero, q, q_ready, k_ready, v_ready, t0, make):
            kk, vv = k_view(kv), v_view(kv)
            hs = []
            for n in range(4):
                h = Head()
                h.kind, h.sink, h.extra = "causal", None, None
                p = t0 + n // 2
                h.q = (q[:, 0, p, :], q[:, 1, p, :])
                h.q_ready = q_ready[p]
                h.k = (kk[:, 0, n, :], kk[:, 1, n, :])
                h.k_ready = [k_ready[n], zero]
                c = slice((n // 2) * P, (n // 2 + 1) * P)
                h.v = (lambda j, c=c: vv[:, 0, j, c], lambda j, c=c: vv[:, 1, j, c])
                h.v_ready = [v_ready[0], v_ready[1]]
                h.r0 = 64 * (n % 2)
                h.o = h.q
                make(h, n)
                hs.append(h)
            return hs

        def bias_loader(h, table, n):
            def start():
                b = ab.bias.next()
                i = nbias[0] % 2
                nbias[0] += 1
                h.bias_ready = pool_dma(d_b[i], [b.rel, bias_in_dram[table], x_free], b.ap[:, 0:n],
                                   scratch["toep"][table, :, 0:n])
                if n == 256:
                    h.bias = lambda q: b.ap[:, 128 if q == 0 else 0:256]
                else:
                    h.bias = lambda q: b.ap[:, 128 * (3 - q):512]
                h.bias_buf = b
            return start

        qa_ready, qb_ready = [None] * 4, [None] * 4
        for c in range(2):
            run(gemm_B("w_in", 256 * c, rhs_H, G_ring, evac_q(Qa, qa_ready, 2 * c, rel1)))
        ka_ready, va_ready = {}, {}
        vt = Buf(x_t[:, 7, :], [x_free])

        def evac_kva(i, bank, tk):
            if i == 0:
                evac_k(KV[0], ka_ready)(0, bank, tk)
                return
            t = act.put([tk, vt.rel], lambda e: e.activation(vt.ap, bank.ap[:, :], ACT.Copy))
            bank.rel = [t]
            tb = T_ring.next()
            for j in range(4):
                tk = pe.put([t, tb.rel, t_cst], lambda e, j=j: e.transpose(
                    tb.ap[:, j * P:(j + 1) * P], vt.ap[:, j * P:(j + 1) * P], ident))
            vv = v_view(KV[0])
            src = tb.ap[:, :].rearrange("p (t n) -> p t n", t=4)
            va_ready[0] = split(src, vv[:, 0, :, 0:P], vv[:, 1, :, 0:P], [tk], KV[0].rel)
            tb.rel = va_ready[0]

        run(gemm_B("w_in", 512, rhs_H, G_ring, evac_kva))

        swa = []
        for n in range(8):
            t_, g = n % 4, n // 4
            h = Head()
            h.kind, h.extra = "swa", None
            hd = t_ + 4 * g
            h.sink = small[:, hd:hd + 1]
            h.q = (Qa[:, 0, t_, :], Qa[:, 1, t_, :])
            h.q_ready = qa_ready[t_]
            kk, vv = k_view(KV[0]), v_view(KV[0])
            h.k = (kk[:, 0, g, :], kk[:, 1, g, :])
            h.k_ready = [ka_ready[g], zeroed[0]]
            h.v = (lambda j: v_view(KV[0])[:, 0, j, 0:P], lambda j: v_view(KV[0])[:, 1, j, 0:P])
            h.v_ready = va_ready[0]
            h.r0 = 64 * g
            h.o = h.q
            h.start = bias_loader(h, hd, 256)
            swa.append(h)
        kb_ready = [{}, {}]
        vb_ready = [{}, {}]

        def kv_gemm(g, wk, ck, wv, cv, rhs, buf):
            return chain(gemm_B(wk, ck, rhs, G_ring, evac_k(buf, kb_ready[g % 2])),
                         gemm_V(wv, cv, rhs, G_ring, evac_v(buf, vb_ready[g % 2])))

        def release_bias(h):
            h.bias_buf.rel = [h.bias_done]

        def wrap(hs):
            for n, h in enumerate(hs):
                s0 = h.start

                def start(h=h, s0=s0, n=n):
                    if n >= 2:
                        release_bias(hs[n - 2])
                    s0()
                h.start = start
            return hs

        attend(wrap(swa), ab, chain(
            gemm_B("w_in", 768, rhs_H, G_ring, evac_q(Qb, qb_ready, 0, rel1)),
            gemm_B("w_in", 1024, rhs_H, G_ring, evac_q(Qb, qb_ready, 2, rel1)),
            kv_gemm(1, "w_in", 1280, "w_in", 1792, rhs_H, KV[1])), 64)
        for h in swa[-2:]:
            release_bias(h)
        oa_ready = [[swa[t_].out_ready, swa[t_ + 4].out_ready] for t_ in range(4)]
        KV[0].rel = [swa[-1].done]
        ob_ready = [None] * 4
        first_gate = [None] * 4

        def evac_gate(i0):
            def f(i, bank, tk):
                b = sg_r.next()
                t = act.put([tk, b.rel], lambda e: e.activation(b.ap, bank.ap[:, :], ACT.Copy))
                bank.rel = [t]
                first_gate[i0 + i] = (b, t)
            return f

        for g in range(2):
            kv = KV[(g + 1) % 2]

            def make(h, n, g=g):
                h.start = bias_loader(h, 8 + 4 * g + n, 512)

            hs = group_heads(kv, zeroed[(g + 1) % 2], Qb, qb_ready, kb_ready[(g + 1) % 2], vb_ready[(g + 1) % 2], 2 * g, make)
            if g == 0:
                nxt = kv_gemm(0, "w_in", 1536, "w_in", 2048, rhs_H, KV[0])
            else:
                nxt = chain(gemm_B("w_in", 2304, rhs_H, G_ring, evac_gate(0)),
                            gemm_B("w_in", 2560, rhs_H, G_ring, evac_gate(2)))
            attend(wrap(hs), ab, nxt, 32)
            for h in hs[-2:]:
                release_bias(h)
            kv.rel = [hs[-1].done]
            for p in range(2):
                ob_ready[2 * g + p] = [hs[2 * p].out_ready, hs[2 * p + 1].out_ready]

        rel2 = barrier()
        ph.close()
        ph = ExitStack()
        MG = sb(ph, [2, KT, T], R)
        m_r = Ring([Buf(sb(ph, [T], F)[:, :], rel2) for _ in range(4)])
        y_r = Ring([Buf(sb(ph, [T], F)[:, :], rel2) for _ in range(2)])
        ada_memory(ph, 2, rel2)
        ada_jobs("ada_t", 2048, 4096, 16, 0)
        load_x(rel2)
        MGt = [None] * KT

        def rhs_of(t, ready):
            return lambda k: (t[:, 0, k, :], t[:, 1, k, :], ready[k])

        for hf in range(2):
            sgs, ms = [None] * 4, [None] * 4

            def evac_sig(i, bank, tk):
                b = sg_r.next()
                t = act.put([tk, b.rel], lambda e: e.activation(b.ap, bank.ap[:, :], ACT.Sigmoid))
                bank.rel = [t]
                sgs[i] = (b, t)

            def evac_ya(i, bank, tk):
                b, t = sgs[i]
                m = m_r.next()
                t = dve.put([tk, t, m.rel], lambda e: e.tensor_tensor(m.ap, bank.ap[:, :], b.ap, ALU.mult))
                bank.rel = [t]
                b.rel = [t]
                ms[i] = (m, t)

            def evac_yb(i, bank, tk):
                b, t = sgs[i]
                y = y_r.next()
                m, tm_ = ms[i]
                t = dve.put([tk, t, y.rel], lambda e: e.tensor_tensor(y.ap, bank.ap[:, :], b.ap, ALU.mult))
                bank.rel = [t]
                b.rel = [t]
                t = pool.put([t, tm_], lambda e: e.tensor_tensor(m.ap, m.ap, y.ap, ALU.add))
                y.rel = [t]
                k = 4 * hf + i
                MGt[k] = split(m.ap, MG[:, 0, k, :], MG[:, 1, k, :], [t], rel2)
                m.rel = MGt[k]

            if hf:
                gemm_A("w_in", 0, 2304 + 512 * hf, 2, rhs_H, 0, evac_sig)
            else:
                for i, (b, t) in enumerate(first_gate):
                    sgs[i] = (b, act.put([t], lambda e: e.activation(b.ap, b.ap, ACT.Sigmoid)))
            gemm_A("w_branch_a", 0, 512 * hf, 1, rhs_of(Qa, oa_ready), 1, evac_ya)
            gemm_A("w_in", 0, 3328 + 512 * hf, 2, rhs_H, 0, evac_sig)
            gemm_A("w_branch_b", 0, 512 * hf, 1, rhs_of(Qb, ob_ready), 1, evac_yb)
        Hrel[0] = [pe.last()]
        t_g1 = mod_bias(16, 8, VCOL["ada_b"] + 16)
        ada_jobs("ada2_0", 0, 6144, 48, 1)
        ada_jobs("adakv_t", 0, 2048, 144, 1)
        ada_jobs("ada2_1", 0, 6144, 96, 1)
        nm = Norm(None, sg_r.bufs + y_r.bufs, False)
        for hf in range(2):
            gemm_A("w_out", 0, 512 * hf, 2, rhs_of(MG, MGt), hf, lambda i, bank, tk, hf=hf: residual(
                4 * hf + i, bank, tk, mcol(2, 4 * hf + i), t_g1, nm), "k" if hf == 0 else "i")
        t_mod = mod_bias(24, 24, VCOL["ada_b"] + 24)
        rms_h(nm, [fold(cA, cB, t_mod, 3, 4, vec8("norm2_g"), None)], cA, cB)
        ada_end()
        rel3 = barrier()
        ph.close()
        outer.close()

        ph = ExitStack()
        ada_memory(ph, 3, rel3)
        nm = Norm(ph, rel3, False)
        AC = [sb(ph, [2, 4, T], R) for _ in range(2)]
        f_r = Ring([Buf(sb(ph, [T], F)[:, :], rel3) for _ in range(4)])
        ac_rel = [rel3, rel3]

        def mlp_in(f):
            act_t = AC[f % 2]
            ready = [None] * 4

            def evac(i, bank, tk):
                b = f_r.next()
                t = act.put([tk, b.rel], lambda e: e.activation(b.ap, bank.ap[:, :], ACT.Relu))
                bank.rel = [t]
                t = pool.put([t], lambda e: e.tensor_tensor(b.ap, b.ap, b.ap, ALU.mult))
                ready[i] = split(b.ap, act_t[:, 0, i, :], act_t[:, 1, i, :], [t], ac_rel[f % 2])
                b.rel = ready[i]
            gemm_A("w_mlp_in", 0, 512 * f, 2, rhs_H, 0, evac)
            return rhs_of(act_t, ready)

        for f in range(FF1 // 512):
            r = mlp_in(f)
            end = f == FF1 // 512 - 1
            for hf in range(2):
                gemm_A("w_mlp_out", 512 * f, 512 * hf, 1, r, hf if end else 1 - hf, lambda i, bank, tk, hf=hf: residual(
                    4 * hf + i, bank, tk, mcol(5, 4 * hf + i), t_mod, nm if end else None), "i" if hf else "k")
            ac_rel[f % 2] = [pe.last()]
        Hrel[0] = [pe.last()]

        def mods2(l, part, n):
            return mod_bias(48 + 48 * l + part, n, VCOL["b_ada_2"] + 48 * l + part)

        V0 = 6
        t_m2 = mods2(0, 0, 48)
        wx = scaled(cC, vec8("final_g"), ALPHA)
        w2 = fold(cA, cB, t_m2, V0, V0 + 1, vec8("final_g"), None)
        wz = dve.put([], lambda e: e.memset(cD, 0.0))
        renorm(nm, rmse, [(cA, cB, w2, HH, Ht, Hrel[0])], cC, cD, [wx, wz])
        ada_end()
        rel4 = barrier()
        ph.close()

        ph = ExitStack()
        ada_memory(ph, 3, rel4)
        nm = Norm(ph, rel4, True)
        YC = sb(ph, [2, KT, T], R)
        g_r = Ring([Buf(sb(ph, [T], F)[:, :], rel4) for _ in range(4)])
        u_r = Ring([Buf(sb(ph, [T + 2], F)[:, :], rel4) for _ in range(2)])
        c_r = Ring([Buf(sb(ph, [T], F)[:, :], rel4) for _ in range(4)])
        for b in u_r.bufs:
            b.rel = [pool.put([rel4], lambda e, b=b: e.memset(b.ap[:, 0:2], 0.0))]
        YCt = [None] * KT
        for hf in range(2):
            gs, cs = [None] * 4, [None] * 4

            def evac_gc(i, bank, tk):
                b = g_r.next()
                t = act.put([tk, b.rel], lambda e: e.activation(b.ap, bank.ap[:, :], ACT.Copy))
                bank.rel = [t]
                gs[i] = (b, t)

            def evac_v2(i, bank, tk):
                k = 4 * hf + i
                b, t = gs[i]
                u, c = u_r.next(), c_r.next()
                t = dve.put([tk, t, u.rel], lambda e: e.tensor_tensor(u.ap[:, 2:T + 2], bank.ap[:, :], b.ap, ALU.mult))
                bank.rel = [t]
                b.rel = [t]
                cw = [vec[:, VCOL["conv_w_2"] + 8 * j + k:VCOL["conv_w_2"] + 8 * j + k + 1] for j in range(3)]
                t = dve.put([t, c.rel, t_vec], lambda e: e.tensor_scalar(c.ap, u.ap[:, 0:T], cw[0], None, ALU.mult))
                for j in (1, 2):
                    t = dve.put([t], lambda e, j=j: e.scalar_tensor_tensor(
                        out=c.ap, in0=u.ap[:, j:T + j], scalar=cw[j], in1=c.ap, op0=ALU.mult, op1=ALU.add))
                u.rel = [t]
                cs[i] = (c, t)

            def evac_gb(i, bank, tk):
                k = 4 * hf + i
                c, t = cs[i]
                t = dve.put([tk, t], lambda e: e.tensor_tensor(c.ap, bank.ap[:, :], c.ap, ALU.mult))
                bank.rel = [t]
                YCt[k] = split(c.ap, YC[:, 0, k, :], YC[:, 1, k, :], [t], rel4)
                c.rel = YCt[k]

            gemm_A("conv_w_in_2", 0, 1024 + 512 * hf, 2, rhs_H, hf, evac_gc)
            gemm_A("conv_w_in_2", 0, 2048 + 512 * hf, 2, rhs_H, 1 - hf, evac_v2)
            gemm_A("conv_w_in_2", 0, 512 * hf, 2, rhs_H, hf, evac_gb)
        Hrel[0] = [pe.last()]
        for hf in range(2):
            gemm_A("conv_w_out_2", 0, 512 * hf, 2, rhs_of(YC, YCt), hf, lambda i, bank, tk, hf=hf: residual(
                4 * hf + i, bank, tk, mcol(V0 + 2, 4 * hf + i), t_m2, nm), "i" if hf else "k")

        def ln1_h(l, nm, t_m):
            V = 6 + 6 * l
            w = fold(cA, cB, t_m, V + 3, V + 4, vec8("ln1_g_2", l), vec8("ln1_b_2", l))
            wx = [scaled(cC, vec8("ln1_g_2", l), ALPHA), scaled(cD, vec8("ln1_b_2", l), ALPHA)]
            renorm(nm, lne, [(cA, cB, w, HH, Ht, Hrel[0])], cC, cD, wx)

        ln1_h(0, nm, t_m2)
        ada_end()
        rel5 = barrier()
        ph.close()

        def ffn2(l, t_m, nm, AC, rel, rings, n):
            V = 6 + 6 * l
            g_r = Ring([Buf(sb(rings, [T], F)[:, :], rel) for _ in range(4)])
            f_r = Ring([Buf(sb(rings, [T], F)[:, :], rel) for _ in range(n)] or nm.sq.bufs)
            ac_rel = [rel, rel]

            def evacs(f):
                act_t = AC[f % 2]
                ready = [None] * 4
                gs = [None] * 4

                def evac_g(i, bank, tk):
                    b = g_r.next()
                    t = act.put([tk, b.rel], lambda e: e.activation(b.ap, bank.ap[:, :], ACT.Silu))
                    bank.rel = [t]
                    gs[i] = (b, t)

                def evac_u(i, bank, tk):
                    g, t = gs[i]
                    b = f_r.next()
                    t = dve.put([tk, t, b.rel], lambda e: e.tensor_tensor(b.ap, bank.ap[:, :], g.ap, ALU.mult))
                    bank.rel = [t]
                    g.rel = [t]
                    ready[i] = split(b.ap, act_t[:, 0, i, :], act_t[:, 1, i, :], [t], ac_rel[f % 2])
                    b.rel = ready[i]

                return evac_g, evac_u, rhs_of(act_t, ready)

            def res(hf, nm):
                return lambda i, bank, tk: residual(4 * hf + i, bank, tk, mcol(V + 5, 4 * hf + i), t_m(), nm)

            def narrow(f):
                eg, eu, r = evacs(f)
                run(gemm_B(f"gate{l}", 2560, rhs_H, Ring(psum[0:2]), eg))
                run(gemm_B(f"up{l}", 2560, rhs_H, Ring(psum[2:4]), eu))
                sl = take("C", f"down{l}", 2560, 0)
                order = [4, 5, 6, 7, 0, 1, 2, 3]
                tks = [None] * 8
                for kt in range(2):
                    hi, lo, tk = r(kt)
                    for i in range(8):
                        bank = psum[order[i]]
                        c = slice(i * P, (i + 1) * P)
                        tks[i] = mm3(bank.ap[:, :], sl.hi[:, kt, c], sl.lo[:, kt, c], hi, lo, kt == 0, kt == 1,
                                     [sl.ready, tk, bank.rel if kt == 0 else None], kt == 1)
                release(sl, tks[7])
                for i in range(8):
                    residual(i, psum[order[i]], tks[i], mcol(V + 5, i), t_m())
                ac_rel[f % 2] = [pe.last()]

            for f in range(5):
                if f == 4:
                    narrow(4)
                n = f + (f == 4)
                eg, eu, r = evacs(n)
                gemm_A(f"gate{l}", 0, 512 * f, 2, rhs_H, 0, eg)
                gemm_A(f"up{l}", 0, 512 * f, 2, rhs_H, 1, eu)
                for hf in range(2):
                    gemm_A(f"down{l}", 512 * f, 512 * hf, 1, r, hf, res(hf, nm if f == 4 else None), "i" if hf else "k")
                ac_rel[n % 2] = [pe.last()]
            Hrel[0] = [pe.last()]

        ph = ExitStack()
        Q2 = sb(ph, [2, KT, T], R)
        inner = ExitStack()
        KVt = sb(inner, [12288], R)
        top = ExitStack()
        nm = Norm(top, rel5, True)
        AC = [KVt[:, 4096 * i:4096 * (i + 1)].rearrange("p (s k n) -> p s k n", s=2, k=4) for i in range(2)]
        ffn2(0, lambda: t_m2, nm, AC, rel5, top, 0)

        V1 = 12
        t_kv = mod_bias(144, 16, VCOL["b_ada_kv_2"])
        t_m3 = mods2(1, 0, 16)
        hq = KVt[:, 0:8192].rearrange("p (s k n) -> p s k n", s=2, k=KT)
        hq = (hq[:, 0, :, :], hq[:, 1, :, :])
        hqt = [None] * KT
        rel6 = [pe.last()]
        g2, b2 = vec8("ln2_g_2"), vec8("ln2_b_2")
        renorm(nm, lne, [(cA, cB, fold(cA, cB, t_m3, V1, V1 + 1, g2, b2), hq, hqt, rel6),
                         (cC, cD, fold(cC, cD, t_kv, 18, 19, g2, b2), HH, Ht, Hrel[0])],
               cE, cF, [scaled(cE, g2, ALPHA), scaled(cF, b2, ALPHA)])
        d_sx = dsem()
        t_spill = dma(d_sx, [xt[k] for k in range(KT)], scratch["x"][:, :].rearrange("(kt p) n -> p kt n", p=P), x_t[:, :, :])
        stores.append(t_spill)
        q_ready = [None] * KT
        for hf in range(2):
            gemm_A("attn_w_q_2", 0, 512 * hf, 2, lambda k: (hq[0][:, k, :], hq[1][:, k, :], hqt[k]), hf,
                   evac_q(Q2, q_ready, 4 * hf, rel6))
        q_done = pe.last()
        rel7 = barrier()
        top.close()
        pt_t = sb(inner, [2, 1280], R)
        KV = [Buf(KVt[:, 6144 * i:6144 * (i + 1)], [q_done]) for i in range(2)]
        zeroed = [zero_halves(KV[i], [q_done]) for i in range(2)]
        AFr = Ring([Buf(sb(inner, [T], R), rel7) for _ in range(2)])
        BF = sb(inner, [T], R)
        st = ExitStack()
        xf = x_t[:, :, :].rearrange("p k n -> p (k n)")
        relx = [t_spill, rel7]
        AF = xf[:, 2560:3072]
        z1, z2, z3 = (xf[0:16, 512 * i:512 * (i + 1)] for i in range(3))
        fr = xf[0:16, 3072:3584]
        e1 = xf[0:16, 3584:4096]
        wfr = sb(st, [P], F)
        wfh, wfl, fhi = sb(st, [P], R), sb(st, [P], R), sb(st, [T], R)
        d_wf = dsem()
        t = dma(d_wf, rel7, wfr[:, :].rearrange("p (k n) -> p k n", k=8), a["w_f_2"].rearrange("(k p) n -> p k n", p=P))
        tw = split(wfr[:, :], wfh[:, :], wfl[:, :], [t], rel7)
        bank = psum[0]
        for k in range(KT):
            hi, lo, tk = rhs_H(k)
            t = mm3(bank.ap[0:16, :], wfh[:, 16 * k:16 * k + 16], wfl[:, 16 * k:16 * k + 16], hi, lo, k == 0, k == 7,
                    [tw, tk, bank.rel], True)
        t = act.put([t, relx], lambda e: e.activation(z1, bank.ap[0:16, :], ACT.Identity, bias=small[0:16, 8:9]))
        bank.rel = [t]
        tz1 = t
        t = act.put([t, relx], lambda e: e.activation(e1, z1, ACT.Abs))
        t = act.put([t], lambda e: e.activation(e1, e1, ACT.Exp, scale=-1.0))
        t = dve.put([t, relx], lambda e: e.tensor_scalar(z2, e1, 2.0, None, ALU.add))
        t = dve.put([t], lambda e: e.reciprocal(z2, z2))
        t = dve.put([t], lambda e: e.tensor_tensor(e1, e1, z2, ALU.mult))
        t = dve.put([t], lambda e: e.tensor_tensor(z2, e1, e1, ALU.mult))
        t = dve.put([t, relx], lambda e: e.tensor_scalar(z3, z2, 2.0 / 17, None, ALU.mult))
        for n in range(15, 2, -2):
            t = dve.put([t], lambda e, n=n: e.scalar_tensor_tensor(
                out=z3, in0=z3, scalar=2.0 / n, in1=z2, op0=ALU.add, op1=ALU.mult))
        t = dve.put([t], lambda e: e.scalar_tensor_tensor(out=z3, in0=z3, scalar=2.0, in1=e1, op0=ALU.add, op1=ALU.mult))
        t = dve.put([t, tz1], lambda e: e.scalar_tensor_tensor(out=z1, in0=z1, scalar=0.0, in1=z3, op0=ALU.min, op1=ALU.subtract))
        t2 = dve.put([t], lambda e: e.memset(z2, 1.0))
        t = dve.put([t, t2, relx], lambda e: e.tensor_tensor_scan(fr, z2, z1, 0.0, ALU.mult, ALU.add))
        thi = act.put([t, rel7], lambda e: e.activation(fhi[0:16, :], fr, ACT.Copy))
        t_lo = dve.put([thi], lambda e: e.tensor_tensor(z3, fr, fhi[0:16, :].bitcast(F), ALU.subtract))
        tz = pool.put([relx], lambda e: e.memset(AF, 0.0))
        tzb = pool.put([rel7], lambda e: e.memset(BF[:, :].bitcast(F), 0.0))
        ft = []
        for r in (64, 96):
            ft.append(pool.put([tz], lambda e, r=r: e.memset(AF[r:r + 16, :], 1.0)))
        for r in (0, 32):
            ft.append(pool.put([tzb], lambda e, r=r: e.memset(BF[r:r + 16, :].bitcast(F), 1.0)))
        ft.append(act.put([tz, thi], lambda e: e.activation(AF[0:16, :], fhi[0:16, :].bitcast(F), ACT.Copy)))
        ft.append(act.put([tz, t_lo], lambda e: e.activation(AF[32:48, :], z3, ACT.Copy)))
        ft.append(act.put([tzb, thi], lambda e: e.activation(BF[64:80, :], fhi[0:16, :].bitcast(F), ACT.Copy, scale=-1.0)))
        ft.append(act.put([tzb, t_lo], lambda e: e.activation(BF[96:112, :], z3, ACT.Copy, scale=-1.0)))
        rel8 = [rel7, t_spill, ft, t_lo]
        st.close()

        ab = attn_bufs(rel8, pt_t)
        kb_ready = [{}, {}]
        vb_ready = [{}, {}]
        run(kv_gemm(0, "w_k_2", 0, "w_v_2", 0, rhs_H, KV[0]))
        o_ready = [None] * KT
        for g in range(4):
            kv = KV[g % 2]

            def make(h, n, g=g):
                hd = 4 * g + n

                def start():
                    b = AFr.next()
                    t = pool.put([ft, b.rel], lambda e: e.tensor_scalar(
                        b.ap[:, :], AF, hmask[:, hd:hd + 1], 1.0, ALU.mult, ALU.mult))
                    h.extra = (b.ap[:, :], BF[:, :], [t, ft])
                    h.bias_ready = None
                    h.bias = lambda q: maskT[:, 128 * (3 - q):512]
                    h.af = b
                h.start = start

            hs = group_heads(kv, zeroed[g % 2], Q2, q_ready, kb_ready[g % 2], vb_ready[g % 2], 2 * g, make)
            for n, h in enumerate(hs):
                s0 = h.start

                def start(h=h, s0=s0, n=n, hs=hs):
                    if n >= 2:
                        hs[n - 2].af.rel = [hs[n - 2].s_done]
                    s0()
                h.start = start
            nxt = None
            if g < 3:
                nxt = kv_gemm(g + 1, "w_k_2", 256 * (g + 1), "w_v_2", 256 * (g + 1), rhs_H, KV[(g + 1) % 2])
            attend(hs, ab, nxt, 32 if nxt else 0)
            for h in hs[-2:]:
                h.af.rel = [h.s_done]
            kv.rel = [hs[-1].done]
            for p in range(2):
                o_ready[2 * g + p] = [hs[2 * p].out_ready, hs[2 * p + 1].out_ready]
        Hrel[0] = [pe.last()]
        rel9 = barrier()
        d_rx = dsem()
        t = dma(d_rx, rel9, x_t[:, :, :], scratch["x"][:, :].rearrange("(kt p) n -> p kt n", p=P))
        for k in range(KT):
            xt[k] = [t]
        inner.close()
        top = ExitStack()
        nm = Norm(top, rel9, True)
        ada_memory(top, 4, rel9)
        ada_load()
        t_m4 = mods2(1, 16, 8)
        for hf in range(2):
            gemm_A("attn_w_o_2", 0, 512 * hf, 2, rhs_of(Q2, o_ready), hf, lambda i, bank, tk, hf=hf: residual(
                4 * hf + i, bank, tk, mcol(V1 + 2, 4 * hf + i), t_m4, nm), "i" if hf else "k")
        ln1_h(1, nm, mods2(1, 24, 16))
        ada_end()
        rel10 = barrier()
        top.close()
        ph.close()
        ph = ExitStack()
        ada_memory(ph, 2, rel10)
        nm = Norm(ph, rel10, True)
        AC = [sb(ph, [2, 4, T], R) for _ in range(2)]
        last_gate = []

        def gate2():
            if not last_gate:
                last_gate.append(mods2(1, 40, 8))
            return last_gate[0]

        ffn2(1, gate2, nm, AC, rel10, ph, 4)
        ada_end()
        renorm(nm, lne, [], vec8("ln2_g_2", 1), vec8("ln2_b_2", 1), t_vec, ACT)
        d_o = dsem()
        for hf in range(2):
            t_out = dma(d_o, [xt[k] for k in range(4 * hf, 4 * hf + 4)],
                        out_t[512 * hf:512 * hf + 512, :].rearrange("(kt p) n -> p kt n", p=P), x_t[:, 4 * hf:4 * hf + 4, :])
        ph.close()
        assert state["take"] == len(plan) and not ada and not ada_pending
        finals = [t_out] + stores

        block = ctx.enter_context(nc.Block())

        @block.sync
        def _(eng):
            sp.replay(eng)
            last = {}
            for sem, value in finals:
                last[id(sem)] = (sem, max(value, last.get(id(sem), (sem, 0))[1]))
            for sem, value in last.values():
                eng.wait_ge(sem, value)

        @block.tensor
        def _(eng):
            pe.replay(eng)

        @block.scalar
        def _(eng):
            act.replay(eng)

        @block.vector
        def _(eng):
            dve.replay(eng)

        @block.gpsimd
        def _(eng):
            pool.replay(eng)


def kernel(**inputs):
    import concourse.bacc as bacc
    from concourse.bass_utils import run_bass_kernel_spmd as launch

    g = {k: np.asarray(v) for k, v in inputs.items()}

    def cols(v):
        return np.asarray(v).reshape(-1, P).T

    arrays = {}
    arrays["x_t"] = np.ascontiguousarray(g["x"][0].T)
    arrays["c_b"] = np.ascontiguousarray(np.broadcast_to(g["c"], (P, D)))
    arrays["c_b2"] = np.ascontiguousarray(np.broadcast_to(g["c_2"], (P, D)))
    arrays["ada_t"] = np.ascontiguousarray(g["ada_w"][0].T)
    arrays["ada2_0"] = np.ascontiguousarray(g["w_ada_2"][0].T)
    arrays["ada2_1"] = np.ascontiguousarray(g["w_ada_2"][1].T)
    arrays["adakv_t"] = np.ascontiguousarray(g["w_ada_kv_2"].T)
    arrays["vecs"] = np.ascontiguousarray(np.concatenate([cols(g[n].reshape(-1)) for n, _ in VECS], axis=1))
    arrays["consts"], arrays["hot"] = constants()
    arrays["sinks"] = np.ascontiguousarray(np.broadcast_to(g["attn_sinks"], (P, 8)))
    arrays["b_f"] = np.ascontiguousarray(g["b_f_2"].reshape(16, 1))
    arrays["rel_bias"] = np.ascontiguousarray(g["rel_bias"])
    order = np.concatenate([np.arange(64) + 64 * (t + 4 * two) for t in range(4) for two in range(2)])
    w_in = g["w_in"][0]
    arrays["w_in"] = np.ascontiguousarray(np.concatenate([w_in[:, order], w_in[:, 512:]], axis=1))
    arrays["w_branch_a"] = np.ascontiguousarray(g["w_branch_a"][0][order])
    for n in ("w_branch_b", "w_out", "w_mlp_in", "w_mlp_out", "conv_w_in_2", "conv_w_out_2", "attn_w_q_2", "attn_w_o_2"):
        arrays[n] = np.ascontiguousarray(g[n][0])
    for n in ("w_k_2", "w_v_2", "w_f_2"):
        arrays[n] = np.ascontiguousarray(g[n])
    for l in range(2):
        arrays[f"gate{l}"] = np.ascontiguousarray(g["ffn_w_gate_2"][l])
        arrays[f"up{l}"] = np.ascontiguousarray(g["ffn_w_up_2"][l])
        arrays[f"down{l}"] = np.ascontiguousarray(g["ffn_w_down_2"][l])

    nc = bacc.Bacc("TRN2", target_bir_lowering=False, num_devices=1)
    aps, feeds = {}, {}
    for n, v in arrays.items():
        feeds[f"in_{n}"] = v
        aps[n] = nc.dram_tensor(f"in_{n}", v.shape, mybir.dt.from_np(v.dtype), kind="ExternalInput").ap()
    out_t = nc.dram_tensor("out_t", (D, T), F, kind="ExternalOutput").ap()
    scratch = {"rows": nc.dram_tensor("rows", (16, 1024), F, kind="Internal").ap(),
               "toep": nc.dram_tensor("toep", (16, P, T), F, kind="Internal").ap(),
               "x": nc.dram_tensor("x_keep", (D, T), F, kind="Internal").ap()}
    build(nc, aps, out_t, scratch)
    r = launch(nc, [feeds], core_ids=[0])
    return np.ascontiguousarray(np.asarray(r.results[0]["out_t"]).T)[None]
```

```python
import math
from contextlib import ExitStack

import numpy as np

import concourse.bass as bass
from concourse import mybir

F = mybir.dt.float32
R = mybir.dt.float32r
ALU = mybir.AluOpType
ACT = mybir.ActivationFunctionType

P = 128
T = 512
D = 1024
KT = D // P
NEG = -1.0e30
LOW = -3.0e38
RMS_EPS = 1e-6
LN_EPS = 1e-5
ALPHA = math.sqrt(2.0)
QSCALE = 0.125
NW = 2
NRAW = 2
FF1 = 4096
FF2 = 2816

VECS = [("ada_b", 48), ("norm1_g", 8), ("norm2_g", 8), ("final_g", 8), ("b_ada_2", 96), ("b_ada_kv_2", 16),
        ("ln1_g_2", 16), ("ln1_b_2", 16), ("ln2_g_2", 16), ("ln2_b_2", 16), ("conv_w_2", 24)]
VCOL = {}
_n = 0
for _name, _w in VECS:
    VCOL[_name] = _n
    _n += _w
NV = _n
C_ID, C_ONE, C_MASK, C_HEAD = 0, 128, 256, 768
NC = 784
SKEW = P * 648


def buckets(dist):
    n = np.maximum(dist, 0)
    nf = np.maximum(n, 1).astype(np.float32)
    large = 16 + (np.log(nf / np.float32(16)) / np.float32(math.log(128.0)) * np.float32(16)).astype(np.int32)
    return np.where(n < 16, n, np.minimum(large, 31))


def constants():
    c = np.zeros((P, NC), np.float32)
    i = np.arange(P)
    c[i, C_ID + i] = 1.0
    c[:, C_ONE:C_ONE + P] = 1.0 / D
    j = np.arange(T)
    c[:, C_MASK:C_MASK + T] = np.where(384 + i[:, None] - j[None, :] >= 0, 0.0, NEG)
    c[:, C_HEAD:C_HEAD + 16] = (i[:, None] % 32 == np.arange(16)[None, :])
    hot = np.zeros((33, 1024), np.float32)
    for col, dist, ok in [(m, 511 - m, 511 - m >= 0) for m in range(640)] + \
                         [(640 + m, 255 - m, 0 <= 255 - m < 128) for m in range(384)]:
        hot[int(buckets(np.array(dist))) if ok else 32, col] = 1.0
    return c, hot


class Bind:

    def matmul(self, *a, **k):
        return lambda e: e.matmul(*a, **k)

    def transpose(self, *a, **k):
        return lambda e: e.transpose(*a, **k)

    def activation(self, *a, **k):
        return lambda e: e.activation(*a, **k)

    def tensor_tensor(self, *a, **k):
        return lambda e: e.tensor_tensor(*a, **k)

    def tensor_scalar(self, *a, **k):
        return lambda e: e.tensor_scalar(*a, **k)

    def tensor_copy(self, *a, **k):
        return lambda e: e.tensor_copy(*a, **k)

    def scalar_tensor_tensor(self, *a, **k):
        return lambda e: e.scalar_tensor_tensor(*a, **k)

    def tensor_tensor_reduce(self, *a, **k):
        return lambda e: e.tensor_tensor_reduce(*a, **k)

    def tensor_tensor_scan(self, *a, **k):
        return lambda e: e.tensor_tensor_scan(*a, **k)

    def reciprocal(self, *a, **k):
        return lambda e: e.reciprocal(*a, **k)

    def memset(self, *a, **k):
        return lambda e: e.memset(*a, **k)

    def dma(self, sem, *a, **k):
        return lambda e: e.dma_start(*a, **k).then_inc(sem, 16)


BIND = Bind()


class Engine:

    def __init__(self, sem, serial=False):
        self.sem, self.count, self.ops, self.seen, self.serial = sem, 0, [], {}, serial

    def put(self, waits, fn, inc=True):
        need = {}
        stack = [waits, self.last() if self.serial and self.count else None]
        while stack:
            w = stack.pop()
            if isinstance(w, list):
                stack.extend(w)
            elif w is not None:
                sem, value = w
                if value > self.seen.get(id(sem), 0):
                    self.seen[id(sem)] = value
                    need[id(sem)] = sem
        self.ops.append(([(s, self.seen[k]) for k, s in need.items()], fn(BIND), inc))
        if inc:
            self.count += 1
        return (self.sem, self.count)

    def last(self):
        return (self.sem, self.count)

    def replay(self, eng):
        for waits, fn, inc in self.ops:
            for sem, value in waits:
                eng.wait_ge(sem, value)
            ins = fn(eng)
            if inc:
                ins.then_inc(self.sem, 1)


class Buf:

    def __init__(self, ap, rel=None):
        self.ap, self.rel = ap, list(rel or [])


class Ring:
    def __init__(self, bufs):
        self.bufs, self.n = bufs, 0

    def next(self):
        self.n += 1
        return self.bufs[(self.n - 1) % len(self.bufs)]


class DmaSem:
    def __init__(self, sem):
        self.sem, self.count = sem, 0


def build(nc, a, out_t, scratch):
    ctx = ExitStack()
    with ctx:
        names = [0]

        def sb(stack, shape, dt):
            names[0] += 1
            return stack.enter_context(nc.sbuf_tensor(f"t{names[0]}", [P] + shape, dt))

        def semaphore(name):
            return ctx.enter_context(nc.semaphore(name))

        pe, act, dve, pool, sp = (Engine(semaphore(f"s_{n}"), n == "pool") for n in ("pe", "act", "dve", "pool", "sp"))
        ndma = [0]

        def dsem():
            ndma[0] += 1
            return DmaSem(semaphore(f"d{ndma[0]}"))

        stores = []

        def dma(ds, waits, dst, src):
            ds.count += 16
            s = ds.sem
            sp.put(waits, lambda e: e.dma(s, dst, src), inc=False)
            return (s, ds.count)

        def pool_dma(ds, waits, dst, src):
            ds.count += 16
            s = ds.sem
            pool.put(waits, lambda e: e.dma(s, dst, src), inc=False)
            return (s, ds.count)

        def barrier():
            return [e.last() for e in (pe, act, dve, pool)] + list(stores)

        psum = [Buf(ctx.enter_context(nc.psum_tensor(f"ps{i}", [P, T], F))) for i in range(8)]

        x_t = sb(ctx, [KT, T], F)
        raw = sb(ctx, [NRAW, 2048], F)
        WH = sb(ctx, [NW, 2048], R)
        WL = sb(ctx, [NW, 2048], R)
        H_t = sb(ctx, [2, KT, T], R)
        csb = sb(ctx, [D], F)
        vec = sb(ctx, [NV], F)
        mods = sb(ctx, [160], F)
        cst = sb(ctx, [NC], F)
        cols = sb(ctx, [64], F)
        stat = sb(ctx, [2, 5, 4], F)
        small = sb(ctx, [32], F)
        wfr = sb(ctx, [P], F)

        ident = cst[:, C_ID:C_ID + P]
        ones = cst[:, C_ONE:C_ONE + P]
        maskT = cst[:, C_MASK:C_MASK + T]
        hmask = cst[:, C_HEAD:C_HEAD + 16]
        zcol, rmse, lne = cols[:, 0:1], cols[:, 1:2], cols[:, 2:3]
        X = [Buf(x_t[:, k, :]) for k in range(KT)]
        xt = [[] for _ in range(KT)]

        d_c, d_v, d_x, d_cs, d_s = (dsem() for _ in range(5))
        t_cb = dma(d_cs, [], csb[:, :], a["c_b"])
        t_cst = pool_dma(d_c, [], cst[:, :], a["consts"])
        t_vec = pool_dma(d_v, [], vec[:, :], a["vecs"])
        t_sink = pool_dma(d_s, [], small[:, 0:8], a["sinks"])
        t_sink = pool_dma(d_s, [], small[0:16, 8:9], a["b_f"])
        xload = [None, None]
        dx = [dsem(), dsem()]

        def load_x(waits):
            for hf in range(2):
                k0 = 4 * hf
                xload[hf] = dma(dx[hf], waits, x_t[:, k0:k0 + 4, :],
                                a["x_t"][k0 * P:(k0 + 4) * P, :].rearrange("(kt p) n -> p kt n", p=P))
                for k in range(k0, k0 + 4):
                    xt[k] = [xload[hf]]

        t_col = [dve.put([], lambda e, v=v, i=i: e.memset(cols[:, i:i + 1], v))
                 for i, v in enumerate((0.0, RMS_EPS, LN_EPS))]

        plan = []

        def plan_A(w, r0, c0, n):
            plan.extend(("A", w, r0 + 512 * s, c0) for s in range(n))

        def plan_B(w, c0):
            plan.append(("B", w, 0, c0))

        for c0 in (0, 256, 512, 768, 1024):
            plan_B("w_in", c0)
        plan_B("w_in", 1280)
        plan_B("w_in", 1792)
        plan_B("w_in", 1536)
        plan_B("w_in", 2048)
        plan_B("w_in", 2304)
        plan_B("w_in", 2560)
        for hf in range(2):
            if hf:
                plan_A("w_in", 0, 2304 + 512 * hf, 2)
            plan_A("w_branch_a", 0, 512 * hf, 1)
            plan_A("w_in", 0, 3328 + 512 * hf, 2)
            plan_A("w_branch_b", 0, 512 * hf, 1)
        for hf in range(2):
            plan_A("w_out", 0, 512 * hf, 2)
        for f in range(FF1 // 512):
            plan_A("w_mlp_in", 0, 512 * f, 2)
            for hf in range(2):
                plan_A("w_mlp_out", 512 * f, 512 * hf, 1)

        def plan_ffn2(l):
            for f in range(5):
                if f == 4:
                    plan_B(f"gate{l}", 2560)
                    plan_B(f"up{l}", 2560)
                    plan.append(("C", f"down{l}", 2560, 0))
                plan_A(f"gate{l}", 0, 512 * f, 2)
                plan_A(f"up{l}", 0, 512 * f, 2)
                for hf in range(2):
                    plan_A(f"down{l}", 512 * f, 512 * hf, 1)

        for hf in range(2):
            for c0 in (1024, 2048, 0):
                plan_A("conv_w_in_2", 0, c0 + 512 * hf, 2)
        for hf in range(2):
            plan_A("conv_w_out_2", 0, 512 * hf, 2)
        plan_ffn2(0)
        for hf in range(2):
            plan_A("attn_w_q_2", 0, 512 * hf, 2)
        for g in range(4):
            plan_B("w_k_2", 256 * g)
            plan_B("w_v_2", 256 * g)
        for g in range(4):
            plan_B("attn_w_o_2", 256 * g)
        plan_ffn2(1)

        class Raw:

            def __init__(self, ap, rel):
                self.ap, self.rel, self.sem, self.busy = ap, list(rel), dsem(), False

            def take(self):
                assert not self.busy
                self.busy = True
                return self

            def done(self, tickets):
                self.rel, self.busy = tickets, False

        raws = [Raw(raw[:, i, :], []) for i in range(NRAW)]
        ada_sems = [DmaSem(semaphore(f"ada{i}")) for i in range(6)]
        ada_raws = []
        w_rel = [[] for _ in range(NW)]
        w_dma, w_conv = {}, {}
        state = {"dma": 0, "conv": 0, "take": 0}
        SHAPE = {"A": (4, 512), "B": (8, 256), "C": (2, 1024)}

        def slot_dma():
            n = state["dma"]
            if n >= len(plan):
                return
            kind, w, r0, c0 = plan[n]
            kt, nn = SHAPE[kind]
            r = raws[n % NRAW].take()
            src = a[w][r0:r0 + kt * P, c0:c0 + nn].rearrange("(kt p) n -> p kt n", p=P)
            dst = r.ap.rearrange("p (kt n) -> p kt n", kt=kt)
            w_dma[n] = (r, dma(r.sem, r.rel, dst, src))
            state["dma"] += 1

        pieces = []

        def conv_start(parts):
            n = state["conv"]
            if n >= len(plan) or pieces:
                return
            r, landed = w_dma.pop(n)
            b = n % NW
            w_conv[n] = tickets = []
            step = 2048 // parts

            def piece(c):
                def go():
                    hi = act.put([landed, w_rel[b]], lambda e: e.activation(WH[:, b, c], r.ap[:, c], ACT.Copy))
                    lo = (pool if parts > 1 else dve).put([landed, hi, w_rel[b]], lambda e: e.tensor_tensor(
                        WL[:, b, c], r.ap[:, c], WH[:, b, c].bitcast(F), ALU.subtract))
                    tickets.extend([hi, lo])
                    if c.stop == 2048:
                        r.done(list(tickets))
                        state["conv"] += 1
                return go

            pieces.extend(piece(slice(step * i, step * (i + 1))) for i in range(parts))

        def slot_conv():
            conv_start(1)
            while pieces:
                pieces.pop(0)()

        def some_conv():
            if pieces:
                pieces.pop(0)()
                if not pieces:
                    more_dma()

        def more_dma():
            while state["dma"] < min(len(plan), state["conv"] + NRAW):
                slot_dma()

        def ready_for(n):
            while state["conv"] <= min(n, len(plan) - 1):
                while state["dma"] <= state["conv"]:
                    slot_dma()
                slot_conv()

        def ahead(n):
            if gentle[0]:
                if state["conv"] <= n < len(plan) and n in w_dma:
                    conv_start(4)
            elif n < len(plan):
                ready_for(n)
            more_dma()

        gentle = [False]
        ada_rate, ada_credit = [1], [0]

        class Slot:
            pass

        def take(kind, w, r0, c0):
            n = state["take"]
            assert plan[n] == (kind, w, r0, c0), (plan[n], kind, w, r0, c0)
            ready_for(n)
            ahead(n + 1)
            ada_credit[0] += ada_rate[0]
            ada_step(int(ada_credit[0]))
            ada_credit[0] %= 1
            ada_load()
            state["take"] += 1
            s = Slot()
            kt, nn = SHAPE[kind]
            b = n % NW
            s.hi = WH[:, b, :].rearrange("p (kt n) -> p kt n", kt=kt)
            s.lo = WL[:, b, :].rearrange("p (kt n) -> p kt n", kt=kt)
            s.ready = w_conv.pop(n)
            s.b = b
            return s

        def release(s, ticket):
            w_rel[s.b] = [ticket]

        ada = []
        ada_pending = []
        cs_ready = [None]
        cs_last = [None]
        mod_raw = {}

        def ada_jobs(name, row0, nrows, col0, which):
            for r in range(0, nrows, 256):
                ada.append((name, row0 + r, col0 + r // P, which))

        def silu_c(landed):
            r = ada_raws[0].take()
            t = act.put([landed, r.rel], lambda e: e.activation(r.ap[:, 0:D], csb[:, :], ACT.Sigmoid))
            t = dve.put([t], lambda e: e.tensor_tensor(csb[:, :], csb[:, :], r.ap[:, 0:D], ALU.mult))
            r.done([t])
            cs_ready[0] = t

        cs_now, cs_next = [0], []
        ada_hold = [False]
        ada_queue = [dma]

        def ada_memory(stack, n, rel):
            assert not ada_pending
            ada_hold[0] = False
            ada_raws[:] = [Raw(sb(stack, [2048], F)[:, :] if type(n) is int else p, rel)
                           for p in (range(n) if type(n) is int else n)]
            for r, sem in zip(ada_raws, ada_sems[:3] if ada_queue[0] is dma else ada_sems[3:]):
                r.sem = sem

        def ada_end():
            ada_step()
            ada_raws[:] = []

        def ada_load():
            while ada and not ada_hold[0]:
                free = [r for r in ada_raws if not r.busy]
                if not free:
                    return
                if ada[0][3] != cs_now[0]:
                    if ada_pending:
                        return
                    if not cs_next:
                        cs_next.append(dma(d_cs, [cs_last[0]], csb[:, :], a["c_b2"]))
                        return
                    silu_c(cs_next.pop())
                    cs_now[0] = ada[0][3]
                name, row, col, _ = ada.pop(0)
                r = free[0].take()
                src = a[name][row:row + 256, :].rearrange("(a p) k -> p a k", p=P)
                ada_pending.append((r, ada_queue[0](r.sem, r.rel, r.ap.rearrange("p (a k) -> p a k", a=2), src), col))

        def ada_step(most=100):
            while ada_pending and most:
                most -= 1
                r, landed, col = ada_pending.pop(0)
                t = None
                for i in range(2):
                    v = r.ap[:, i * D:(i + 1) * D]
                    t = dve.put([landed, cs_ready[0]], lambda e: e.tensor_tensor_reduce(
                        out=v, in0=v, in1=csb[:, :], scale=1.0, scalar=0.0, op0=ALU.mult, op1=ALU.add,
                        accum_out=mods[:, col + i:col + i + 1]))
                r.done([t])
                cs_last[0] = t
                mod_raw[col] = t

        def ada_until(col_end, col0):
            need = range(col0, col_end, 2)
            while not all(c in mod_raw for c in need):
                assert ada_pending or not ada_hold[0]
                ada_load()
                ada_step(1)
            return [mod_raw[c] for c in need]

        def mod_bias(col0, n, vcol):
            w = ada_until(col0 + n, col0)
            return dve.put([w, t_vec], lambda e: e.tensor_tensor(
                mods[:, col0:col0 + n], mods[:, col0:col0 + n], vec[:, vcol:vcol + n], ALU.add))

        def mcol(v, k):
            return mods[:, v * 8 + k:v * 8 + k + 1]

        def vcol(name, k):
            return vec[:, VCOL[name] + k:VCOL[name] + k + 1]

        def mm3(bank, w_hi, w_lo, h_hi, h_lo, first, last, waits, inc):
            pe.put(waits, lambda e: e.matmul(bank, w_hi, h_hi, start=first, stop=False), inc=False)
            pe.put([], lambda e: e.matmul(bank, w_hi, h_lo, start=False, stop=False), inc=False)
            return pe.put([], lambda e: e.matmul(bank, w_lo, h_hi, start=False, stop=last), inc=inc)

        def gemm_A(w, r0, c0, nslots, rhs, bset, evac, last="i", mid=None, second=None, first=None):
            banks = [psum[4 * bset + i] for i in range(4)]
            done = [None] * 4

            def tile(sl, i, kt, first, final, waits):
                hi, lo, tk = rhs(kt)
                c = slice(i * P, (i + 1) * P)
                return mm3(banks[i].ap[:, :], sl.hi[:, kt % 4, c], sl.lo[:, kt % 4, c], hi, lo, first, final,
                           [sl.ready, tk, waits], final or (kt % 4 == 3 and i == 3))

            for s in range(nslots):
                sl = take("A", w, r0 + 512 * s, c0)
                if s == 1 and second:
                    second()
                final = s == nslots - 1
                ks = range(4 * s, 4 * s + 4)
                if final and last == "i":
                    for i in range(4):
                        for kt in ks:
                            done[i] = tile(sl, i, kt, kt == 0, kt == ks[3], banks[i].rel if kt == 0 else None)
                        if i == 3:
                            release(sl, done[3])
                        if i == 1 and mid:
                            mid()
                        evac(i, banks[i], done[i])
                else:
                    for kt in ks:
                        for i in range(4):
                            done[i] = tile(sl, i, kt, kt == 0, final and kt == ks[3], banks[i].rel if kt == 0 else None)
                        if kt == 0 and first:
                            first()
                    release(sl, done[3])
                    if final:
                        for i in range(4):
                            evac(i, banks[i], done[i])

        def gemm_B(w, c0, rhs, ring, evac):
            sl = take("B", w, 0, c0)
            for i in range(2):
                bank = ring.next()
                for kt in range(8):
                    hi, lo, tk = rhs(kt)
                    c = slice(i * P, (i + 1) * P)
                    t = mm3(bank.ap[:, :], sl.hi[:, kt, c], sl.lo[:, kt, c], hi, lo, kt == 0, kt == 7,
                            [sl.ready, tk, bank.rel if kt == 0 else None], kt == 7)
                    yield
                if i == 1:
                    release(sl, t)
                evac(i, bank, t)

        def gemm_V(w, c0, lhs, ring, evac):
            sl = take("B", w, 0, c0)
            for pair in range(2):
                bank = ring.next()
                for hf in range(2):
                    tok = slice((2 * pair + hf) * P, (2 * pair + hf + 1) * P)
                    o = bank.ap[:, 256 * hf:256 * hf + 256]
                    for kt in range(8):
                        hi, lo, tk = lhs(kt)
                        t = mm3(o, hi[:, tok], lo[:, tok], sl.hi[:, kt, :], sl.lo[:, kt, :], kt == 0, kt == 7,
                                [sl.ready, tk, bank.rel if kt == 0 and hf == 0 else None], kt == 7)
                        if kt % 2:
                            yield
                if pair == 1:
                    release(sl, t)
                evac(pair, bank, t)

        def run(gen):
            for _ in gen or ():
                pass

        def chain(*gens):
            for g in gens:
                yield from g

        def split(src, hi_ap, lo_ap, waits, hi_waits):
            hi = act.put([waits, hi_waits], lambda e: e.activation(hi_ap, src, ACT.Copy))
            lo = dve.put([waits, hi, hi_waits], lambda e: e.tensor_tensor(lo_ap, src, hi_ap.bitcast(F), ALU.subtract))
            return [hi, lo]

        col4 = cols[:, 56:64]
        root = []
        col_rel = []

        class Norm:

            spare = 7

            def __init__(self, stack, rel, layer, adder=dve):
                self.adder = adder
                self.ahead = adder is dve
                m = [Buf(sb(stack, [T], F)[:, :], rel) for _ in range(6)] if stack is not None else rel
                self.acc, self.rs, self.sq = m[0], m[1], Ring(m[2:4])
                self.tm = Ring(m[4:6])
                self.layer = layer
                if layer:
                    self.s, self.dsum = m[4], m[5]
                self.t = self.td = self.late = None

            def shift(self):
                t = pe.put([xt[0], psum[self.spare].rel, t_cst], lambda e: e.matmul(
                    psum[self.spare].ap[:, :], ones, X[0].ap, start=True, stop=True))
                t = act.put([t, self.s.rel], lambda e: e.activation(self.s.ap, psum[self.spare].ap[:, :], ACT.Copy, scale=8.0))
                psum[self.spare].rel = [t]
                for k in range(KT):
                    xt[k] = [dve.put([t, xt[k]], lambda e: e.tensor_tensor(X[k].ap, X[k].ap, self.s.ap, ALU.subtract))]
                self.sums(0)

            def add(self, k):
                if k or not self.layer:
                    self.sums(k)

            def sums(self, k):
                if k == 5:
                    root[:] = [act.put([t_col, root], lambda e: e.activation(cols[:, 4:5], rmse, ACT.Sqrt))]
                if self.layer:
                    if self.td is None:
                        self.td = pool.put([xt[k], self.dsum.rel], lambda e: e.tensor_copy(self.dsum.ap, X[k].ap))
                    else:
                        self.td = pool.put([xt[k], self.td], lambda e: e.tensor_tensor(
                            self.dsum.ap, self.dsum.ap, X[k].ap, ALU.add))
                if self.t is None:
                    self.t = act.put([xt[k], self.acc.rel], lambda e: e.activation(self.acc.ap, X[k].ap, ACT.Square))
                    return
                b = self.sq.next()
                t = act.put([xt[k], b.rel], lambda e: e.activation(b.ap, X[k].ap, ACT.Square))
                self.flush()

                def late():
                    self.t = self.adder.put([t, self.t], lambda e: e.tensor_tensor(self.acc.ap, self.acc.ap, b.ap, ALU.add))
                    b.rel = [self.t]
                self.late = late

            def flush(self):
                if self.late:
                    self.late()
                self.late = None

            def finish(self, eps):
                self.flush()
                q, d, r = psum[3], psum[7], psum[5]
                dg = self.rs
                blocks = [slice(i * P, (i + 1) * P) for i in range(4)]
                w = [self.t, self.td, q.rel, t_cst]
                for i, c in enumerate(blocks):
                    t = pe.put(w, lambda e: e.matmul(q.ap[:, i:i + 1], self.acc.ap[:, c], ones[:, 0:1], start=True, stop=True))
                if self.layer:
                    for i, c in enumerate(blocks):
                        t = pe.put([], lambda e: e.matmul(
                            q.ap[:, 4 + i:5 + i], self.dsum.ap[:, c], ones[:, 0:1], start=True, stop=True))
                    td = pe.put([d.rel], lambda e: e.matmul(d.ap[:, :], ones, self.dsum.ap, start=True, stop=True))
                    self.m_done = td
                self.acc.rel = [pe.last()]
                v = col4[:, 0:4]
                if self.layer:
                    m = col4[:, 4:8]
                    t = act.put([t, col_rel], lambda e: e.activation(m, q.ap[:, 4:8], ACT.Square))
                    t = dve.put([t], lambda e: e.tensor_tensor(v, q.ap[:, 0:4], m, ALU.subtract))
                    t = act.put([t, t_col], lambda e: e.activation(v, v, ACT.Sqrt, bias=eps))
                else:
                    t = act.put([t, t_col, col_rel], lambda e: e.activation(v, q.ap[:, 0:4], ACT.Sqrt, bias=eps))
                q.rel = [t]
                t = dve.put([t], lambda e: e.reciprocal(v, v))
                for i, c in enumerate(blocks):
                    t = dve.put([t if i == 0 else None, dg.rel, t_cst], lambda e: e.tensor_scalar(
                        dg.ap[:, c], ident, v[:, i:i + 1], float(D), ALU.mult, ALU.mult))
                    t2 = pe.put([t, r.rel], lambda e: e.matmul(r.ap[:, c], ones, dg.ap[:, c], start=True, stop=True))
                col_rel[:] = [t]
                dg.rel = [t2]
                self.rsb = r
                return [t2, self.m_done] if self.layer else [t2]

        def halves(t):
            return (t[:, 0, :, :], t[:, 1, :, :])

        HH = halves(H_t)
        Ht = [[] for _ in range(KT)]
        Hrel = [[]]

        def rhs_H(k):
            return HH[0][:, k, :], HH[1][:, k, :], Ht[k]

        cA, cB, cC, cD, cE, cF = (cols[:, 8 + 8 * i:16 + 8 * i] for i in range(6))

        def modulated(nm, k, src, waits, A, B, cw, dst, rel):
            b = nm.sq.next()
            t = act.put([waits, cw, b.rel], lambda e: e.activation(
                b.ap, src, ACT.Identity, bias=B[:, k:k + 1], scale=A[:, k:k + 1]))
            hi = act.put([t, rel], lambda e: e.activation(dst[0][:, k, :], b.ap, ACT.Copy))

            def rest(tick):
                lo = dve.put([hi, rel], lambda e: e.tensor_tensor(
                    dst[1][:, k, :], b.ap, dst[0][:, k, :].bitcast(F), ALU.subtract))
                tick[k] = b.rel = [hi, lo]
            return t, rest

        def mod8(v):
            return mods[:, 8 * v:8 * v + 8]

        def vec8(name, l=0):
            return vec[:, VCOL[name] + 8 * l:VCOL[name] + 8 * l + 8]

        def fold(A, B, w, v_shift, v_scale, g, b):
            t = dve.put([w, t_vec], lambda e: e.scalar_tensor_tensor(
                out=A, in0=mod8(v_scale), scalar=1.0, in1=g, op0=ALU.add, op1=ALU.mult))
            if b is None:
                return [t, dve.put([w], lambda e: e.tensor_copy(B, mod8(v_shift)))]
            t2 = dve.put([w, t_vec], lambda e: e.scalar_tensor_tensor(
                out=B, in0=mod8(v_scale), scalar=1.0, in1=b, op0=ALU.add, op1=ALU.mult))
            return [t, dve.put([t2], lambda e: e.tensor_tensor(B, B, mod8(v_shift), ALU.add))]

        def conv_between(k, nm):
            if k == 0 and nm.ahead and state["conv"] == state["take"] + 1 and state["conv"] in w_dma:
                conv_start(4)
            elif k > 0:
                some_conv()

        def rms_h(nm, w, A, B, t_rs=None):
            t_rs = t_rs or nm.finish(rmse)
            late = None
            for k in range(KT):
                b = nm.tm.next()
                t = dve.put([t_rs, xt[k], b.rel], lambda e: e.tensor_tensor(b.ap, X[k].ap, nm.rsb.ap[:, :], ALU.mult))
                nm.rsb.rel = [t]
                tr, rest = modulated(nm, k, b.ap, [t], A, B, w, HH, Hrel[0])
                b.rel = [tr]
                if late:
                    late(Ht)
                late = rest
                conv_between(k, nm)
            late(Ht)

        def renorm(nm, eps, hs, xA, xB, xw, x_eng=None):
            for _ in renorm_parts(nm, eps, hs, xA, xB, xw, x_eng):
                pass

        def renorm_parts(nm, eps, hs, xA, xB, xw, x_eng=None):
            t_rs = nm.finish(eps)
            reads = [[] for _ in range(KT)]
            nm.sq.bufs.append(nm.acc)
            late = None
            for n, (A, B, w, dst, tick, rel) in enumerate(hs or [(None,) * 6]):
                for k in range(KT):
                    if n == 0:
                        if nm.layer:
                            xt[k] = [dve.put([t_rs, xt[k]], lambda e: e.tensor_tensor(
                                X[k].ap, X[k].ap, psum[7].ap[:, :], ALU.subtract))]
                            psum[7].rel = xt[k]
                        xt[k] = [dve.put([t_rs, xt[k]], lambda e: e.tensor_tensor(
                            X[k].ap, X[k].ap, nm.rsb.ap[:, :], ALU.mult))]
                        nm.rsb.rel = xt[k]
                    if A is not None:
                        tr, rest = modulated(nm, k, X[k].ap, xt[k], A, B, w, dst, rel)
                        reads[k].append(tr)
                        if late:
                            late[0](late[1])
                        late = (rest, tick)
                    if n == 0:
                        conv_between(k, nm)
                    if n == max(1, len(hs)) - 1:
                        if x_eng is None:
                            xt[k] = [pool.put([xt[k], reads[k], xw], lambda e: e.tensor_scalar(
                                X[k].ap, X[k].ap, xA[:, k:k + 1], xB[:, k:k + 1], ALU.mult, ALU.add))]
                        else:
                            xt[k] = [act.put([xt[k], reads[k], xw], lambda e: e.activation(
                                X[k].ap, X[k].ap, ACT.Identity, bias=xB[:, k:k + 1], scale=xA[:, k:k + 1]))]
                if late:
                    late[0](late[1])
                    late = None
                yield

        def scaled(dst, src, f):
            return dve.put([t_vec], lambda e: e.tensor_scalar(dst, src, f, None, ALU.mult))

        def residual(k, bank, tk, gate, w, nm=None):
            xt[k] = [dve.put([tk, xt[k], w], lambda e: e.scalar_tensor_tensor(
                out=X[k].ap, in0=bank.ap[:, :], scalar=gate, in1=X[k].ap, op0=ALU.mult, op1=ALU.add))]
            bank.rel = xt[k]
            if nm is not None:
                nm.add(k)

        S_ring = Ring([psum[0], psum[1]])
        T_ring = Ring([psum[2], psum[3]])
        O_ring = Ring([psum[4], psum[5]])
        G_ring = Ring([psum[6], psum[7]])
        OFF = {"causal": [0, 128, 384, 768], "swa": [0, 128, 384, 640]}

        class Head:
            pass

        def scores(h, ab):
            off = OFF[h.kind]
            st = ab.stats.next()
            sp_ = ab.sp.next()
            h.st, h.sp = st, sp_
            mx, nm, sm, es = (st.ap[:, q, :] for q in (0, 1, 2, 3))
            h.exp = [None] * 4
            nms = []
            for i in range(4):
                k0 = 0 if h.kind == "causal" else max(0, i - 1) * P
                n = (i + 1) * P - k0
                N = max(256, n)
                bank = S_ring.next()
                o = bank.ap[:, 0:N]
                tok = slice(i * P, (i + 1) * P)
                assert None not in h.k_ready()
                w = [h.q_ready(), h.k_ready(), bank.rel]
                kr = slice(k0, k0 + N)
                pairs = [(h.q[0][:, tok], h.k[0][:, kr]), (h.q[1][:, tok], h.k[0][:, kr]),
                         (h.q[0][:, tok], h.k[1][:, kr])]
                if h.extra:
                    pairs.append((h.extra[0][:, tok], h.extra[1][:, kr]))
                    w.append(h.extra[2])
                for m, (lt, rr) in enumerate(pairs):
                    tk = pe.put(w if m == 0 else [], lambda e, lt=lt, rr=rr, m=m: e.matmul(
                        o, lt, rr, start=m == 0, stop=m == len(pairs) - 1), inc=m == len(pairs) - 1)
                h.s_done = tk
                piece = sp_.ap[:, off[i]:off[i] + n]
                bias = h.bias(i)
                t = dve.put([tk, h.bias_ready, sp_.rel, st.rel], lambda e: e.tensor_tensor_reduce(
                    out=piece, in0=bank.ap[:, 0:n], in1=bias, scale=1.0, scalar=LOW, op0=ALU.add, op1=ALU.max,
                    accum_out=mx[:, i:i + 1]))
                bank.rel = [t]
                h.bias_done = t
                top = h.sink if h.sink is not None else LOW
                t = dve.put([t, t_sink], lambda e: e.tensor_scalar(
                    nm[:, i:i + 1], mx[:, i:i + 1], top, -1.0, ALU.max, ALU.mult))
                nms.append(t)
                h.exp[i] = act.put([t], lambda e: e.activation(
                    piece, piece, ACT.Exp, bias=nm[:, i:i + 1], accum_out=sm[:, i:i + 1]))
                if i == 3 and h.sink is not None:
                    h.es = act.put([nms, st.rel], lambda e: e.activation(es, nm, ACT.Exp, bias=h.sink))
                yield

        def normalise(h, ab):
            off = OFF[h.kind]
            st, sp_ = h.st, h.sp
            sm, es, rs = (st.ap[:, q, :] for q in (2, 3, 4))
            t = None
            if h.sink is not None:
                t = dve.put([h.exp, h.es], lambda e: e.tensor_tensor(sm, sm, es, ALU.add))
            t = dve.put([h.exp, t, st.rel], lambda e: e.reciprocal(rs, sm))
            h.norm = [None] * 4
            for i in (0, 1, 2, 3):
                n = ((i + 1) if h.kind == "causal" else min(2, i + 1)) * P
                piece = sp_.ap[:, off[i]:off[i] + n]
                if i == 3:
                    h.norm[i] = act.put([t, h.exp[i]], lambda e: e.activation(
                        piece, piece, ACT.Copy, scale=rs[:, i:i + 1]))
                else:
                    h.norm[i] = dve.put([t, h.exp[i]], lambda e: e.tensor_scalar(
                        piece, piece, rs[:, i:i + 1], 1.0, ALU.mult, ALU.mult))
            st.rel = h.norm

        def weighted(h, ab, steps):
            off = OFF[h.kind]
            sp_ = h.sp
            if h.kind == "causal":
                groups = [[0], [1], [2], [3]]
                blocks = {j: list(range(j, 4)) for j in range(4)}
                base = [0, 512, 896, 1152]
                need = {0: 0, 1: 1, 2: 2, 3: 3}
            else:
                groups = [[0, 1], [2, 3]]
                blocks = {0: [0, 1], 1: [1, 2], 2: [2, 3], 3: [3]}
                base = [0, 256, 512, 768]
                need = {0: 0, 1: 0, 2: 1, 3: 1}
            for step in steps:
                if step[0] == "t":
                    g = groups[int(step[1])]
                    tb = T_ring.next()
                    pos = 0
                    tk = None
                    for j in g:
                        for i in blocks[j]:
                            col = off[i] + (j * P if h.kind == "causal" else (j - max(0, i - 1)) * P)
                            tk = pe.put([h.norm[i], tb.rel if pos == 0 else None], lambda e, pos=pos, col=col: e.transpose(
                                tb.ap[:, pos:pos + P], sp_.ap[:, col:col + P], ident), inc=True)
                            pos += P
                    b0 = base[g[0]]
                    hi_ap, lo_ap = ab.pt[0][:, b0:b0 + pos], ab.pt[1][:, b0:b0 + pos]
                    tb.rel = split(tb.ap[:, 0:pos], hi_ap, lo_ap, [tk], ab.pt_rel[int(step[1])])
                    h.pt_ready[int(step[1])] = tb.rel
                    if g is groups[-1]:
                        sp_.rel = [tk]
                else:
                    j = int(step[1])
                    if j == 0:
                        h.bank = O_ring.next()
                    bank = h.bank
                    n = len(blocks[j]) * P
                    o = bank.ap[:, j * P:j * P + n]
                    ph, pl = ab.pt[0][:, base[j]:base[j] + n], ab.pt[1][:, base[j]:base[j] + n]
                    vh, vl = h.v[0](j), h.v[1](j)
                    assert None not in h.v_ready()
                    firstw = [bank.rel if j == 0 else None, h.v_ready(), h.pt_ready[need[j]]]
                    pe.put(firstw, lambda e, o=o, vh=vh, ph=ph, j=j: e.matmul(
                        o, vh, ph, start=j == 0, stop=False, skip_group_check=True), inc=False)
                    pe.put([], lambda e, o=o, vh=vh, pl=pl: e.matmul(
                        o, vh, pl, start=False, stop=False, skip_group_check=True), inc=False)
                    tk = pe.put([], lambda e, o=o, vl=vl, ph=ph, j=j: e.matmul(
                        o, vl, ph, start=False, stop=j == 3, skip_group_check=True))
                    ab.pt_rel[need[j]] = [tk]
                    if j == 3:
                        r = slice(h.r0, h.r0 + 64)
                        h.out_ready = split(bank.ap[r, :], h.o[0][r, :], h.o[1][r, :], [tk], [h.s_done])
                        bank.rel = h.out_ready
                        h.done = tk
                        h.after()

        SEQ = {"causal": ["v0", "t2", "v1", "t3", "+t0", "v2", "+t1", "v3"],
               "swa": ["v0", "v1", "+t0", "v2", "v3", "+t1"]}
        LEAD = {"causal": [8, 8, 8, 9, 10, 11, 12, 12], "swa": [10, 11, 12, 12, 12, 13]}
        NORM = {"causal": 1, "swa": 0}

        def attend(heads, ab, gemm, quota):
            def fill(n):
                for _ in range(n):
                    next(gemm, None)
                    some_conv()

            def score_stream():
                for h in heads:
                    yield from scores(h, ab)

            stream = score_stream()
            count = [0, 0]

            def start(n):
                while count[0] < min(n, len(heads)):
                    heads[count[0]].start()
                    count[0] += 1

            def tiles(n):
                while count[1] < min(n, 4 * len(heads)):
                    next(stream)
                    count[1] += 1
                    start(count[1] // 4 + 2)

            gentle[0] = True
            start(2)
            for n in range(8):
                tiles(n + 1)
                fill(1)
            normalise(heads[0], ab)
            fill(1)
            for step in ("t0", "t1"):
                weighted(heads[0], ab, [step])
                fill(1)
            for n, h in enumerate(heads):
                nxt = heads[n + 1] if n + 1 < len(heads) else None
                seq = SEQ[h.kind]
                extra = max(0, quota[n] - len(seq))
                for at, step in enumerate(seq):
                    if at == NORM[h.kind] and nxt:
                        normalise(nxt, ab)
                    if step[0] != "+":
                        weighted(h, ab, [step])
                    elif nxt:
                        weighted(nxt, ab, [step[1:]])
                    lead = LEAD[h.kind][at]
                    tiles(4 * n + (lead if nxt and nxt.kind == h.kind else min(lead, 12)))
                    fill(2 if at < extra else (1 if at < quota[n] else 0))
            run(gemm)
            gentle[0] = False

        class AttnBufs:
            pass

        ada_jobs("ada_t", 0, 2048, 0, 0)
        ph = ExitStack()
        ada_memory(ph, 3, [])
        nm = Norm(ph, [], False, pool)
        silu_c(t_cb)
        ada_load()
        load_x([])
        tb33 = sb(ph, [16], F)
        hot = sb(ph, [1024], F)
        rrow = sb(ph, [1024], F)
        d_t, d_r = dsem(), dsem()
        t_tab = pool_dma(d_t, [], tb33[0:32, :], a["rel_bias"])
        t_tab = pool_dma(d_t, [], hot[0:33, :], a["hot"])
        t_m = dve.put([], lambda e: e.memset(tb33[32:33, :], NEG))
        tr = []
        for i, (c0, n) in enumerate(((0, 512), (512, 128), (640, 384))):
            t = pe.put([t_tab, t_m], lambda e: e.matmul(
                psum[i].ap[0:16, 0:n], tb33[0:33, :], hot[0:33, c0:c0 + n], start=True, stop=True))
            t = act.put([t], lambda e: e.activation(rrow[0:16, c0:c0 + n], psum[i].ap[0:16, 0:n], ACT.Copy))
            psum[i].rel = [t]
            tr.append(t)
        skew = scratch["skew"][0:1, 0:1]

        for k in range(KT):
            nm.add(k)
        t_rs = None
        for i in range(6):
            ada_step(1)
            ada_load()
            if i == 3:
                slot_dma()
            if i == 5:
                t_rs = nm.finish(rmse)
        t_mod = mod_bias(0, 16, VCOL["ada_b"])
        ready_for(0)
        slot_dma()
        for h0, c0, n in ((0, 640, 384), (8, 0, 640)):
            src = rrow[h0:h0 + 8, c0:c0 + n].unsqueeze(1).broadcast_to([8, P, n])
            dst = bass.AP(tensor=skew.tensor, offset=h0 * SKEW, ap=[[SKEW, 8], [n + 1, P], [1, n]])
            t_bias = dma(d_r, tr, dst, src)
        stores.append(t_bias)
        rms_h(nm, [fold(cA, cB, t_mod, 0, 1, vec8("norm1_g"), None)], cA, cB, t_rs)
        ada_end()
        x_free = [Ht[k] for k in range(KT)] + [nm.rsb.rel]
        rel1 = barrier()
        ph.close()

        outer = ExitStack()
        Qa = sb(outer, [2, 4, T], R)
        Qb = sb(outer, [2, 4, T], R)
        sg_r = Ring([Buf(sb(outer, [T], F)[:, :], rel1) for _ in range(4)])
        ph = ExitStack()
        KV = [Buf(sb(ph, [6144], R), rel1) for _ in range(2)]
        pt_t = sb(ph, [2, 1280], R)

        def k_view(b):
            return b.ap[:, 0:4096].rearrange("p (s h n) -> p s h n", s=2, h=4)

        def v_view(b):
            return b.ap[:, 4096:6144].rearrange("p (s t n) -> p s t n", s=2, t=4)

        def zero_halves(b, rel, eng=pool):
            tks = []
            kv = k_view(b)
            for s in range(2):
                for odd in range(2):
                    r = slice(0, 64) if odd else slice(64, 128)
                    v = kv[r, s, odd::2, :].bitcast(F)
                    tks.append(eng.put(rel, lambda e, v=v: e.memset(v, 0.0)))
            return tks

        def attn_bufs(rel, pt):
            ab = AttnBufs()
            xf = x_t[:, :, :].rearrange("p k n -> p (k n)")
            ab.sp = Ring([Buf(xf[:, 0:1280], rel), Buf(xf[:, 1280:2560], rel)])
            ab.bias = Ring([Buf(xf[:, 2560:3072], rel), Buf(xf[:, 3072:3584], rel)])
            ab.stats = Ring([Buf(stat[:, 0, :, :], rel), Buf(stat[:, 1, :, :], rel)])
            ab.pt = (pt[:, 0, :], pt[:, 1, :])
            ab.pt_rel = [list(rel) for _ in range(4)]
            return ab

        ab = attn_bufs(rel1, pt_t)
        d_b = [dsem(), dsem()]
        nbias = [0]
        zeroed = [zero_halves(KV[i], rel1) for i in range(2)]

        def evac_q(dst, ready, t0, rel):
            def f(i, bank, tk):
                hi_ap, lo_ap = dst[:, 0, t0 + i, :], dst[:, 1, t0 + i, :]
                hi = act.put([tk, rel], lambda e: e.activation(hi_ap, bank.ap[:, :], ACT.Copy, scale=QSCALE))
                lo = dve.put([hi], lambda e: e.scalar_tensor_tensor(
                    out=lo_ap, in0=bank.ap[:, :], scalar=QSCALE, in1=hi_ap.bitcast(F), op0=ALU.mult, op1=ALU.subtract))
                bank.rel = [hi, lo]
                ready[t0 + i] = [hi, lo]
            return f

        def evac_k(b, ready):
            def f(i, bank, tk):
                kv = k_view(b)
                for odd in range(2):
                    r = slice(64 * odd, 64 * odd + 64)
                    n = 2 * i + odd
                    ready[n] = split(bank.ap[r, :], kv[r, 0, n, :], kv[r, 1, n, :], [tk], b.rel)
                bank.rel = [ready[2 * i], ready[2 * i + 1]]
            return f

        def evac_v(b, ready):
            def f(pair, bank, tk):
                vv = v_view(b)
                src = bank.ap[:, :].rearrange("p (t n) -> p t n", t=2)
                ready[pair] = split(src, vv[:, 0, 2 * pair:2 * pair + 2, :], vv[:, 1, 2 * pair:2 * pair + 2, :], [tk], b.rel)
                bank.rel = ready[pair]
            return f

        def group_heads(kv, zero, q, q_ready, k_ready, v_ready, t0, make):
            kk, vv = k_view(kv), v_view(kv)
            hs = []
            for n in range(4):
                h = Head()
                h.kind, h.sink, h.extra, h.pt_ready, h.after = "causal", None, None, {}, lambda: None
                p = t0 + n // 2
                h.q = (q[:, 0, p, :], q[:, 1, p, :])
                h.q_ready = lambda p=p: q_ready[p]
                h.k = (kk[:, 0, n, :], kk[:, 1, n, :])
                h.k_ready = lambda n=n: [k_ready[n], zero]
                c = slice((n // 2) * P, (n // 2 + 1) * P)
                h.v = (lambda j, c=c: vv[:, 0, j, c], lambda j, c=c: vv[:, 1, j, c])
                h.v_ready = lambda: [v_ready[0], v_ready[1]]
                h.r0 = 64 * (n % 2)
                h.o = h.q
                make(h, n)
                hs.append(h)
            return hs

        def bias_loader(h, table, n):
            def start():
                b = ab.bias.next()
                i = nbias[0] % 2
                nbias[0] += 1
                pitch = 384 if n == 256 else 640
                src = bass.AP(tensor=skew.tensor, offset=table * SKEW + P - 1, ap=[[pitch, P], [1, n]])
                h.bias_ready = pool_dma(d_b[i], [b.rel, t_bias, x_free], b.ap[:, 0:n], src)
                if n == 256:
                    h.bias = lambda q: b.ap[:, 128 if q == 0 else 0:256]
                else:
                    h.bias = lambda q: b.ap[:, 128 * (3 - q):512]
                h.bias_buf = b
            return start

        qa_ready, qb_ready = [None] * 4, [None] * 4
        for c in range(2):
            run(gemm_B("w_in", 256 * c, rhs_H, G_ring, evac_q(Qa, qa_ready, 2 * c, rel1)))
        ka_ready, va_ready = {}, {}
        vt = Buf(x_t[:, 7, :], [x_free])

        def evac_kva(i, bank, tk):
            if i == 0:
                evac_k(KV[0], ka_ready)(0, bank, tk)
                return
            t = act.put([tk, vt.rel], lambda e: e.activation(vt.ap, bank.ap[:, :], ACT.Copy))
            bank.rel = [t]
            tb = T_ring.next()
            for j in range(4):
                tk = pe.put([t, tb.rel, t_cst], lambda e, j=j: e.transpose(
                    tb.ap[:, j * P:(j + 1) * P], vt.ap[:, j * P:(j + 1) * P], ident))
            vv = v_view(KV[0])
            src = tb.ap[:, :].rearrange("p (t n) -> p t n", t=4)
            va_ready[0] = split(src, vv[:, 0, :, 0:P], vv[:, 1, :, 0:P], [tk], KV[0].rel)
            tb.rel = va_ready[0]

        run(gemm_B("w_in", 512, rhs_H, G_ring, evac_kva))

        swa = []
        for n in range(8):
            t_, g = n % 4, n // 4
            h = Head()
            h.kind, h.extra, h.pt_ready, h.after = "swa", None, {}, lambda: None
            hd = t_ + 4 * g
            h.sink = small[:, hd:hd + 1]
            h.q = (Qa[:, 0, t_, :], Qa[:, 1, t_, :])
            h.q_ready = lambda t_=t_: qa_ready[t_]
            kk, vv = k_view(KV[0]), v_view(KV[0])
            h.k = (kk[:, 0, g, :], kk[:, 1, g, :])
            h.k_ready = lambda g=g: [ka_ready[g], zeroed[0]]
            h.v = (lambda j: v_view(KV[0])[:, 0, j, 0:P], lambda j: v_view(KV[0])[:, 1, j, 0:P])
            h.v_ready = lambda: va_ready[0]
            h.r0 = 64 * g
            h.o = h.q
            h.start = bias_loader(h, hd, 256)
            swa.append(h)
        kb_ready = [{k: None for k in range(4)} for _ in range(2)]
        vb_ready = [{k: None for k in range(2)} for _ in range(2)]

        def free_kv(kv, h):
            def after():
                kv.rel = [h.done]
            h.after = after

        def kv_gemm(g, wk, ck, wv, cv, rhs, buf):
            return chain(gemm_B(wk, ck, rhs, G_ring, evac_k(buf, kb_ready[g % 2])),
                         gemm_V(wv, cv, rhs, G_ring, evac_v(buf, vb_ready[g % 2])))

        def release_bias(h):
            h.bias_buf.rel = [h.bias_done]

        def wrap(hs):
            for n, h in enumerate(hs):
                s0 = h.start

                def start(h=h, s0=s0, n=n):
                    if n >= 2:
                        release_bias(hs[n - 2])
                    s0()
                h.start = start
            return hs

        free_kv(KV[0], swa[7])
        first_gate = [None] * 4

        def evac_gate(i0):
            def f(i, bank, tk):
                b = sg_r.next()
                t = act.put([tk, b.rel], lambda e: e.activation(b.ap, bank.ap[:, :], ACT.Copy))
                bank.rel = [t]
                first_gate[i0 + i] = (b, t)
            return f

        moba = []
        for g in range(2):
            kv = KV[(g + 1) % 2]

            def make(h, n, g=g):
                h.start = bias_loader(h, 8 + 4 * g + n, 512)

            moba += group_heads(kv, zeroed[(g + 1) % 2], Qb, qb_ready, kb_ready[(g + 1) % 2],
                                vb_ready[(g + 1) % 2], 2 * g, make)
        free_kv(KV[1], moba[3])
        attend(wrap(swa + moba), ab, chain(
            gemm_B("w_in", 768, rhs_H, G_ring, evac_q(Qb, qb_ready, 0, rel1)),
            gemm_B("w_in", 1024, rhs_H, G_ring, evac_q(Qb, qb_ready, 2, rel1)),
            kv_gemm(1, "w_in", 1280, "w_in", 1792, rhs_H, KV[1]),
            kv_gemm(0, "w_in", 1536, "w_in", 2048, rhs_H, KV[0]),
            gemm_B("w_in", 2304, rhs_H, G_ring, evac_gate(0)),
            gemm_B("w_in", 2560, rhs_H, G_ring, evac_gate(2))), [8] * 16)
        oa_ready = [[swa[t_].out_ready, swa[t_ + 4].out_ready] for t_ in range(4)]
        ob_ready = [[moba[2 * t_].out_ready, moba[2 * t_ + 1].out_ready] for t_ in range(4)]

        rel2 = barrier()
        ph.close()
        ph = ExitStack()
        MG = sb(ph, [2, KT, T], R)
        m_r = Ring([Buf(sb(ph, [T], F)[:, :], rel2) for _ in range(4)])
        y_r = Ring([Buf(sb(ph, [T], F)[:, :], rel2) for _ in range(2)])
        t_wf = pool_dma(dsem(), [], wfr[:, :].rearrange("p (k n) -> p k n", k=8), a["w_f_2"].rearrange("(k p) n -> p k n", p=P))
        ada_queue[0] = pool_dma
        ada_memory(ph, 2, rel2)
        ada_rate[0] = 1.25
        ada_jobs("ada_t", 2048, 4096, 16, 0)
        ada_jobs("ada2_0", 0, 6144, 48, 1)
        ada_jobs("adakv_t", 0, 2048, 144, 1)
        ada_jobs("ada2_1", 0, 6144, 96, 1)
        load_x(rel2)
        MGt = [None] * KT

        def rhs_of(t, ready):
            return lambda k: (t[:, 0, k, :], t[:, 1, k, :], ready[k])

        for hf in range(2):
            sgs, ms, parts = [None] * 4, [None] * 4, []

            def evac_sig(i, bank, tk):
                b = sg_r.next()
                t = act.put([tk, b.rel], lambda e: e.activation(b.ap, bank.ap[:, :], ACT.Sigmoid))
                bank.rel = [t]
                sgs[i] = (b, t)

            def evac_ya(i, bank, tk):
                b, t = sgs[i]
                m = m_r.next()
                t = dve.put([tk, t, m.rel], lambda e: e.tensor_tensor(m.ap, bank.ap[:, :], b.ap, ALU.mult))
                bank.rel = [t]
                b.rel = [t]
                ms[i] = (m, t)

            def evac_yb(i, bank, tk):
                b, t = sgs[i]
                y = y_r.next()
                m, tm_ = ms[i]
                t = dve.put([tk, t, y.rel], lambda e: e.tensor_tensor(y.ap, bank.ap[:, :], b.ap, ALU.mult))
                bank.rel = [t]
                b.rel = [t]
                t = pool.put([t, tm_], lambda e: e.tensor_tensor(m.ap, m.ap, y.ap, ALU.add))
                y.rel = [t]
                k = 4 * hf + i
                while parts:
                    parts.pop()()

                def halves():
                    MGt[k] = split(m.ap, MG[:, 0, k, :], MG[:, 1, k, :], [t], rel2)
                    m.rel = MGt[k]
                parts.append(halves)

            if hf:
                gemm_A("w_in", 0, 2304 + 512 * hf, 2, rhs_H, 0, evac_sig)
            else:
                for i, (b, t) in enumerate(first_gate):
                    sgs[i] = (b, act.put([t], lambda e: e.activation(b.ap, b.ap, ACT.Sigmoid)))
            gemm_A("w_branch_a", 0, 512 * hf, 1, rhs_of(Qa, oa_ready), 1, evac_ya)
            gemm_A("w_in", 0, 3328 + 512 * hf, 2, rhs_H, 0, evac_sig)
            gemm_A("w_branch_b", 0, 512 * hf, 1, rhs_of(Qb, ob_ready), 1, evac_yb)
            parts.pop()()
        Hrel[0] = [pe.last()]
        t_g1 = mod_bias(16, 8, VCOL["ada_b"] + 16)
        nm = Norm(None, sg_r.bufs + y_r.bufs, False)
        for hf in range(2):
            ada_hold[0] = True
            if hf:
                t_mod = mod_bias(24, 16, VCOL["ada_b"] + 24)
                w2 = fold(cA, cB, t_mod, 3, 4, vec8("norm2_g"), None)
            gemm_A("w_out", 0, 512 * hf, 2, rhs_of(MG, MGt), hf, lambda i, bank, tk, hf=hf: residual(
                4 * hf + i, bank, tk, mcol(2, 4 * hf + i), t_g1, nm), "k" if hf == 0 else "i")
        rms_h(nm, [w2], cA, cB)
        ada_end()
        rel3 = barrier()
        ph.close()
        outer.close()

        ph = ExitStack()
        ada_queue[0] = dma
        ada_memory(ph, 3, rel3)
        nm = Norm(ph, rel3, False)
        ada_rate[0] = 1.25
        AC = [sb(ph, [2, 4, T], R) for _ in range(2)]
        f_r = Ring([Buf(sb(ph, [T], F)[:, :], rel3) for _ in range(4)])
        ac_rel = [rel3, rel3]

        def mlp_in(f):
            act_t = AC[f % 2]
            ready = [None] * 4

            def evac(i, bank, tk):
                b = f_r.next()
                t = act.put([tk, b.rel], lambda e: e.activation(b.ap, bank.ap[:, :], ACT.Relu))
                bank.rel = [t]
                t = pool.put([t], lambda e: e.tensor_tensor(b.ap, b.ap, b.ap, ALU.mult))
                ready[i] = split(b.ap, act_t[:, 0, i, :], act_t[:, 1, i, :], [t], ac_rel[f % 2])
                b.rel = ready[i]
            gemm_A("w_mlp_in", 0, 512 * f, 2, rhs_H, 0, evac)
            return rhs_of(act_t, ready)

        def mods2(l, part, n):
            return mod_bias(48 + 48 * l + part, n, VCOL["b_ada_2"] + 48 * l + part)

        V0 = 6
        for f in range(FF1 // 512):
            r = mlp_in(f)
            end = f == FF1 // 512 - 1
            if f == 0:
                t_mod = mod_bias(40, 8, VCOL["ada_b"] + 40)
            if f == FF1 // 512 - 2:
                ada_hold[0] = True
            if end:
                t_m2 = mods2(0, 0, 48)
                wx = scaled(cC, vec8("final_g"), ALPHA)
                w2 = fold(cE, cF, t_m2, V0, V0 + 1, vec8("final_g"), None)
                wz = dve.put([], lambda e: e.memset(cD, 0.0))
            for hf in range(2):
                gemm_A("w_mlp_out", 512 * f, 512 * hf, 1, r, hf if end else 1 - hf, lambda i, bank, tk, hf=hf: residual(
                    4 * hf + i, bank, tk, mcol(5, 4 * hf + i), t_mod, nm if end else None), "i" if hf else "k")
            ac_rel[f % 2] = [pe.last()]
        Hrel[0] = [pe.last()]


        renorm(nm, rmse, [(cE, cF, w2, HH, Ht, Hrel[0])], cC, cD, [wx, wz])
        ada_end()
        rel4 = barrier()
        ph.close()

        ph = ExitStack()
        ada_memory(ph, 3, rel4)
        nm = Norm(ph, rel4, True)
        ada_rate[0] = 0.6
        YC = sb(ph, [2, KT, T], R)
        g_r = Ring([Buf(sb(ph, [T], F)[:, :], rel4) for _ in range(4)])
        u_r = Ring([Buf(sb(ph, [T + 2], F)[:, :], rel4) for _ in range(2)])
        c_r = Ring([Buf(sb(ph, [T], F)[:, :], rel4) for _ in range(4)])
        for b in u_r.bufs:
            b.rel = [pool.put([rel4], lambda e, b=b: e.memset(b.ap[:, 0:2], 0.0))]
        YCt = [None] * KT
        for hf in range(2):
            gs, cs = [None] * 4, [None] * 4

            def evac_gc(i, bank, tk):
                b = g_r.next()
                t = act.put([tk, b.rel], lambda e: e.activation(b.ap, bank.ap[:, :], ACT.Copy))
                bank.rel = [t]
                gs[i] = (b, t)

            def evac_v2(i, bank, tk):
                k = 4 * hf + i
                b, t = gs[i]
                u, c = u_r.next(), c_r.next()
                t = dve.put([tk, t, u.rel], lambda e: e.tensor_tensor(u.ap[:, 2:T + 2], bank.ap[:, :], b.ap, ALU.mult))
                bank.rel = [t]
                b.rel = [t]
                cw = [vec[:, VCOL["conv_w_2"] + 8 * j + k:VCOL["conv_w_2"] + 8 * j + k + 1] for j in range(3)]
                t = dve.put([t, c.rel, t_vec], lambda e: e.tensor_scalar(c.ap, u.ap[:, 0:T], cw[0], None, ALU.mult))
                for j in (1, 2):
                    t = dve.put([t], lambda e, j=j: e.scalar_tensor_tensor(
                        out=c.ap, in0=u.ap[:, j:T + j], scalar=cw[j], in1=c.ap, op0=ALU.mult, op1=ALU.add))
                u.rel = [t]
                cs[i] = (c, t)

            def evac_gb(i, bank, tk):
                k = 4 * hf + i
                c, t = cs[i]
                t = dve.put([tk, t], lambda e: e.tensor_tensor(c.ap, bank.ap[:, :], c.ap, ALU.mult))
                bank.rel = [t]
                YCt[k] = split(c.ap, YC[:, 0, k, :], YC[:, 1, k, :], [t], rel4)
                c.rel = YCt[k]

            gemm_A("conv_w_in_2", 0, 1024 + 512 * hf, 2, rhs_H, hf, evac_gc)
            gemm_A("conv_w_in_2", 0, 2048 + 512 * hf, 2, rhs_H, 1 - hf, evac_v2)
            ada_hold[0] = hf == 1
            gemm_A("conv_w_in_2", 0, 512 * hf, 2, rhs_H, hf, evac_gb)
        Hrel[0] = [pe.last()]
        def ln1_cols(l, t_m):
            V = 6 + 6 * l
            return [fold(cA, cB, t_m, V + 3, V + 4, vec8("ln1_g_2", l), vec8("ln1_b_2", l)),
                    [scaled(cC, vec8("ln1_g_2", l), ALPHA), scaled(cD, vec8("ln1_b_2", l), ALPHA)]]

        w_ln1 = ln1_cols(0, t_m2)
        for hf in range(2):
            gemm_A("conv_w_out_2", 0, 512 * hf, 2, rhs_of(YC, YCt), hf, lambda i, bank, tk, hf=hf: residual(
                4 * hf + i, bank, tk, mcol(V0 + 2, 4 * hf + i), t_m2, nm), mid=None if hf else nm.shift)

        def ln1_h(nm, w):
            renorm(nm, lne, [(cA, cB, w[0], HH, Ht, Hrel[0])], cC, cD, w[1])

        ln1_h(nm, w_ln1)
        ada_end()
        rel5 = barrier()
        ph.close()

        def nothing():
            pass

        def ffn2(l, t_m, before, nm, AC, rel, rings, n):
            V = 6 + 6 * l
            g_r = Ring([Buf(sb(rings, [T], F)[:, :], rel) for _ in range(4)])
            f_r = Ring([Buf(sb(rings, [T], F)[:, :], rel) for _ in range(n)] or nm.sq.bufs)
            ac_rel = [rel, rel]

            def evacs(f):
                act_t = AC[f % 2]
                ready = [None] * 4
                gs = [None] * 4

                def evac_g(i, bank, tk):
                    b = g_r.next()
                    t = act.put([tk, b.rel], lambda e: e.activation(b.ap, bank.ap[:, :], ACT.Silu))
                    bank.rel = [t]
                    gs[i] = (b, t)

                def evac_u(i, bank, tk):
                    g, t = gs[i]
                    b = f_r.next()
                    t = dve.put([tk, t, b.rel], lambda e: e.tensor_tensor(b.ap, bank.ap[:, :], g.ap, ALU.mult))
                    bank.rel = [t]
                    g.rel = [t]
                    ready[i] = split(b.ap, act_t[:, 0, i, :], act_t[:, 1, i, :], [t], ac_rel[f % 2])
                    b.rel = ready[i]

                return evac_g, evac_u, rhs_of(act_t, ready)

            def res(hf, nm):
                return lambda i, bank, tk: residual(4 * hf + i, bank, tk, mcol(V + 5, 4 * hf + i), t_m, nm)

            def narrow(f):
                eg, eu, r = evacs(f)
                run(gemm_B(f"gate{l}", 2560, rhs_H, Ring(psum[0:2]), eg))
                run(gemm_B(f"up{l}", 2560, rhs_H, Ring(psum[2:4]), eu))
                sl = take("C", f"down{l}", 2560, 0)
                order = [4, 5, 6, 7, 0, 1, 2, 3]
                tks = [None] * 8
                for kt in range(2):
                    hi, lo, tk = r(kt)
                    for i in range(8):
                        bank = psum[order[i]]
                        c = slice(i * P, (i + 1) * P)
                        tks[i] = mm3(bank.ap[:, :], sl.hi[:, kt, c], sl.lo[:, kt, c], hi, lo, kt == 0, kt == 1,
                                     [sl.ready, tk, bank.rel if kt == 0 else None], kt == 1)
                release(sl, tks[7])
                for i in range(8):
                    residual(i, psum[order[i]], tks[i], mcol(V + 5, i), t_m)
                ac_rel[f % 2] = [pe.last()]

            for f in range(5):
                if f == 4:
                    narrow(4)
                    before()
                n = f + (f == 4)
                eg, eu, r = evacs(n)
                gemm_A(f"gate{l}", 0, 512 * f, 2, rhs_H, 0, eg)
                gemm_A(f"up{l}", 0, 512 * f, 2, rhs_H, 1, eu)
                for hf in range(2):
                    gemm_A(f"down{l}", 512 * f, 512 * hf, 1, r, hf, res(hf, nm if f == 4 else None),
                           "i" if hf or f == 4 else "k", nm.shift if f == 4 and not hf else None)
                ac_rel[n % 2] = [pe.last()]
            Hrel[0] = [pe.last()]

        ph = ExitStack()
        before_q = ExitStack()
        q2_room = sb(before_q, [2 * KT * T], F)
        inner = ExitStack()
        KVt = sb(inner, [12288], R)
        top = ExitStack()
        nm = Norm(top, rel5, True)
        AC = [KVt[:, 4096 * i:4096 * (i + 1)].rearrange("p (s k n) -> p s k n", s=2, k=4) for i in range(2)]
        V1 = 12
        g2, b2 = vec8("ln2_g_2"), vec8("ln2_b_2")
        w_fox = []

        def fox_cols():
            t_kv = mod_bias(144, 16, VCOL["b_ada_kv_2"])
            t_m3 = mods2(1, 0, 48)
            w_fox.extend([fold(cA, cB, t_m3, V1, V1 + 1, g2, b2), fold(cC, cD, t_kv, 18, 19, g2, b2),
                          [scaled(cE, g2, ALPHA), scaled(cF, b2, ALPHA)], t_m3])

        wfh, wfl = KVt[:, 8192:8320], KVt[:, 8320:8448]
        tw = split(wfr[:, :], wfh, wfl, [t_wf], rel5)
        ada_memory(None, [q2_room[:, 2048 * i:2048 * (i + 1)] for i in range(3)], rel5)
        ada_rate[0] = 0.9
        ffn2(0, t_m2, fox_cols, nm, AC, rel5, top, 0)

        for st in (top, inner, before_q):
            st.close()
        Q2 = sb(ph, [2, KT, T], R)
        inner = ExitStack()
        KVt = sb(inner, [12288], R)
        t_m3 = w_fox[3]
        hq = KVt[:, 0:8192].rearrange("p (s k n) -> p s k n", s=2, k=KT)
        hq = (hq[:, 0, :, :], hq[:, 1, :, :])
        hqt = [None] * KT
        ada_end()
        rel6 = [pe.last(), dve.last()]
        parts = renorm_parts(nm, lne, [(cA, cB, w_fox[0], hq, hqt, rel6), (cC, cD, w_fox[1], HH, Ht, Hrel[0])],
                             cE, cF, w_fox[2])
        next(parts)
        d_sx = dsem()
        relx = []

        def kv_norm():
            run(parts)
            relx.append(dma(d_sx, [xt[k] for k in range(KT)], scratch["x"][:, :].rearrange("(kt p) n -> p kt n", p=P),
                            x_t[:, :, :]))
            stores.append(relx[0])

        q_ready = [None] * KT
        xf = x_t[:, :, :].rearrange("p k n -> p (k n)")
        AF = xf[:, 2560:3072]
        z1, z2, z3 = (xf[0:16, 512 * i:512 * (i + 1)] for i in range(3))
        fr = xf[0:16, 3072:3584]
        e1 = xf[0:16, 3584:4096]
        fF = xf[0:16, 1536:2048]
        fhi = KVt[:, 8448:8960]
        fgate = {}
        ft, tz = [], []

        def forget():
            tz.append(pool.put([relx], lambda e: e.memset(AF, 0.0)))
            for r in (64, 96):
                ft.append(pool.put([tz], lambda e, r=r: e.memset(AF[r:r + 16, :], 1.0)))
            bank = psum[0]
            for k in range(KT):
                hi, lo, tk = rhs_H(k)
                t = mm3(bank.ap[0:16, :], wfh[:, 16 * k:16 * k + 16], wfl[:, 16 * k:16 * k + 16], hi, lo, k == 0, k == 7,
                        [tw, tk, bank.rel], True)
            t = act.put([t, relx], lambda e: e.activation(z1, bank.ap[0:16, :], ACT.Identity, bias=small[0:16, 8:9]))
            bank.rel = [t]
            tz1 = t
            t = act.put([t, relx], lambda e: e.activation(e1, z1, ACT.Abs))
            t = act.put([t], lambda e: e.activation(e1, e1, ACT.Exp, scale=-1.0))
            t = dve.put([t, relx], lambda e: e.tensor_scalar(z2, e1, 2.0, None, ALU.add))
            t = dve.put([t], lambda e: e.reciprocal(z2, z2))
            t = pool.put([t], lambda e: e.tensor_tensor(e1, e1, z2, ALU.mult))
            t = pool.put([t], lambda e: e.tensor_tensor(z2, e1, e1, ALU.mult))
            t = pool.put([t, relx], lambda e: e.tensor_scalar(z3, z2, 2.0 / 17, 2.0 / 15, ALU.mult, ALU.add))
            for n in range(13, 0, -2):
                t = pool.put([t], lambda e: e.tensor_tensor(z3, z3, z2, ALU.mult))
                t = pool.put([t], lambda e: e.tensor_scalar(z3, z3, 2.0 / n, 1.0, ALU.add, ALU.mult))
            t = pool.put([t], lambda e: e.tensor_tensor(z3, z3, e1, ALU.mult))
            t2 = pool.put([t], lambda e: e.memset(z2, 1.0))
            fgate.update(t=t, t2=t2, z=tz1)

        def forget_sums():
            t, t2, tz1 = fgate["t"], fgate["t2"], fgate["z"]
            t = dve.put([t, tz1], lambda e: e.scalar_tensor_tensor(out=z1, in0=z1, scalar=0.0, in1=z3, op0=ALU.min, op1=ALU.subtract))
            t = dve.put([t, t2, relx], lambda e: e.tensor_tensor_scan(fr, z2, z1, 0.0, ALU.mult, ALU.add))
            thi = act.put([t], lambda e: e.activation(fhi[0:16, :], fr, ACT.Copy))
            t_lo = dve.put([thi], lambda e: e.tensor_tensor(z3, fr, fhi[0:16, :].bitcast(F), ALU.subtract))
            t_hi = act.put([thi, relx], lambda e: e.activation(fF, fhi[0:16, :].bitcast(F), ACT.Copy))
            fgate.update(lo=t_lo, hi=t_hi)

        for hf in range(2):
            gemm_A("attn_w_q_2", 0, 512 * hf, 2, lambda k: (hq[0][:, k, :], hq[1][:, k, :], hqt[k]), hf,
                   evac_q(Q2, q_ready, 4 * hf, rel6),
                   second=None if hf else kv_norm, first=forget if hf else None)
        q_done = [pe.last()]
        rel7 = barrier()
        pt_t = sb(inner, [2, 1280], R)
        KV = [Buf(KVt[:, 6144 * i:6144 * (i + 1)], q_done) for i in range(2)]
        AFr = Ring([Buf(sb(inner, [T], R), rel7) for _ in range(2)])
        BF = sb(inner, [T], R)
        kb_ready = [{k: None for k in range(4)} for _ in range(2)]
        vb_ready = [{k: None for k in range(2)} for _ in range(2)]
        zeroed = [zero_halves(KV[0], KV[0].rel, dve), []]
        run(gemm_B("w_k_2", 0, rhs_H, G_ring, evac_k(KV[0], kb_ready[0])))
        forget_sums()
        KV[1].rel = [q_done, fgate["hi"], fgate["lo"]]
        tzb = pool.put([rel7], lambda e: e.memset(BF[:, :].bitcast(F), 0.0))
        for r in (0, 32):
            ft.append(pool.put([tzb], lambda e, r=r: e.memset(BF[r:r + 16, :].bitcast(F), 1.0)))
        ft.append(act.put([tz, fgate["hi"]], lambda e: e.activation(AF[0:16, :], fF, ACT.Copy)))
        ft.append(act.put([tz, fgate["lo"]], lambda e: e.activation(AF[32:48, :], z3, ACT.Copy)))
        ft.append(act.put([tzb, fgate["hi"]], lambda e: e.activation(BF[64:80, :], fF, ACT.Copy, scale=-1.0)))
        ft.append(act.put([tzb, fgate["lo"]], lambda e: e.activation(BF[96:112, :], z3, ACT.Copy, scale=-1.0)))
        rel8 = [rel7, relx, ft, fgate["lo"]]

        ab = attn_bufs(rel8, pt_t)
        run(gemm_V("w_v_2", 0, rhs_H, G_ring, evac_v(KV[0], vb_ready[0])))
        fox = []
        for g in range(4):
            kv = KV[g % 2]

            def make(h, n, g=g):
                hd = 4 * g + n

                def start():
                    if hd >= 2:
                        fox[hd - 2].af.rel = [fox[hd - 2].s_done]
                    b = AFr.next()
                    t = pool.put([ft, b.rel], lambda e: e.tensor_scalar(
                        b.ap[:, :], AF, hmask[:, hd:hd + 1], 1.0, ALU.mult, ALU.mult))
                    h.extra = (b.ap[:, :], BF[:, :], [t, ft])
                    h.bias_ready = None
                    h.bias = lambda q: maskT[:, 128 * (3 - q):512]
                    h.af = b
                    if hd == 1:
                        zeroed[1].extend(zero_halves(KV[1], KV[1].rel))
                h.start = start

            fox += group_heads(kv, zeroed[g % 2], Q2, q_ready, kb_ready[g % 2], vb_ready[g % 2], 2 * g, make)
            free_kv(kv, fox[-1])
        o_ready = [None] * KT

        def w_o(g, kts, sl, banks, evac=None, mid=None):
            for i in range(2):
                c = slice(i * P, (i + 1) * P)
                for kt in kts:
                    tk = mm3(banks[i].ap[:, :], sl.hi[:, kt, c], sl.lo[:, kt, c], Q2[:, 0, kt, :], Q2[:, 1, kt, :],
                             kt == 0, kt == 7, [sl.ready, o_ready[kt], banks[i].rel if kt == 0 else None], kt == kts[-1])
                    yield
                if i == 1 and kts[-1] == 7:
                    release(sl, tk)
                if i == 1 and mid:
                    mid()
                if evac:
                    evac(2 * g + i, banks[i], tk)

        first_o = {}

        def early_o():
            yield
            for t_ in range(5):
                o_ready[t_] = [fox[2 * t_].out_ready, fox[2 * t_ + 1].out_ready]
            first_o["sl"] = take("B", "attn_w_o_2", 0, 0)
            yield from w_o(0, range(5), first_o["sl"], psum[6:8])

        attend(fox, ab, chain(*(kv_gemm(g, "w_k_2", 256 * g, "w_v_2", 256 * g, rhs_H, KV[g % 2]) for g in (1, 2, 3)),
                              early_o()), [8] * 12 + [3] * 4)
        for t_ in (5, 6, 7):
            o_ready[t_] = [fox[2 * t_].out_ready, fox[2 * t_ + 1].out_ready]
        Hrel[0] = [pe.last()]
        rel9 = barrier()
        d_rx = dsem()
        t = dma(d_rx, rel9, x_t[:, :, :], scratch["x"][:, :].rearrange("(kt p) n -> p kt n", p=P))
        for k in range(KT):
            xt[k] = [t]
        inner.close()
        top = ExitStack()
        nm = Norm(top, rel9, True)
        w_ln1 = ln1_cols(1, t_m3)
        nm.spare = 3
        held = []

        def o_res(k, bank, tk):
            residual(k, bank, tk, mcol(V1 + 2, k), t_m3, nm)

        def o_hold(k, bank, tk):
            if k == 0 or k > 2:
                o_res(k, bank, tk)
            else:
                held.append((k, bank, tk))

        def o_shift():
            nm.shift()
            for h in held:
                o_res(*h)

        run(w_o(0, (5, 6, 7), first_o["sl"], psum[6:8], o_hold))
        for g, banks in ((1, (0, 1)), (2, (2, 4)), (3, (6, 0))):
            sl = take("B", "attn_w_o_2", 0, 256 * g)
            run(w_o(g, range(8), sl, [psum[b] for b in banks], o_hold, o_shift if g == 1 else None))
        ln1_h(nm, w_ln1)
        rel10 = barrier()
        top.close()
        ph.close()
        ph = ExitStack()
        nm = Norm(ph, rel10, True)
        AC = [sb(ph, [2, 4, T], R) for _ in range(2)]
        ffn2(1, t_m3, nothing, nm, AC, rel10, ph, 4)
        renorm(nm, lne, [], vec8("ln2_g_2", 1), vec8("ln2_b_2", 1), t_vec, ACT)
        d_o = dsem()
        for k in range(0, KT, 2):
            t_out = dma(d_o, [xt[k], xt[k + 1]], out_t[k * P:(k + 2) * P, :].rearrange("(kt p) n -> p kt n", p=P),
                        x_t[:, k:k + 2, :])
        ph.close()
        assert state["take"] == len(plan) and not ada and not ada_pending
        finals = [t_out] + stores

        block = ctx.enter_context(nc.Block())

        @block.sync
        def _(eng):
            sp.replay(eng)
            last = {}
            for sem, value in finals:
                last[id(sem)] = (sem, max(value, last.get(id(sem), (sem, 0))[1]))
            for sem, value in last.values():
                eng.wait_ge(sem, value)

        @block.tensor
        def _(eng):
            pe.replay(eng)

        @block.scalar
        def _(eng):
            act.replay(eng)

        @block.vector
        def _(eng):
            dve.replay(eng)

        @block.gpsimd
        def _(eng):
            pool.replay(eng)


def kernel(**inputs):
    import concourse.bacc as bacc
    from concourse.bass_utils import run_bass_kernel_spmd as launch

    g = {k: np.asarray(v) for k, v in inputs.items()}

    def cols(v):
        return np.asarray(v).reshape(-1, P).T

    arrays = {}
    arrays["x_t"] = np.ascontiguousarray(g["x"][0].T)
    arrays["c_b"] = np.ascontiguousarray(np.broadcast_to(g["c"], (P, D)))
    arrays["c_b2"] = np.ascontiguousarray(np.broadcast_to(g["c_2"], (P, D)))
    arrays["ada_t"] = np.ascontiguousarray(g["ada_w"][0].T)
    arrays["ada2_0"] = np.ascontiguousarray(g["w_ada_2"][0].T)
    arrays["ada2_1"] = np.ascontiguousarray(g["w_ada_2"][1].T)
    arrays["adakv_t"] = np.ascontiguousarray(g["w_ada_kv_2"].T)
    arrays["vecs"] = np.ascontiguousarray(np.concatenate([cols(g[n].reshape(-1)) for n, _ in VECS], axis=1))
    arrays["consts"], arrays["hot"] = constants()
    arrays["sinks"] = np.ascontiguousarray(np.broadcast_to(g["attn_sinks"], (P, 8)))
    arrays["b_f"] = np.ascontiguousarray(g["b_f_2"].reshape(16, 1))
    arrays["rel_bias"] = np.ascontiguousarray(g["rel_bias"])
    order = np.concatenate([np.arange(64) + 64 * (t + 4 * two) for t in range(4) for two in range(2)])
    w_in = g["w_in"][0]
    arrays["w_in"] = np.ascontiguousarray(np.concatenate([w_in[:, order], w_in[:, 512:]], axis=1))
    arrays["w_branch_a"] = np.ascontiguousarray(g["w_branch_a"][0][order])
    for n in ("w_branch_b", "w_out", "w_mlp_in", "w_mlp_out", "conv_w_in_2", "conv_w_out_2", "attn_w_q_2", "attn_w_o_2"):
        arrays[n] = np.ascontiguousarray(g[n][0])
    for n in ("w_k_2", "w_v_2", "w_f_2"):
        arrays[n] = np.ascontiguousarray(g[n])
    for l in range(2):
        arrays[f"gate{l}"] = np.ascontiguousarray(g["ffn_w_gate_2"][l])
        arrays[f"up{l}"] = np.ascontiguousarray(g["ffn_w_up_2"][l])
        arrays[f"down{l}"] = np.ascontiguousarray(g["ffn_w_down_2"][l])

    nc = bacc.Bacc("TRN2", target_bir_lowering=False, num_devices=1)
    aps, feeds = {}, {}
    for n, v in arrays.items():
        feeds[f"in_{n}"] = v
        aps[n] = nc.dram_tensor(f"in_{n}", v.shape, mybir.dt.from_np(v.dtype), kind="ExternalInput").ap()
    out_t = nc.dram_tensor("out_t", (D, T), F, kind="ExternalOutput").ap()
    scratch = {"skew": nc.dram_tensor("skew", (16, SKEW), F, kind="Internal").ap(),
               "x": nc.dram_tensor("x_keep", (D, T), F, kind="Internal").ap()}
    build(nc, aps, out_t, scratch)
    r = launch(nc, [feeds], core_ids=[0])
    return np.ascontiguousarray(np.asarray(r.results[0]["out_t"]).T)[None]
```
